# Optimizing a Trainium2 kernel written in Bass

```python
import math
import jax, jax.numpy as jnp
from jax import lax
import numpy as np

D_MODEL = 1024
BATCH = 1
SEQ = 256
DEPTH = 2

A_QK_DIM = 64
A_V_DIM = 2 * A_QK_DIM
A_WIDTH = D_MODEL // 2
A_HEADS = A_WIDTH // A_V_DIM
Q_BLOCK = 128
ROPE_THETA = 10000.0
POOL_WINDOWS = (2, 4, 8, 16)
B_WIDTH = D_MODEL // 2
POOL_GROUP = B_WIDTH // len(POOL_WINDOWS)
AB_IN = 3 * A_WIDTH + B_WIDTH
C_DIM = 128
C_HEADS = D_MODEL // C_DIM
C_IN = 4 * D_MODEL
CHUNK = 64
D_FF = ((8 * D_MODEL // 3 + 255) // 256) * 256
ALPHA = (2 * DEPTH) ** 0.25
BETA = (8 * DEPTH) ** -0.25
LN_EPS = 1e-5
N_AB = (DEPTH + 1) // 2
N_C = DEPTH // 2

kernel_name = "diffattn_pool_hgrn2_macaron_deepnorm"

def layer_norm(x, g, b):
    xf = x.astype(jnp.float32)
    mu = jnp.mean(xf, -1, keepdims=True)
    var = jnp.mean(jnp.square(xf - mu), -1, keepdims=True)
    return ((xf - mu) * lax.rsqrt(var + LN_EPS) * g + b).astype(x.dtype)

def rms_norm(x, g):
    xf = x.astype(jnp.float32)
    return (xf * lax.rsqrt(jnp.mean(jnp.square(xf), -1, keepdims=True) + LN_EPS) * g).astype(x.dtype)

def swiglu(x, w_in, w_out):
    gate, up = jnp.split(x @ w_in, 2, axis=-1)
    return (jax.nn.silu(gate) * up) @ w_out

def rope_tables(positions):
    inv_freq = ROPE_THETA ** (-jnp.arange(0, A_QK_DIM, 2, dtype=jnp.float32) / A_QK_DIM)
    ang = positions.astype(jnp.float32)[..., None] * inv_freq
    ang = ang[:, :, None, None, :]
    return jnp.cos(ang), jnp.sin(ang)

def apply_rope(t, cos, sin):
    t1, t2 = jnp.split(t.astype(jnp.float32), 2, axis=-1)
    return jnp.concatenate([t1 * cos - t2 * sin, t2 * cos + t1 * sin], -1).astype(t.dtype)

def diff_attention(q, k, v, lam):
    B, S, H, _, dq = q.shape
    nb = S // Q_BLOCK
    scale = dq ** -0.5
    qb = q.reshape(B, nb, Q_BLOCK, H, 2, dq).transpose(1, 0, 2, 3, 4, 5)
    key_idx = jnp.arange(S)

    def block(args):
        q_blk, i = args
        s = jnp.einsum('bqhcd,bkhcd->bhcqk', q_blk, k).astype(jnp.float32) * scale
        q_idx = i * Q_BLOCK + jnp.arange(Q_BLOCK)
        s = jnp.where(key_idx[None, :] <= q_idx[:, None], s, -jnp.inf)
        p = jax.nn.softmax(s, axis=-1)
        w = p[:, :, 0] - lam * p[:, :, 1]
        return jnp.einsum('bhqk,bkhv->bqhv', w.astype(v.dtype), v)

    o = lax.map(block, (qb, jnp.arange(nb)))
    return o.transpose(1, 0, 2, 3, 4).reshape(B, S, H, v.shape[-1])

def multiscale_pool(u, pool_w, pool_scale):
    B, S, _ = u.shape
    uf = u.astype(jnp.float32)
    c = jnp.cumsum(uf, axis=1)
    t1 = jnp.arange(1, S + 1, dtype=jnp.float32)
    outs = []
    for g, w in enumerate(POOL_WINDOWS):
        sl = slice(g * POOL_GROUP, (g + 1) * POOL_GROUP)
        cg = c[..., sl]
        lagged = jnp.pad(cg[:, :S - w], ((0, 0), (w, 0), (0, 0)))
        mean = (cg - lagged) / jnp.minimum(t1, float(w))[None, :, None]
        outs.append(mean - uf[..., sl])
    d = jnp.stack(outs, axis=2).astype(u.dtype)
    y = jnp.einsum('bsgc,gcd->bsgd', d, pool_w)
    return y.reshape(B, S, B_WIDTH) * pool_scale

def diff_pool_mixer(x, cos, sin, w_in, w_o, lam_vecs, subln_g, pool_w, pool_scale, lambda_init):
    B, S, _ = x.shape
    h = x @ w_in
    q = apply_rope(h[..., :A_WIDTH].reshape(B, S, A_HEADS, 2, A_QK_DIM), cos, sin)
    k = apply_rope(h[..., A_WIDTH:2 * A_WIDTH].reshape(B, S, A_HEADS, 2, A_QK_DIM), cos, sin)
    v = h[..., 2 * A_WIDTH:3 * A_WIDTH].reshape(B, S, A_HEADS, A_V_DIM)
    u = h[..., 3 * A_WIDTH:]
    lv = lam_vecs.astype(jnp.float32)
    lam = jnp.exp(jnp.sum(lv[0] * lv[1])) - jnp.exp(jnp.sum(lv[2] * lv[3])) + lambda_init
    o = diff_attention(q, k, v, lam)
    o_a = (rms_norm(o, subln_g) * (1.0 - lambda_init)).reshape(B, S, A_WIDTH).astype(x.dtype)
    o_b = multiscale_pool(u, pool_w, pool_scale).astype(x.dtype)
    return jnp.concatenate([o_a, o_b], axis=-1) @ w_o

def hgrn2_chunk_scan(q, k, v, log_f):
    _, B, H, C, dk = q.shape
    dv = v.shape[-1]
    causal = jnp.tril(jnp.ones((C, C), dtype=bool))

    def step(state, inp):
        qc, kc, vc, lfc = inp
        b = jnp.cumsum(lfc, axis=-2)
        inter = jnp.einsum('bhtk,bhkv->bhtv', qc * jnp.exp(b), state)
        rel = b[:, :, :, None, :] - b[:, :, None, :, :]
        decay = jnp.exp(jnp.where(causal[:, :, None], rel, -jnp.inf))
        scores = jnp.einsum('bhtk,bhsk,bhtsk->bhts', qc, kc, decay)
        intra = jnp.einsum('bhts,bhsv->bhtv', scores, vc)
        b_last = b[:, :, -1:, :]
        state = jnp.exp(b_last[:, :, 0, :])[..., None] * state + jnp.einsum(
            'bhsk,bhsv->bhkv', kc * jnp.exp(b_last - b), vc)
        return state, inter + intra

    s0 = jnp.zeros((B, H, dk, dv), jnp.float32)
    _, o = lax.scan(step, s0, (q, k, v, log_f))
    return o

def hgrn2_mixer(x, w_in, w_o, g_norm, lower_bound):
    B, S, _ = x.shape
    q, fz, i, g = jnp.split(x @ w_in, 4, axis=-1)
    q = jax.nn.silu(q.astype(jnp.float32))
    f = lower_bound + (1.0 - lower_bound) * jax.nn.sigmoid(fz.astype(jnp.float32))
    log_f = jnp.log(f)
    k = 1.0 - f

    def heads(t):
        return t.astype(jnp.float32).reshape(B, S // CHUNK, CHUNK, C_HEADS, C_DIM).transpose(1, 0, 3, 2, 4)

    o = hgrn2_chunk_scan(heads(q), heads(k), heads(i), heads(log_f))
    o = o.transpose(1, 0, 3, 2, 4).reshape(B, S, C_HEADS, C_DIM)
    o = rms_norm(o, g_norm).reshape(B, S, D_MODEL).astype(x.dtype) * jax.nn.silu(g)
    return o @ w_o

def setup_inputs(seed: int = 0) -> dict:
    key = jax.random.key(seed)
    ks = jax.random.split(key, 20)

    def n(k, shape, s):
        return jax.random.normal(k, shape, jnp.float32) * s

    x = n(ks[0], (BATCH, SEQ, D_MODEL), 1.0)
    offsets = jax.random.randint(ks[1], (BATCH, 1), 0, 4096, dtype=jnp.int32)
    positions = offsets + jnp.arange(SEQ, dtype=jnp.int32)[None, :]
    return {
        "x": x,
        "positions": positions,
        "ln_gain": 1.0 + n(ks[2], (DEPTH, 3, D_MODEL), 0.05),
        "ln_bias": n(ks[3], (DEPTH, 3, D_MODEL), 0.02),
        "ffn1_w_in": n(ks[4], (DEPTH, D_MODEL, 2 * D_FF), D_MODEL ** -0.5),
        "ffn1_w_out": n(ks[5], (DEPTH, D_FF, D_MODEL), BETA * D_FF ** -0.5),
        "ffn2_w_in": n(ks[6], (DEPTH, D_MODEL, 2 * D_FF), D_MODEL ** -0.5),
        "ffn2_w_out": n(ks[7], (DEPTH, D_FF, D_MODEL), BETA * D_FF ** -0.5),
        "ab_w_in": n(ks[8], (N_AB, D_MODEL, AB_IN), D_MODEL ** -0.5),
        "ab_w_o": n(ks[9], (N_AB, A_WIDTH + B_WIDTH, D_MODEL), BETA * (A_WIDTH + B_WIDTH) ** -0.5),
        "diff_lambda": n(ks[10], (N_AB, 4, A_QK_DIM), 0.1),
        "diff_subln": 1.0 + n(ks[11], (N_AB, A_V_DIM), 0.05),
        "pool_w": n(ks[12], (N_AB, len(POOL_WINDOWS), POOL_GROUP, POOL_GROUP), POOL_GROUP ** -0.5),
        "pool_scale": 1.0 + n(ks[13], (N_AB, B_WIDTH), 0.1),
        "c_w_in": n(ks[14], (N_C, D_MODEL, C_IN), D_MODEL ** -0.5),
        "c_w_o": n(ks[15], (N_C, D_MODEL, D_MODEL), BETA * D_MODEL ** -0.5),
        "c_norm": 1.0 + n(ks[16], (N_C, C_DIM), 0.05),
        "hgrn_gamma": n(ks[17], (DEPTH, D_MODEL), 0.1),
    }

def reference(x, positions, ln_gain, ln_bias, ffn1_w_in, ffn1_w_out, ffn2_w_in, ffn2_w_out,
              ab_w_in, ab_w_o, diff_lambda, diff_subln, pool_w, pool_scale,
              c_w_in, c_w_o, c_norm, hgrn_gamma):
    cos, sin = rope_tables(positions)
    p = jax.nn.softmax(hgrn_gamma.astype(jnp.float32), axis=0)
    lower_bounds = jnp.cumsum(p, axis=0) - p[0]
    for l in range(DEPTH):
        j = l // 2
        x = layer_norm(ALPHA * x + 0.5 * swiglu(x, ffn1_w_in[l], ffn1_w_out[l]), ln_gain[l, 0], ln_bias[l, 0])
        if l % 2 == 0:
            lambda_init = 0.8 - 0.6 * math.exp(-0.3 * l)
            y = diff_pool_mixer(x, cos, sin, ab_w_in[j], ab_w_o[j], diff_lambda[j], diff_subln[j],
                                pool_w[j], pool_scale[j], lambda_init)
        else:
            y = hgrn2_mixer(x, c_w_in[j], c_w_o[j], c_norm[j], lower_bounds[l])
        x = layer_norm(ALPHA * x + y, ln_gain[l, 1], ln_bias[l, 1])
        x = layer_norm(ALPHA * x + 0.5 * swiglu(x, ffn2_w_in[l], ffn2_w_out[l]), ln_gain[l, 2], ln_bias[l, 2])
    return x


_drawn_inputs = setup_inputs


def setup_inputs(seed=0):
    import zlib

    import numpy as np

    out = dict(_drawn_inputs(seed))
    spreads = {}
    factors = {'diff_subln': 5.021, 'pool_scale': 2.676, 'c_norm': 5.266, 'hgrn_gamma': 8.0}
    for name, (base, spread) in spreads.items():
        noise = np.random.default_rng([zlib.crc32(name.encode()), seed]).standard_normal(out[name].shape)
        drawn = base * np.exp(spread * noise) if base else spread * noise
        out[name] = __import__('jax').numpy.asarray(drawn.astype(out[name].dtype))
    for name, factor in factors.items():
        out[name] = (out[name] * factor).astype(out[name].dtype)
    return out
```

```python
from contextlib import ExitStack

import concourse.bass as bass
from concourse import mybir

ALU = mybir.AluOpType
ACT = mybir.ActivationFunctionType
AX = mybir.AxisListType
F32 = mybir.dt.float32
F32R = mybir.dt.float32r
I32 = mybir.dt.int32
U8 = mybir.dt.uint8

P = 128
D = 1024
SEQ = 256
TT = SEQ // P
KB = D // P
D_FF = 2816
FC = 256
NC = D_FF // FC
NPAIR = (NC - 3) // 2
HEADS_A = 4
POOLS = (2, 4, 8, 16)
UNIT = 2048
RAW = 3
RING = 6
LEVELS = (64, 32, 16, 8, 4, 2, 1)
NL = len(LEVELS)
N_DECAY = NL + 2
DEPTH = 2
ALPHA = (2 * DEPTH) ** 0.25
LN_EPS = 1e-5
LAMBDA_INIT = 0.2
SM_SCALE = 64 ** -0.5
TWO_PI_1, TWO_PI_2, TWO_PI_3 = 6.28125, 0.0019350051879882812, 3.019916050561733e-07
ROUND = 1.5 * 2.0 ** 23
NEG = -1e30

C_ID = 0
C_CAUSAL = C_ID + P
C_INVF = C_CAUSAL + P
C_BAND = C_INVF + 32
C_DECAY = C_BAND + 4 * 3 * P
C_MASK = C_DECAY + N_DECAY * P
C_END = C_MASK + (NL + 1) * P

ORDER = ("F0", "AB", "F1", "F2", "C", "F3")


def build(nc, x, positions, ln_gain, ln_bias, ffn1_w_in, ffn1_w_out, ffn2_w_in, ffn2_w_out, ab_w_in, ab_w_o,
          diff_lambda, diff_subln, pool_w, pool_scale, c_w_in, c_w_o, c_norm, hgrn_gamma, consts, out):
    with ExitStack() as ctx:
        def sb(name, shape, dt=F32):
            return ctx.enter_context(nc.sbuf_tensor(name, shape, dt))

        def sem(name):
            return ctx.enter_context(nc.semaphore(name))

        raw = sb("raw", [P, RAW, UNIT])
        w_hi = sb("w_hi", [P, RING, UNIT], F32R)
        w_lo = sb("w_lo", [P, RING, UNIT], F32R)
        x_tok = sb("x_tok", [P, TT, D])
        xT_hi = sb("xT_hi", [P, KB, SEQ], F32R)
        xT_lo = sb("xT_lo", [P, KB, SEQ], F32R)
        hT_hi = sb("hT_hi", [P, 2, 512], F32R)
        hT_lo = sb("hT_lo", [P, 2, 512], F32R)
        ffn_tok = sb("ffn_tok", [P, 2, TT, FC])
        ln_gb = sb("ln_gb", [P, 2, D])
        arena = sb("arena", [P, 8704])
        decay = sb("decay", [P, N_DECAY, P], F32R)
        level_mask = sb("level_mask", [P, NL + 1, P], U8)
        ident = sb("ident", [P, P])
        causal = sb("causal", [P, P])
        stats = sb("stats", [P, TT, 2, 6])
        mv = sb("mv", [P, TT, 2])
        veps = sb("veps", [P, TT])
        rstd = sb("rstd", [P, TT])
        mhalf = sb("mhalf", [P, 8])
        cols = sb("cols", [P, 8])
        lam = sb("lam", [P, 8])
        sm = sb("sm", [P, 4, 2, 2])
        ssq = sb("ssq", [P, 2, 8])
        pos_i = sb("pos_i", [P, TT], I32)

        pair = [ctx.enter_context(nc.psum_tensor(f"banks{2 * i}{2 * i + 1}", [P, 2, 512], F32)) for i in range(4)]
        bank = [pair[i // 2][:, i % 2] for i in range(8)]
        Y = [bank[0:2], bank[2:4]]
        G = bank[4:6]
        T = bank[6:8]

        raw_landed = [sem(f"raw_landed{i}") for i in range(RAW)]
        hi_ready, lo_ready, unit_used = sem("hi_ready"), sem("lo_ready"), sem("unit_used")
        x_landed, const_landed, gb_landed = sem("x_landed"), sem("const_landed"), sem("gb_landed")
        chunk_done = [sem(f"chunk_done{t}") for t in range(TT)]
        silu_ready, hid_ready, hidT_done, hidT_hi, hidT_lo = (
            sem("silu_ready"), sem("hid_ready"), sem("hidT_done"), sem("hidT_hi_ready"), sem("hidT_lo_ready"))
        y_done, var_ready, rstd_ready, x_ready = sem("y_done"), sem("var_ready"), sem("rstd_ready"), sem("x_ready")
        gb_used = sem("gb_used")
        xT_done, xT_hi_ready, xT_lo_ready = sem("xT_done"), sem("xT_hi_ready"), sem("xT_lo_ready")
        dve_step, act_step, pool_step = sem("dve_step"), sem("act_step"), sem("pool_step")
        out_stored = sem("out_stored")
        S = {n: sem(n) for n in (
            "setup_pool", "ab_tables_landed", "rope_done", "mixA_evac", "u_ready", "v_ready", "dT_done", "dT_ready", "poolT_done",
            "poolT_hi", "poolT_lo", "qk_done", "qkT_done", "qkT_ready", "score_done", "prob_bias", "prob_ready",
            "w_ready", "wT_done", "wT_ready", "o_done", "o_copied", "o_ssq", "o_rms", "o_ready", "oT_done", "oT_hi", "oT_lo",
            "ang_ready", "sincos_ready", "lam_prod", "lam_exp",
            "c_tables_landed", "gamma_landed", "gamma_used", "lb_arg", "lb_exp", "lb_ready", "sig_ready", "f_ready",
            "logf_ready", "logf_hi", "logf_lo", "q_ready", "val_ready", "gate_ready", "c_tab_ready",
            "c_qkT_done", "c_qkT_ready", "expo_done", "expo_ready", "fac_ready", "lvl_done", "sc_ready",
            "klT_done", "klT_ready", "st_done", "st_ready", "co_done", "co_copied", "c_ssq", "c_rms", "c_on",
            "c_oT_done", "c_oT_hi", "c_oT_lo", "c_half_done")}

        FFN_UNITS = 3 * NC
        AB_CHUNKS = (3, 0, 1, 2)
        C_CHUNKS = tuple(g + hf for hf in range(2) for g in (2, 0, 4, 6))
        phases, at = {}, 0
        for name, n in (("F0", FFN_UNITS), ("AB", 2 * len(AB_CHUNKS) + 4), ("F1", FFN_UNITS), ("F2", FFN_UNITS),
                        ("C", 2 * len(C_CHUNKS) + 4), ("F3", FFN_UNITS)):
            if name in ORDER:
                phases[name] = at
                at += n
        N_UNITS = at
        AHEAD = 3

        FFN = {"F0": (0, ffn1_w_in, ffn1_w_out), "F1": (0, ffn2_w_in, ffn2_w_out),
               "F2": (1, ffn1_w_in, ffn1_w_out), "F3": (1, ffn2_w_in, ffn2_w_out)}
        NORMS = {"F0": (0, 0.5 / ALPHA), "AB": (1, 1.0 / ALPHA), "F1": (2, 0.5 / ALPHA),
                 "F2": (3, 0.5 / ALPHA), "C": (4, 1.0 / ALPHA), "F3": (5, 0.5 / ALPHA)}
        SILUS = {"F0": 0, "F1": 1, "F2": 2, "F3": 3}

        CHUNKS_BEFORE, n = {}, 0
        for name in ORDER:
            CHUNKS_BEFORE[name] = n
            n += {"AB": len(AB_CHUNKS), "C": len(C_CHUNKS)}.get(name, NC)

        used_by = []
        n_used = n_chunk = 0
        for m, name in enumerate(ORDER):
            if name in FFN:
                kinds = "AB" + "ABO" * (NC - 1) + "Y"
            else:
                kinds = "AB" * len(AB_CHUNKS if name == "AB" else C_CHUNKS) + "OOOY"
            for kind in kinds:
                if kind in "AO":
                    n_used += 1
                    used_by.append((unit_used, n_used, 4))
                elif kind == "B":
                    n_chunk += 1
                    used_by.append((chunk_done[TT - 1], n_chunk, 2))
                else:
                    used_by.append((y_done, 2 * (m + 1), 0))

        block = ctx.enter_context(nc.Block())

        def region(a, *shape):
            n = 1
            for s in shape:
                n *= s
            v = arena[:, a:a + n]
            if len(shape) == 2:
                v = v.rearrange("p (a b) -> p a b", a=shape[0])
            if len(shape) == 3:
                v = v.rearrange("p (a b c) -> p a b c", a=shape[0], b=shape[1])
            return v

        kT = region(0, HEADS_A, SEQ)
        u_tok = region(0, TT, 512)
        v_tok = region(1024, TT, 512)
        qk_rot = region(2048, 2, TT, 512)
        probs = region(2048, 2, 2, SEQ)
        wts = region(3072, 2, SEQ)
        wT = region(3584, 2, SEQ)
        qT = region(4096, HEADS_A, SEQ)
        dT = region(5120, 4, SEQ)
        band = region(6144, 4, 3 * P)
        o_tok = region(6144, TT, 512)
        poolw = region(7680, 4, P)
        rope_tmp = region(8192, 512)
        sincos = region(4096, 2, TT, 32)
        ang = region(4096 + 128, 6, TT * 32)
        invf = region(4096 + 512, 32)
        lamv = region(5120, 4, 64)

        q_tok = region(0, TT, 512)
        k_tok = region(1024, TT, 512)
        logf = region(2048, TT, 512)
        val = region(3072, TT, 512)
        gate = region(4096, TT, 512)
        qkT = region(5120, 2, TT, P)
        fac = region(5632, TT, NL + 1, P)
        scT = region(7680, TT, P)
        state = region(7936, P)
        klT = region(8064, P)
        o_raw = region(8192, TT, P)
        o_sq = region(8448, P)
        stage = region(5120, N_DECAY + NL + 1, P)
        o_half = [ffn_tok[:].rearrange("p a t f -> p (a t f)").rearrange("p (t f) -> p t f", t=TT), q_tok]

        @block.sync
        def _(sp):
            def load_gate_up(n, n_static, w, kh, c):
                if not (type(n) is int and n < RAW):
                    sp.wait_ge(lo_ready, n - RAW + 1)
                dst = raw[:, n_static % RAW].rearrange("p (k g f) -> p k g f", k=4, g=2)
                src = w.rearrange("(k p) (g f) -> p k g f", p=P, g=2)
                for g in range(2):
                    sp.dma_start(dst[:, :, g], src[:, 4 * kh:4 * kh + 4, g, bass.ds(c * FC, FC)]
                                 ).then_inc(raw_landed[n_static % RAW], 16)

            def load_rows(n, n_static, w, c):
                sp.wait_ge(lo_ready, n - RAW + 1)
                for k in range(2):
                    sp.dma_start(raw[:, n_static % RAW, k * D:(k + 1) * D], w[bass.ds((2 * c + k) * P, P), :]
                                 ).then_inc(raw_landed[n_static % RAW], 16)

            for name in ORDER:
                s0 = phases[name]
                if name in FFN:
                    layer, w_in, w_out = FFN[name]
                    wi, wo = w_in[layer], w_out[layer]
                    for kh in range(2):
                        load_gate_up(s0 + kh, s0 + kh, wi, kh, 0)
                    for kh in range(2):
                        load_gate_up(s0 + 2 + kh, s0 + 2 + kh, wi, kh, 1)
                    load_rows(s0 + 4, s0 + 4, wo, 0)
                    with sp.Fori(0, NPAIR) as i:
                        for par in range(2):
                            a = s0 + 5 + 3 * par
                            for kh in range(2):
                                load_gate_up(i * 6 + (a + kh), a + kh, wi, kh, i * 2 + (2 + par))
                            load_rows(i * 6 + (a + 2), a + 2, wo, i * 2 + (1 + par))
                    a = s0 + FFN_UNITS - 4
                    for kh in range(2):
                        load_gate_up(a + kh, a + kh, wi, kh, NC - 1)
                    load_rows(a + 2, a + 2, wo, NC - 2)
                    load_rows(a + 3, a + 3, wo, NC - 1)
                else:
                    w_in, w_out, order = ((ab_w_in[0], ab_w_o[0], AB_CHUNKS) if name == "AB"
                                          else (c_w_in[0], c_w_o[0], C_CHUNKS))
                    for j, c in enumerate(order):
                        for kh in range(2):
                            n = s0 + 2 * j + kh
                            sp.wait_ge(lo_ready, n - RAW + 1)
                            for k in range(0, 4, 2):
                                sp.dma_start(
                                    raw[:, n % RAW, k * 512:(k + 2) * 512].rearrange("p (k f) -> p k f", k=2),
                                    w_in.rearrange("(k p) f -> p k f", p=P)[:, 4 * kh + k:4 * kh + k + 2,
                                                                            c * 512:(c + 1) * 512]
                                ).then_inc(raw_landed[n % RAW], 16)
                    for m in range(4):
                        n = s0 + 2 * len(order) + m
                        load_rows(n, n, w_out, m)
            for t in range(TT):
                for h in range(2):
                    sp.wait_ge(x_ready, 4 * len(ORDER) - 3 + 2 * t + h)
                    sp.dma_start(out[0, t * P:(t + 1) * P, h * 512:(h + 1) * 512],
                                 x_tok[:, t, h * 512:(h + 1) * 512]).then_inc(out_stored, 16)
            sp.wait_ge(out_stored, 16 * 4)

        @block.scalar
        def _(act):
            steps = [0]

            def step(ins):
                steps[0] += 1
                ins.then_inc(act_step, 1)
                act.wait_ge(act_step, steps[0])

            def split_hi(n, i=None):
                slot, use = n % RAW, n // RAW
                if n >= N_UNITS:
                    return
                if i is None:
                    act.wait_ge(raw_landed[slot], 32 * (use + 1))
                    if n >= RING:
                        used, value, _ = used_by[n - RING]
                        act.wait_ge(used, value)
                else:
                    used, value, per_iteration = used_by[n - RING]
                    act.wait_ge(raw_landed[slot], i * (32 * RING // RAW) + 32 * (use + 1))
                    act.wait_ge(used, i * per_iteration + value)
                nc.scalar.copy(w_hi[:, n % RING], raw[:, slot]).then_inc(hi_ready, 1)

            def xT_split(m, t):
                for h in range(2):
                    act.wait_ge(xT_done, 4 * m + 2 * t + h + 1)
                    nc.scalar.copy(xT_hi[:, 4 * h:4 * h + 4, t * P:(t + 1) * P],
                                   T[h].rearrange("p (k f) -> p k f", k=4)).then_inc(xT_hi_ready, 1)

            def ffn_chunk_silu(name, t, c):
                k = CHUNKS_BEFORE[name]
                act.wait_ge(chunk_done[t], c + (k + 1))
                nc.scalar.activation(ffn_tok[:, 0, t], G[t][:, 0:FC], ACT.Silu).then_inc(silu_ready, 1)

            def ffn_hidT(name, c, par):
                act.wait_ge(hidT_done, c + (SILUS[name] * NC + 1))
                nc.scalar.copy(hT_hi[:, par], T[0]).then_inc(hidT_hi, 1)

            def ffn(name, m):
                s0 = phases[name]
                xT_split(m, 0)
                split_hi(s0 + 3)
                xT_split(m, 1)
                split_hi(s0 + 4)
                for t in range(TT):
                    ffn_chunk_silu(name, t, 0)
                ffn_hidT(name, 0, 0)
                ffn_chunk(name, s0 + 5, None, 1, 1)
                with act.Fori(0, NPAIR) as i:
                    for par in range(2):
                        ffn_chunk(name, s0 + 8 + 3 * par, i, i * 2 + (2 + par), par)
                ffn_chunk(name, s0 + FFN_UNITS - 1, None, NC - 1, 0)
                split_hi(s0 + FFN_UNITS + 2)

            def ffn_chunk(name, n, i, c, par):
                split_hi(n, i)
                ffn_chunk_silu(name, 0, c)
                split_hi(n + 1, i)
                ffn_chunk_silu(name, 1, c)
                split_hi(n + 2, i)
                ffn_hidT(name, c, par)

            def mix_ab(m):
                s0 = phases["AB"]
                k = CHUNKS_BEFORE["AB"]
                xT_split(m, 0)
                xT_split(m, 1)
                for j, c in enumerate(AB_CHUNKS):
                    for t in range(TT):
                        split_hi(s0 + AHEAD + 2 * j + t)
                        if c == 3:
                            act.wait_ge(chunk_done[t], k + j + 1)
                            nc.scalar.copy(u_tok[:, t], G[t]).then_inc(S["u_ready"], 1)
                        if c == 2:
                            act.wait_ge(chunk_done[t], k + j + 1)
                            nc.scalar.copy(v_tok[:, t], G[t]).then_inc(S["v_ready"], 1)
                    if c == 3:
                        act.wait_ge(S["ang_ready"], 1)
                        nc.scalar.activation(sincos, ang[:, 4:6].rearrange("p a (t f) -> p a t f", t=TT), ACT.Sin
                                             ).then_inc(S["sincos_ready"], 1)
                        act.wait_ge(S["lam_prod"], 1)
                        nc.scalar.activation(lam[:, 2:4], lam[:, 0:2], ACT.Exp).then_inc(S["lam_exp"], 1)
                    if c == 0:
                        for b in range(2):
                            act.wait_ge(S["dT_done"], b + 1)
                            nc.scalar.copy(dT[:, 2 * b:2 * b + 2], bank[b].rearrange("p (g f) -> p g f", g=2)
                                           ).then_inc(S["dT_ready"], 1)
                act.wait_ge(S["setup_pool"], 16 * 4)
                for b in range(2):
                    act.wait_ge(S["poolT_done"], b + 1)
                    for g in (2 * b, 2 * b + 1):
                        nc.scalar.activation(xT_hi[:, 4 + g], bank[2 + b][:, (g % 2) * SEQ:(g % 2 + 1) * SEQ],
                                             ACT.Copy, scale=cols[:, 2 + g:3 + g]).then_inc(S["poolT_hi"], 1)
                for i, (b, dst) in enumerate(((bank[0], qT), (bank[1], qT), (bank[4], kT), (bank[5], kT))):
                    act.wait_ge(S["qkT_done"], i + 1)
                    nc.scalar.copy(dst[:, :, (i % 2) * P:(i % 2 + 1) * P], b.rearrange("p (h f) -> p h f", h=4)
                                   ).then_inc(S["qkT_ready"], 1)
                for it in range(2 * HEADS_A):
                    h, t = it // 2, it % 2
                    act.wait_ge(S["prob_bias"], it + 1)
                    if it >= 2:
                        act.wait_ge(S["w_ready"], it - 1)
                    L = P * (t + 1)
                    for c in range(2):
                        nc.scalar.activation(probs[:, it % 2, c, 0:L], bank[2 * (it % 2) + c][:, 0:L], ACT.Exp,
                                             bias=sm[:, 1, it % 2, c:c + 1], scale=SM_SCALE,
                                             accum_out=sm[:, 2, it % 2, c:c + 1]).then_inc(S["prob_ready"], 1)
                    if it >= 1:
                        wT_copy(it - 1)
                wT_copy(2 * HEADS_A - 1)
                for t in range(TT):
                    act.wait_ge(S["o_done"], t + 1)
                    nc.scalar.copy(o_tok[:, t], bank[4 + t]).then_inc(S["o_copied"], 1)
                for t in range(TT):
                    act.wait_ge(S["oT_done"], t + 1)
                    nc.scalar.activation(xT_hi[:, 0:4, t * P:(t + 1) * P], T[t].rearrange("p (h f) -> p h f", h=4),
                                         ACT.Copy, scale=cols[:, 0:1]).then_inc(S["oT_hi"], 1)
                for j in range(4):
                    split_hi(s0 + AHEAD + 2 * len(AB_CHUNKS) + j)

            def wT_copy(it):
                t = it % 2
                act.wait_ge(S["wT_done"], it + 1)
                nc.scalar.copy(wT[:, it % 2, 0:P * (t + 1)], T[it % 2][:, 0:P * (t + 1)]
                               ).then_inc(S["wT_ready"], 1)

            def mix_c(m):
                s0 = phases["C"]
                k = CHUNKS_BEFORE["C"]
                xT_split(m, 0)
                xT_split(m, 1)
                act.wait_ge(S["lb_arg"], 1)
                for src in (val, gate):
                    nc.scalar.activation(src, src, ACT.Exp).then_inc(S["lb_exp"], 1)
                for hf in range(2):
                    for j, kind in enumerate("fqig"):
                        jj = 4 * hf + j
                        for t in range(TT):
                            split_hi(s0 + AHEAD + 2 * jj + t)
                            act.wait_ge(chunk_done[t], k + jj + 1)
                            if kind == "f":
                                nc.scalar.activation(logf[:, t], G[t], ACT.Sigmoid).then_inc(S["sig_ready"], 1)
                            if kind == "q":
                                if hf:
                                    act.wait_ge(S["c_qkT_done"], 4)
                                nc.scalar.activation(q_tok[:, t], G[t], ACT.Silu).then_inc(S["q_ready"], 1)
                            if kind == "i":
                                act.wait_ge(S["lb_ready"], 1)
                                nc.scalar.copy(val[:, t], G[t]).then_inc(S["val_ready"], 1)
                            if kind == "g":
                                if hf:
                                    act.wait_ge(S["c_on"], 8)
                                nc.scalar.activation(gate[:, t], G[t], ACT.Silu).then_inc(S["gate_ready"], 1)
                        if kind == "f":
                            for t in range(TT):
                                act.wait_ge(S["f_ready"], 2 * hf + t + 1)
                                step(nc.scalar.activation(logf[:, t], logf[:, t], ACT.Ln))
                                nc.scalar.copy(hT_hi[:, t], logf[:, t]).then_inc(S["logf_hi"], 1)
                    for hh in range(4):
                        hd = 4 * hf + hh
                        act.wait_ge(S["c_qkT_done"], hd + 1)
                        nc.scalar.copy(qkT[:].rearrange("p a t f -> p (a t f)"), bank[0]
                                       ).then_inc(S["c_qkT_ready"], 1)
                        for t in range(TT):
                            act.wait_ge(S["expo_done"], 2 * hd + t + 1)
                            nc.scalar.activation(fac[:, t].rearrange("p l f -> p (l f)"),
                                                 pair[3][:].rearrange("p a f -> p (a f)"), ACT.Exp
                                                 ).then_inc(S["expo_ready"], 1)
                        act.wait_ge(S["klT_done"], hd + 1)
                        nc.scalar.copy(klT, bank[0][:, 0:P]).then_inc(S["klT_ready"], 1)
                        act.wait_ge(S["st_done"], hd + 1)
                        nc.scalar.copy(state, bank[0][:, 0:P]).then_inc(S["st_ready"], 1)
                        act.wait_ge(S["co_done"], hd + 1)
                        if hd:
                            act.wait_ge(S["c_on"], 2 * hd)
                        nc.scalar.copy(o_raw.rearrange("p t f -> p (t f)"), bank[3][:, 0:2 * P]
                                       ).then_inc(S["co_copied"], 1)
                for i in range(4):
                    hf, t = i // 2, i % 2
                    act.wait_ge(S["c_oT_done"], i + 1)
                    nc.scalar.activation(xT_hi[:, 4 * hf:4 * hf + 4, t * P:(t + 1) * P],
                                         T[t].rearrange("p (h f) -> p h f", h=4), ACT.Copy, scale=cols[:, 1:2]
                                         ).then_inc(S["c_oT_hi"], 1)
                for j in range(4):
                    split_hi(s0 + AHEAD + 2 * len(C_CHUNKS) + j)

            for n in range(AHEAD):
                split_hi(n)
            for m, name in enumerate(ORDER):
                if name == "AB":
                    mix_ab(m)
                elif name == "C":
                    mix_c(m)
                else:
                    ffn(name, m)

        @block.vector
        def _(dve):
            steps = [0]

            def step(ins):
                steps[0] += 1
                ins.then_inc(dve_step, 1)
                dve.wait_ge(dve_step, steps[0])

            def split_lo(n, i=None):
                if n >= N_UNITS:
                    return
                dve.wait_ge(hi_ready, n + 1 if i is None else i * RING + (n + 1))
                nc.vector.tensor_tensor(w_lo[:, n % RING], raw[:, n % RAW], w_hi[:, n % RING].bitcast(F32),
                                        ALU.subtract).then_inc(lo_ready, 1)

            def xT_split(m, t):
                for h in range(2):
                    dve.wait_ge(xT_hi_ready, 4 * m + 2 * t + h + 1)
                    dst = (slice(None), slice(4 * h, 4 * h + 4), slice(t * P, (t + 1) * P))
                    nc.vector.tensor_tensor(xT_lo[dst], T[h].rearrange("p (k f) -> p k f", k=4),
                                            xT_hi[dst].bitcast(F32), ALU.subtract).then_inc(xT_lo_ready, 1)

            def norm(name, t):
                n, factor = NORMS[name]
                dve.wait_ge(y_done, 2 * n + t + 1)
                for h in range(2):
                    xs = x_tok[:, t, h * 512:(h + 1) * 512]
                    step(nc.vector.scalar_tensor_tensor(out=xs, in0=Y[t][h], scalar=factor, in1=xs,
                                                        op0=ALU.mult, op1=ALU.add))
                    step(nc.vector.bn_stats(stats[:, t, h], xs))
                nc.vector.bn_aggr(mv[:, t], stats[:, t].rearrange("p a b -> p (a b)")).then_inc(var_ready, 1)
                dve.wait_ge(var_ready, 2 * n + t + 1)
                dve.wait_ge(gb_landed, 32 * (n + 1))
                for h in range(2):
                    xs = x_tok[:, t, h * 512:(h + 1) * 512]
                    step(nc.vector.scalar_tensor_tensor(out=xs, in0=xs, scalar=mv[:, t, 0:1],
                                                        in1=ln_gb[:, 0, h * 512:(h + 1) * 512],
                                                        op0=ALU.subtract, op1=ALU.mult))
                dve.wait_ge(rstd_ready, 2 * n + t + 1)
                for h in range(2):
                    xs = x_tok[:, t, h * 512:(h + 1) * 512]
                    nc.vector.scalar_tensor_tensor(out=xs, in0=xs, scalar=rstd[:, t:t + 1],
                                                   in1=ln_gb[:, 1, h * 512:(h + 1) * 512],
                                                   op0=ALU.mult, op1=ALU.add).then_inc(x_ready, 1)

            def ffn_chunk_hidden(name, t, c):
                dve.wait_ge(silu_ready, c * 2 + (2 * SILUS[name] * NC + t + 1))
                nc.vector.tensor_tensor(ffn_tok[:, 1, t], G[t][:, FC:2 * FC], ffn_tok[:, 0, t],
                                        ALU.mult).then_inc(hid_ready, 1)

            def ffn_hidT(name, c, par):
                dve.wait_ge(hidT_hi, c + (SILUS[name] * NC + 1))
                nc.vector.tensor_tensor(hT_lo[:, par], T[0], hT_hi[:, par].bitcast(F32),
                                        ALU.subtract).then_inc(hidT_lo, 1)

            def ffn(name, m):
                s0 = phases[name]
                xT_split(m, 0)
                split_lo(s0 + 3)
                if m:
                    norm(ORDER[m - 1], 1)
                xT_split(m, 1)
                split_lo(s0 + 4)
                for t in range(TT):
                    ffn_chunk_hidden(name, t, 0)
                ffn_hidT(name, 0, 0)
                ffn_chunk(name, s0 + 5, None, 1, 1)
                with dve.Fori(0, NPAIR) as i:
                    for par in range(2):
                        ffn_chunk(name, s0 + 8 + 3 * par, i, i * 2 + (2 + par), par)
                ffn_chunk(name, s0 + FFN_UNITS - 1, None, NC - 1, 0)
                split_lo(s0 + FFN_UNITS + 2)
                norm(name, 0)

            def ffn_chunk(name, n, i, c, par):
                split_lo(n, i)
                ffn_chunk_hidden(name, 0, c)
                split_lo(n + 1, i)
                ffn_chunk_hidden(name, 1, c)
                split_lo(n + 2, i)
                ffn_hidT(name, c, par)

            def rope_tables():
                dve.wait_ge(S["ab_tables_landed"], 16 * 5)
                step(nc.vector.tensor_copy(sm[:, 0, 0, :], pos_i[:]))
                a3 = ang[:, 0].rearrange("p (t f) -> p t f", t=TT)
                for t in range(TT):
                    step(nc.vector.tensor_scalar(a3[:, t], invf, sm[:, 0, 0, t:t + 1], None, ALU.mult))
                step(nc.vector.tensor_scalar(ang[:, 1], ang[:, 0], 0.15915494309189535, ROUND, ALU.mult, ALU.add))
                step(nc.vector.tensor_scalar(ang[:, 2], ang[:, 1], ROUND, None, ALU.subtract))
                src = ang[:, 0]
                for part in (TWO_PI_1, TWO_PI_2, TWO_PI_3):
                    step(nc.vector.scalar_tensor_tensor(out=ang[:, 3], in0=ang[:, 2], scalar=-part, in1=src,
                                                        op0=ALU.mult, op1=ALU.add))
                    src = ang[:, 3]
                step(nc.vector.tensor_scalar(ang[:, 4], ang[:, 3], 3.1415925, -3.1415925, ALU.min, ALU.max))
                step(nc.vector.tensor_scalar(ang[:, 1], ang[:, 4], -1.0, None, ALU.mult))
                step(nc.vector.tensor_tensor(ang[:, 1], ang[:, 1], ang[:, 4], ALU.max))
                nc.vector.tensor_scalar(ang[:, 5], ang[:, 1], -1.0, 1.5707963267948966, ALU.mult, ALU.add
                                        ).then_inc(S["ang_ready"], 1)
                for a in range(2):
                    ins = nc.vector.tensor_tensor_reduce(out=ang[:, 2], in0=lamv[:, 2 * a], in1=lamv[:, 2 * a + 1],
                                                         scale=1.0, scalar=0.0, op0=ALU.mult, op1=ALU.add,
                                                         accum_out=lam[:, a:a + 1])
                    if a == 0:
                        step(ins)
                    else:
                        ins.then_inc(S["lam_prod"], 1)

            def rope(j, t, i):
                dve.wait_ge(chunk_done[t], CHUNKS_BEFORE["AB"] + j + 1)
                g = G[t].rearrange("p (h a f) -> p h a f", h=8, a=2)
                o = qk_rot[:, i, t].rearrange("p (h a f) -> p h a f", h=8, a=2)
                tmp = rope_tmp.rearrange("p (h a f) -> p h a f", h=8, a=2)
                sn = sincos[:, 0, t].unsqueeze(1).to_broadcast([P, 8, 32])
                cs = sincos[:, 1, t].unsqueeze(1).to_broadcast([P, 8, 32])
                for a in range(2):
                    nc.vector.tensor_tensor(o[:, :, a], g[:, :, a], cs, ALU.mult)
                if 2 * i + t:
                    dve.wait_ge(S["rope_done"], 2 * i + t)
                for a in range(2):
                    ins = nc.vector.tensor_tensor(tmp[:, :, a], g[:, :, 1 - a], sn, ALU.mult)
                step(ins)
                nc.vector.tensor_tensor(o[:, :, 0], o[:, :, 0], tmp[:, :, 0], ALU.subtract)
                nc.vector.tensor_tensor(o[:, :, 1], o[:, :, 1], tmp[:, :, 1], ALU.add).then_inc(S["rope_done"], 1)

            def mix_ab(m):
                s0 = phases["AB"]
                xT_split(m, 0)
                norm(ORDER[m - 1], 1)
                xT_split(m, 1)
                rope_tables()
                for j, c in enumerate(AB_CHUNKS):
                    for t in range(TT):
                        split_lo(s0 + AHEAD + 2 * j + t)
                        if c in (0, 1):
                            if c == 0 and t == 0:
                                dve.wait_ge(S["sincos_ready"], 1)
                            rope(j, t, c)
                dve.wait_ge(S["lam_exp"], 1)
                step(nc.vector.tensor_tensor(lam[:, 4:5], lam[:, 3:4], lam[:, 2:3], ALU.subtract))
                step(nc.vector.tensor_scalar(lam[:, 5:6], lam[:, 4:5], LAMBDA_INIT, None, ALU.subtract))
                step(nc.vector.tensor_scalar(cols[:, 0:1], cols[:, 0:1], 1.0 - LAMBDA_INIT, None, ALU.mult))
                for g in range(4):
                    dve.wait_ge(S["poolT_hi"], 2 * (g // 2) + 2)
                    nc.vector.scalar_tensor_tensor(
                        out=xT_lo[:, 4 + g], in0=bank[2 + g // 2][:, (g % 2) * SEQ:(g % 2 + 1) * SEQ],
                        scalar=cols[:, 2 + g:3 + g], in1=xT_hi[:, 4 + g].bitcast(F32),
                        op0=ALU.mult, op1=ALU.subtract).then_inc(S["poolT_lo"], 1)
                for it in range(2 * HEADS_A):
                    h, t = it // 2, it % 2
                    L = P * (t + 1)
                    b = pair[it % 2]
                    dve.wait_ge(S["score_done"], it + 1)
                    step(nc.vector.tensor_tensor(b[:, :, t * P:L], b[:, :, t * P:L],
                                                 causal[:].unsqueeze(1).to_broadcast([P, 2, P]), ALU.add))
                    step(nc.vector.tensor_reduce(sm[:, 0, it % 2], b[:, :, 0:L], AX.X, ALU.max))
                    nc.vector.tensor_scalar(sm[:, 1, it % 2], sm[:, 0, it % 2], -SM_SCALE, None, ALU.mult
                                            ).then_inc(S["prob_bias"], 1)
                    dve.wait_ge(S["prob_ready"], 2 * it + 2)
                    step(nc.vector.reciprocal(sm[:, 3, it % 2], sm[:, 2, it % 2]))
                    step(nc.vector.tensor_scalar(sm[:, 3, it % 2, 1:2], sm[:, 3, it % 2, 1:2], lam[:, 5:6], None,
                                                 ALU.mult))
                    if it >= 2:
                        dve.wait_ge(S["wT_done"], it - 1)
                    step(nc.vector.tensor_scalar(wts[:, it % 2, 0:L], probs[:, it % 2, 0, 0:L],
                                                 sm[:, 3, it % 2, 0:1], None, ALU.mult))
                    nc.vector.scalar_tensor_tensor(out=wts[:, it % 2, 0:L], in0=probs[:, it % 2, 1, 0:L],
                                                   scalar=sm[:, 3, it % 2, 1:2], in1=wts[:, it % 2, 0:L],
                                                   op0=ALU.mult, op1=ALU.add).then_inc(S["w_ready"], 1)
                for t in range(TT):
                    dve.wait_ge(S["o_copied"], t + 1)
                    for h in range(4):
                        ins = nc.vector.tensor_tensor_reduce(
                            out=rope_tmp[:, h * P:(h + 1) * P], in0=o_tok[:, t, h * P:(h + 1) * P],
                            in1=o_tok[:, t, h * P:(h + 1) * P], scale=1.0, scalar=0.0, op0=ALU.mult, op1=ALU.add,
                            accum_out=ssq[:, 0, 4 * t + h:4 * t + h + 1])
                    ins.then_inc(S["o_ssq"], 1)
                    dve.wait_ge(S["o_rms"], t + 1)
                    o3 = o_tok[:, t].rearrange("p (h f) -> p h f", h=4)
                    nc.vector.tensor_tensor(o3, o3, ssq[:, 1, 4 * t:4 * t + 4].unsqueeze(2).to_broadcast([P, 4, P]),
                                            ALU.mult).then_inc(S["o_ready"], 1)
                for t in range(TT):
                    dve.wait_ge(S["oT_hi"], t + 1)
                    nc.vector.scalar_tensor_tensor(
                        out=xT_lo[:, 0:4, t * P:(t + 1) * P], in0=T[t].rearrange("p (h f) -> p h f", h=4),
                        scalar=cols[:, 0:1], in1=xT_hi[:, 0:4, t * P:(t + 1) * P].bitcast(F32),
                        op0=ALU.mult, op1=ALU.subtract).then_inc(S["oT_lo"], 1)
                for j in range(4):
                    split_lo(s0 + AHEAD + 2 * len(AB_CHUNKS) + j)
                norm("AB", 0)

            def lower_bound():
                g0, g1 = val.rearrange("p t f -> p (t f)"), gate.rearrange("p t f -> p (t f)")
                dve.wait_ge(S["gamma_landed"], 32)
                lb, rest = ln_gb[:, 0], ln_gb[:, 1]
                step(nc.vector.tensor_tensor(lb, g0, g1, ALU.max))
                nc.vector.tensor_tensor(g0, g0, lb, ALU.subtract)
                nc.vector.tensor_tensor(g1, g1, lb, ALU.subtract).then_inc(S["lb_arg"], 1)
                dve.wait_ge(S["lb_exp"], 2)
                step(nc.vector.tensor_tensor(rest, g0, g1, ALU.add))
                step(nc.vector.reciprocal(rest, rest))
                step(nc.vector.tensor_tensor(lb, rest, g1, ALU.mult))
                nc.vector.tensor_tensor(rest, rest, g0, ALU.mult).then_inc(S["lb_ready"], 1)
                dve.wait_ge(S["lb_ready"], 1)

            def mix_c(m):
                s0 = phases["C"]
                xT_split(m, 0)
                norm(ORDER[m - 1], 1)
                xT_split(m, 1)
                dve.wait_ge(S["c_tables_landed"], 16)
                nc.vector.tensor_copy(decay[:], stage[:, 0:N_DECAY])
                step(nc.vector.tensor_copy(level_mask[:], stage[:, N_DECAY:]))
                nc.vector.memset(scT, 0.0).then_inc(S["c_tab_ready"], 1)
                dve.wait_ge(S["c_tab_ready"], 1)
                lower_bound()
                for hf in range(2):
                    lb_row = [ln_gb[:, a, hf * 512:(hf + 1) * 512] for a in range(2)]
                    for j, kind in enumerate("fqig"):
                        for t in range(TT):
                            split_lo(s0 + AHEAD + 8 * hf + 2 * j + t)
                        if kind == "f":
                            for t in range(TT):
                                f = logf[:, t]
                                dve.wait_ge(S["sig_ready"], 2 * hf + t + 1)
                                step(nc.vector.tensor_tensor(f, f, lb_row[1], ALU.mult))
                                step(nc.vector.tensor_tensor(k_tok[:, t], lb_row[1], f, ALU.subtract))
                                nc.vector.scalar_tensor_tensor(out=f, in0=f, scalar=1e-18, in1=lb_row[0],
                                                               op0=ALU.max, op1=ALU.add).then_inc(S["f_ready"], 1)
                            for t in range(TT):
                                dve.wait_ge(S["logf_hi"], 2 * hf + t + 1)
                                nc.vector.tensor_tensor(hT_lo[:, t], logf[:, t], hT_hi[:, t].bitcast(F32),
                                                        ALU.subtract).then_inc(S["logf_lo"], 1)
                    for hh in range(4):
                        hd = 4 * hf + hh
                        head(hf, hh, hd)
                for i in range(4):
                    hf, t = i // 2, i % 2
                    dst = (slice(None), slice(4 * hf, 4 * hf + 4), slice(t * P, (t + 1) * P))
                    dve.wait_ge(S["c_oT_hi"], i + 1)
                    nc.vector.scalar_tensor_tensor(
                        out=xT_lo[dst], in0=T[t].rearrange("p (h f) -> p h f", h=4), scalar=cols[:, 1:2],
                        in1=xT_hi[dst].bitcast(F32), op0=ALU.mult, op1=ALU.subtract).then_inc(S["c_oT_lo"], 1)
                for j in range(4):
                    split_lo(s0 + AHEAD + 2 * len(C_CHUNKS) + j)
                norm("C", 0)

            def head(hf, hh, hd):
                dve.wait_ge(S["c_qkT_ready"], hd + 1)
                dve.wait_ge(S["expo_ready"], 2 * hd + 2)
                nc.vector.tensor_tensor(fac[:, 0, 0], fac[:, 0, 0], qkT[:, 1, 0], ALU.mult)
                nc.vector.tensor_tensor(fac[:, 1, 0], fac[:, 1, 0], qkT[:, 0, 1], ALU.mult)
                for l, half in enumerate(LEVELS):
                    for side in range(2):
                        v = fac[:, :, 1 + l].rearrange("p t (n s j) -> p t n s j", s=2, j=half)[:, :, :, side]
                        o = qkT[:, 1 - side].rearrange("p t (n s j) -> p t n s j", s=2, j=half)[:, :, :, side]
                        ins = nc.vector.tensor_tensor(v, v, o, ALU.mult)
                ins.then_inc(S["fac_ready"], 1)
                for t in range(TT):
                    dve.wait_ge(S["lvl_done"], 2 * hd + t + 1)
                    if hd:
                        dve.wait_ge(S["co_done"], hd)
                    for l in range(NL + 1):
                        ins = nc.vector.copy_predicated(scT[:, t], level_mask[:, l],
                                                        bank[1 + l // 4][:, (l % 4) * P:(l % 4 + 1) * P])
                        if l < NL:
                            step(ins)
                    ins.then_inc(S["sc_ready"], 1)
                dve.wait_ge(S["co_copied"], hd + 1)
                for t in range(TT):
                    ins = nc.vector.tensor_tensor_reduce(out=o_sq, in0=o_raw[:, t], in1=o_raw[:, t], scale=1.0,
                                                         scalar=0.0, op0=ALU.mult, op1=ALU.add,
                                                         accum_out=ssq[:, 0, t:t + 1])
                    if t == 0:
                        step(ins)
                ins.then_inc(S["c_ssq"], 1)
                dve.wait_ge(S["c_rms"], hd + 1)
                dve.wait_ge(S["gate_ready"], 2 * hf + 2)
                for t in range(TT):
                    nc.vector.scalar_tensor_tensor(out=o_half[hf][:, t, hh * P:(hh + 1) * P], in0=o_raw[:, t],
                                                   scalar=ssq[:, 1, t:t + 1], in1=gate[:, t, hh * P:(hh + 1) * P],
                                                   op0=ALU.mult, op1=ALU.mult).then_inc(S["c_on"], 1)

            for n in range(AHEAD):
                split_lo(n)
            for m, name in enumerate(ORDER):
                if name == "AB":
                    mix_ab(m)
                elif name == "C":
                    mix_c(m)
                else:
                    ffn(name, m)
            norm(ORDER[-1], 1)

        @block.gpsimd
        def _(pool):
            steps = [0]

            def step(ins):
                steps[0] += 1
                ins.then_inc(pool_step, 1)
                pool.wait_ge(pool_step, steps[0])

            pool.dma_start(ident[:], consts[:, C_ID:C_ID + P]).then_inc(const_landed, 16)
            for t in range(TT):
                pool.dma_start(x_tok[:, t], x[0, t * P:(t + 1) * P]).then_inc(x_landed, 16)
            step(nc.gpsimd.memset(mhalf[:], -0.5))

            def load_gb(n):
                l, j = divmod(n, 3)
                for a, src in enumerate((ln_gain, ln_bias)):
                    pool.dma_start(ln_gb[:, a], src[l, j:j + 1].to_broadcast([P, D])).then_inc(gb_landed, 16)

            def norm(n):
                for t in range(TT):
                    pool.wait_ge(var_ready, 2 * n + t + 1)
                    step(nc.gpsimd.tensor_scalar(veps[:, t:t + 1], mv[:, t, 1:2], 1.0, LN_EPS / ALPHA ** 2,
                                                 ALU.mult, ALU.add))
                    nc.gpsimd.tensor_tensor(rstd[:, t:t + 1], veps[:, t:t + 1], mhalf[:, 0:1], ALU.pow
                                            ).then_inc(rstd_ready, 1)

            load_gb(0)
            with nc.allow_non_contiguous_dma(reason="a few columns of parameters"):
                pool.dma_start(causal[:], consts[:, C_CAUSAL:C_CAUSAL + P]).then_inc(S["ab_tables_landed"], 16)
                pool.dma_start(pos_i[:], positions[0].rearrange("(t p) -> p t", p=P)
                               ).then_inc(S["ab_tables_landed"], 16)
                pool.dma_start(invf, consts[:, C_INVF:C_INVF + 32]).then_inc(S["ab_tables_landed"], 16)
                pool.dma_start(lamv.rearrange("p a b -> p (a b)"),
                               diff_lambda.rearrange("n a b -> n (a b)").to_broadcast([P, 256])
                               ).then_inc(S["ab_tables_landed"], 16)
                pool.dma_start(cols[:, 0:1], diff_subln.rearrange("n p -> p n")).then_inc(S["ab_tables_landed"], 16)
                pool.dma_start(cols[:, 1:2], c_norm.rearrange("n p -> p n")).then_inc(S["setup_pool"], 16)
                pool.dma_start(cols[:, 2:6], pool_scale[0].rearrange("(g p) -> p g", p=P)
                               ).then_inc(S["setup_pool"], 16)
                pool.dma_start(poolw, pool_w[0].rearrange("g p f -> p g f")).then_inc(S["setup_pool"], 16)
                pool.dma_start(band, consts[:, C_BAND:C_DECAY].rearrange("p (g f) -> p g f", g=4)
                               ).then_inc(S["setup_pool"], 16)
            for n, name in enumerate(ORDER):
                if name == "AB":
                    for t in range(TT):
                        pool.wait_ge(S["o_ssq"], t + 1)
                        step(nc.gpsimd.tensor_scalar(ssq[:, 0, 4 * t:4 * t + 4], ssq[:, 0, 4 * t:4 * t + 4], 1.0 / P,
                                                     LN_EPS, ALU.mult, ALU.add))
                        nc.gpsimd.tensor_tensor(ssq[:, 1, 4 * t:4 * t + 4], ssq[:, 0, 4 * t:4 * t + 4],
                                                mhalf[:, 0:4], ALU.pow).then_inc(S["o_rms"], 1)
                if name == "C":
                    for hd in range(8):
                        pool.wait_ge(S["c_ssq"], hd + 1)
                        step(nc.gpsimd.tensor_scalar(ssq[:, 0, 0:2], ssq[:, 0, 0:2], 1.0 / P, LN_EPS,
                                                     ALU.mult, ALU.add))
                        nc.gpsimd.tensor_tensor(ssq[:, 1, 0:2], ssq[:, 0, 0:2], mhalf[:, 0:2], ALU.pow
                                                ).then_inc(S["c_rms"], 1)
                    load_gb(n)
                norm(n)
                pool.wait_ge(x_ready, 4 * (n + 1))
                if n + 1 < len(ORDER) and ORDER[n + 1] != "C":
                    load_gb(n + 1)
                if name == "AB":
                    pool.dma_start(stage.rearrange("p a b -> p (a b)"), consts[:, C_DECAY:C_END]
                                   ).then_inc(S["c_tables_landed"], 16)
                    for l, dst in enumerate((val, gate)):
                        pool.dma_start(dst.rearrange("p t f -> p (t f)"), hgrn_gamma[l:l + 1].to_broadcast([P, D])
                                       ).then_inc(S["gamma_landed"], 16)

        @block.tensor
        def _(pe):
            def xT(m, t):
                for h in range(2):
                    if m:
                        pe.wait_ge(x_ready, 4 * (m - 1) + 2 * t + h + 1)
                    elif h == 0:
                        pe.wait_ge(x_landed, 32)
                    if t:
                        pe.wait_ge(xT_lo_ready, 4 * m + h + 1)
                    for k in range(4):
                        ins = nc.tensor.transpose(T[h][:, k * P:(k + 1) * P],
                                                  x_tok[:, t, (4 * h + k) * P:(4 * h + k + 1) * P], ident[:])
                    ins.then_inc(xT_done, 1)

            def three_passes(dst, a_hi, a_lo, b_hi, b_lo, first, last):
                nc.tensor.matmul(dst, a_hi, b_hi, start=first, stop=False)
                nc.tensor.matmul(dst, a_hi, b_lo, start=False, stop=False)
                return nc.tensor.matmul(dst, a_lo, b_hi, start=False, stop=last)

            def project(n, i, t):
                for kh in range(2):
                    pe.wait_ge(lo_ready, n + kh + 1 if i is None else i * RING + (n + kh + 1))
                    slot = (n + kh) % RING
                    for k in range(4):
                        kk, ts = 4 * kh + k, slice(t * P, (t + 1) * P)
                        ins = three_passes(G[t], xT_hi[:, kk, ts], xT_lo[:, kk, ts],
                                           w_hi[:, slot, k * 512:(k + 1) * 512], w_lo[:, slot, k * 512:(k + 1) * 512],
                                           kk == 0, kk == KB - 1)
                    if t == TT - 1 and kh == 0:
                        ins.then_inc(unit_used, 1)
                return ins

            def rows(n, i, t, a_hi, a_lo, first, last, free):
                pe.wait_ge(lo_ready, n + 1 if i is None else i * RING + (n + 1))
                slot = n % RING
                for k in range(2):
                    for h in range(2):
                        cs = slice(k * D + h * 512, k * D + (h + 1) * 512)
                        ins = three_passes(Y[t][h], a_hi(k), a_lo(k), w_hi[:, slot, cs], w_lo[:, slot, cs],
                                           first and k == 0, last and k == 1)
                if free and not last:
                    ins.then_inc(unit_used, 1)
                return ins

            def down(name, n, i, c, par, t, first, last):
                if t == 0:
                    pe.wait_ge(hidT_lo, c + (SILUS[name] * NC + 1))
                o = t * P
                return rows(n, i, t, lambda k: hT_hi[:, par, k * SEQ + o:k * SEQ + o + P],
                            lambda k: hT_lo[:, par, k * SEQ + o:k * SEQ + o + P], first, last, t == TT - 1)

            def hidden_T(name, c):
                for t in range(TT):
                    pe.wait_ge(hid_ready, c * 2 + (2 * SILUS[name] * NC + t + 1))
                    for j in range(2):
                        ins = nc.tensor.transpose(T[0][:, j * SEQ + t * P:j * SEQ + (t + 1) * P],
                                                  ffn_tok[:, 1, t, j * P:(j + 1) * P], ident[:])
                ins.then_inc(hidT_done, 1)

            def ffn(name, m):
                s0 = phases[name]
                for t in range(TT):
                    xT(m, t)
                    pe.wait_ge(xT_lo_ready, 4 * m + 2 * t + 2)
                    project(s0, None, t).then_inc(chunk_done[t], 1)
                hidden_T(name, 0)
                chunk(name, s0 + 2, None, 1, 0, True)
                with pe.Fori(0, NPAIR) as i:
                    for par in range(2):
                        chunk(name, s0 + 5 + 3 * par, i, i * 2 + (2 + par), (1 + par) % 2, False)
                a, c = s0 + FFN_UNITS - 4, NC - 1
                gate_up(name, a, None, c)
                down(name, a + 2, None, c - 1, (c - 1) % 2, 0, False, False)
                hidden_T(name, c)
                down(name, a + 2, None, c - 1, (c - 1) % 2, 1, False, False)
                for t in range(TT):
                    down(name, a + 3, None, c, c % 2, t, False, True).then_inc(y_done, 1)

            def gate_up(name, n, i, c):
                for t in range(TT):
                    pe.wait_ge(hid_ready, c * 2 + (2 * SILUS[name] * NC - 1 + t))
                    project(n, i, t).then_inc(chunk_done[t], 1)

            def chunk(name, n, i, c, par, first):
                gate_up(name, n, i, c)
                for t in range(TT):
                    down(name, n + 2, i, c - 1, par, t, first, False)
                hidden_T(name, c)

            def out_project(n, m):
                for t in range(TT):
                    ts = slice(t * P, (t + 1) * P)
                    for j in range(4):
                        ins = rows(n + j, None, t, lambda k: xT_hi[:, 2 * j + k, ts], lambda k: xT_lo[:, 2 * j + k, ts],
                                   j == 0, j == 3, t == TT - 1)
                    ins.then_inc(y_done, 1)

            def mix_ab(m):
                s0 = phases["AB"]
                read_by = {3: "u_ready", 0: "rope_done", 1: "rope_done", 2: "v_ready"}
                reads = {3: 0, 0: 0, 1: 2, 2: 0}
                for j, c in enumerate(AB_CHUNKS):
                    for t in range(TT):
                        if j == 0:
                            xT(m, t)
                            pe.wait_ge(xT_lo_ready, 4 * m + 2 * t + 2)
                        else:
                            b = AB_CHUNKS[j - 1]
                            pe.wait_ge(S[read_by[b]], reads[b] + t + 1)
                        project(s0 + 2 * j, None, t).then_inc(chunk_done[t], 1)
                    if c == 0:
                        pe.wait_ge(S["u_ready"], 2)
                        pe.wait_ge(S["setup_pool"], 16 * 4)
                        for g in range(4):
                            dst, us = bank[g // 2][:, (g % 2) * SEQ:(g % 2 + 1) * SEQ], slice(g * P, (g + 1) * P)
                            nc.tensor.matmul(dst, u_tok[:, 0, us], band[:, g, 0:SEQ], start=True, stop=False)
                            ins = nc.tensor.matmul(dst[:, P:SEQ], u_tok[:, 1, us], band[:, g, SEQ:],
                                                   start=False, stop=True)
                            if g % 2:
                                ins.then_inc(S["dT_done"], 1)
                for b in range(2):
                    pe.wait_ge(S["dT_ready"], b + 1)
                    for g in (2 * b, 2 * b + 1):
                        ins = nc.tensor.matmul(bank[2 + b][:, (g % 2) * SEQ:(g % 2 + 1) * SEQ], poolw[:, g], dT[:, g],
                                               start=True, stop=True)
                    ins.then_inc(S["poolT_done"], 1)
                pe.wait_ge(S["rope_done"], 4)
                for i in range(4):
                    if i >= 2:
                        pe.wait_ge(S["v_ready"], i - 1)
                    b = (bank[0], bank[1], bank[4], bank[5])[i]
                    for h in range(HEADS_A):
                        ins = nc.tensor.transpose(b[:, h * P:(h + 1) * P], qk_rot[:, i // 2, i % 2, h * P:(h + 1) * P],
                                                  ident[:])
                    ins.then_inc(S["qkT_done"], 1)
                pe.wait_ge(S["qkT_ready"], 4)
                pe.wait_ge(S["poolT_lo"], 4)

                def scores(it):
                    h, t = it // 2, it % 2
                    if it >= 2:
                        pe.wait_ge(S["prob_ready"], 2 * it - 2)
                    for c in range(2):
                        rs = slice(64 * c, 64 * c + 64)
                        ins = nc.tensor.matmul(bank[2 * (it % 2) + c][:, 0:P * (t + 1)],
                                               qT[rs, h, t * P:(t + 1) * P], kT[rs, h, 0:P * (t + 1)],
                                               start=True, stop=True)
                    ins.then_inc(S["score_done"], 1)

                def weigh(it):
                    h, t = it // 2, it % 2
                    pe.wait_ge(S["w_ready"], it + 1)
                    for kb in range(t + 1):
                        ins = nc.tensor.transpose(T[it % 2][:, kb * P:(kb + 1) * P],
                                                  wts[:, it % 2, kb * P:(kb + 1) * P], ident[:])
                    ins.then_inc(S["wT_done"], 1)
                    pe.wait_ge(S["wT_ready"], it + 1)
                    for kb in range(t + 1):
                        ins = nc.tensor.matmul(bank[4 + t][:, h * P:(h + 1) * P], wT[:, it % 2, kb * P:(kb + 1) * P],
                                               v_tok[:, kb, h * P:(h + 1) * P], start=kb == 0, stop=kb == t)
                    if h == HEADS_A - 1:
                        ins.then_inc(S["o_done"], 1)

                scores(0)
                for it in range(2 * HEADS_A):
                    if it + 1 < 2 * HEADS_A:
                        scores(it + 1)
                    weigh(it)
                for t in range(TT):
                    pe.wait_ge(S["o_ready"], t + 1)
                    for h in range(HEADS_A):
                        ins = nc.tensor.transpose(T[t][:, h * P:(h + 1) * P], o_tok[:, t, h * P:(h + 1) * P], ident[:])
                    ins.then_inc(S["oT_done"], 1)
                pe.wait_ge(S["oT_lo"], 2)
                out_project(s0 + 2 * len(AB_CHUNKS), m)

            def mix_c(m):
                s0 = phases["C"]
                read_by = ("sig_ready", "q_ready", "val_ready", "gate_ready")
                for hf in range(2):
                    for j in range(4):
                        jj = 4 * hf + j
                        for t in range(TT):
                            if jj == 0:
                                xT(m, t)
                                pe.wait_ge(xT_lo_ready, 4 * m + 2 * t + 2)
                            else:
                                pe.wait_ge(S[read_by[(j - 1) % 4]], 2 * ((jj - 1) // 4) + t + 1)
                            project(s0 + 2 * jj, None, t).then_inc(chunk_done[t], 1)
                    for hh in range(4):
                        head(hf, hh, 4 * hf + hh)
                for i in range(4):
                    hf, t = i // 2, i % 2
                    if i == 0:
                        pe.wait_ge(S["c_on"], 16)
                    if i >= 2:
                        pe.wait_ge(S["c_oT_lo"], i - 1)
                    for h in range(4):
                        ins = nc.tensor.transpose(T[t][:, h * P:(h + 1) * P], o_half[hf][:, t, h * P:(h + 1) * P],
                                                  ident[:])
                    ins.then_inc(S["c_oT_done"], 1)
                pe.wait_ge(S["c_oT_lo"], 4)
                out_project(s0 + 2 * len(C_CHUNKS), m)

            def head(hf, hh, hd):
                hs = slice(hh * P, (hh + 1) * P)
                pe.wait_ge(S["q_ready"], 2 * hf + 2)
                pe.wait_ge(S["f_ready"], 2 * hf + 2)
                if hd:
                    pe.wait_ge(S["st_ready"], hd)
                for a, src in enumerate((q_tok, k_tok)):
                    for t in range(TT):
                        ins = nc.tensor.transpose(bank[0][:, (2 * a + t) * P:(2 * a + t + 1) * P], src[:, t, hs],
                                                  ident[:])
                ins.then_inc(S["c_qkT_done"], 1)
                pe.wait_ge(S["logf_lo"], 2 * hf + 2)
                for t in range(TT):
                    if hd or t:
                        pe.wait_ge(S["expo_ready"], 2 * hd + t)
                    parts = (((0, 0, 4), (1, 4, 8)) if t == 0 else ((0, 8, 9), (0, 1, 4), (1, 4, 8)))
                    for b, d0, d1 in parts:
                        c0 = P if (d0, d1) == (1, 4) else 0
                        dst = bank[6 + b][:, c0:c0 + (d1 - d0) * P]
                        rhs = decay[:, d0:d1].rearrange("p l f -> p (l f)")
                        nc.tensor.matmul(dst, hT_hi[:, t, hs], rhs, start=True, stop=False)
                        ins = nc.tensor.matmul(dst, hT_lo[:, t, hs], rhs, start=False, stop=True)
                    ins.then_inc(S["expo_done"], 1)
                pe.wait_ge(S["fac_ready"], hd + 1)
                for t in range(TT):
                    if hd or t:
                        pe.wait_ge(S["sc_ready"], 2 * hd + t)
                    for l in range(NL + 1):
                        k_side = fac[:, t, 1 + l] if l < NL else qkT[:, 1, t]
                        q_side = fac[:, t, 1 + l] if l < NL else qkT[:, 0, t]
                        ins = nc.tensor.matmul(bank[1 + l // 4][:, (l % 4) * P:(l % 4 + 1) * P], k_side, q_side,
                                               start=True, stop=True)
                    ins.then_inc(S["lvl_done"], 1)
                nc.tensor.transpose(bank[0][:, 0:P], fac[:, 0, 0], ident[:]).then_inc(S["klT_done"], 1)
                pe.wait_ge(S["klT_ready"], hd + 1)
                pe.wait_ge(S["val_ready"], 2 * hf + 2)
                nc.tensor.matmul(bank[0][:, 0:P], klT, val[:, 0, hs], start=True, stop=True).then_inc(S["st_done"], 1)
                pe.wait_ge(S["st_ready"], hd + 1)
                pe.wait_ge(S["sc_ready"], 2 * hd + 2)
                if hd:
                    pe.wait_ge(S["co_copied"], hd)
                nc.tensor.matmul(bank[3][:, 0:P], scT[:, 0], val[:, 0, hs], start=True, stop=True)
                nc.tensor.matmul(bank[3][:, P:2 * P], scT[:, 1], val[:, 1, hs], start=True, stop=False)
                nc.tensor.matmul(bank[3][:, P:2 * P], fac[:, 1, 0], state, start=False, stop=True
                                 ).then_inc(S["co_done"], 1)

            pe.wait_ge(const_landed, 16)
            for m, name in enumerate(ORDER):
                if name == "AB":
                    mix_ab(m)
                elif name == "C":
                    mix_c(m)
                else:
                    ffn(name, m)


def shape_constants():
    import numpy as np
    c = np.zeros((P, C_END), np.float32)
    p, f = np.arange(P)[:, None], np.arange(P)[None, :]
    c[:, C_ID:C_ID + P] = p == f
    c[:, C_CAUSAL:C_CAUSAL + P] = np.where(f <= p, 0.0, NEG)
    c[:, C_INVF:C_INVF + 32] = (10000.0 ** (-np.arange(0, 64, 2) / 64)).astype(np.float32)
    tok = np.arange(SEQ)[None, :]
    for g, w in enumerate(POOLS):
        b = np.zeros((SEQ, SEQ))
        s = np.arange(SEQ)[:, None]
        b += np.where((s <= tok) & (s > tok - w), 1.0 / np.minimum(tok + 1, w), 0.0)
        b -= s == tok
        c[:, C_BAND + g * 3 * P:C_BAND + g * 3 * P + SEQ] = b[0:P]
        c[:, C_BAND + g * 3 * P + SEQ:C_BAND + (g + 1) * 3 * P] = b[P:, P:]
    decay = [p > f]
    mask = []
    for half in LEVELS:
        mid = f // (2 * half) * (2 * half) + half
        decay.append(np.where(f >= mid, (p >= mid) & (p <= f), (p > f) & (p < mid)))
        same = p // (2 * half) == f // (2 * half)
        mask.append(same & (p % (2 * half) < half) & (f % (2 * half) >= half))
    decay.append(p <= f)
    mask.append(p == f)
    for i, a in enumerate(decay + mask):
        c[:, C_DECAY + i * P:C_DECAY + (i + 1) * P] = a
    return c


_INS = ["x", "positions", "ln_gain", "ln_bias", "ffn1_w_in", "ffn1_w_out", "ffn2_w_in", "ffn2_w_out", "ab_w_in",
        "ab_w_o", "diff_lambda", "diff_subln", "pool_w", "pool_scale", "c_w_in", "c_w_o", "c_norm", "hgrn_gamma"]


def kernel(**inputs):
    import numpy as np
    import concourse.bacc as bacc
    from concourse.bass_utils import run_bass_kernel_spmd

    nc = bacc.Bacc("TRN2", target_bir_lowering=False, num_devices=1)
    arrays, args = {}, []
    for name in _INS:
        a = np.ascontiguousarray(inputs[name])
        arrays[f"in_{name}"] = a
        args.append(nc.dram_tensor(f"in_{name}", a.shape, mybir.dt.from_np(a.dtype), kind="ExternalInput").ap())
    arrays["shape_constants"] = shape_constants()
    args.append(nc.dram_tensor("shape_constants", (P, C_END), F32, kind="ExternalInput").ap())
    args.append(nc.dram_tensor("out_x", (1, SEQ, D), F32, kind="ExternalOutput").ap())
    build(nc, *args)
    r = run_bass_kernel_spmd(nc, [arrays], core_ids=[0])
    return r.results[0]["out_x"]
```

```python
from contextlib import ExitStack

import concourse.bass as bass
from concourse import mybir

ALU = mybir.AluOpType
ACT = mybir.ActivationFunctionType
AX = mybir.AxisListType
F32 = mybir.dt.float32
F32R = mybir.dt.float32r
I32 = mybir.dt.int32
U8 = mybir.dt.uint8

P = 128
D = 1024
SEQ = 256
TT = SEQ // P
KB = D // P
D_FF = 2816
FC = 256
NC = D_FF // FC
NPAIR = (NC - 3) // 2
NH = NC + 1
HEADS_A = 4
POOLS = (2, 4, 8, 16)
UNIT = 2048
RAW = 3
RING = 6
LEVELS = (64, 32, 16, 8, 4, 2, 1)
NL = len(LEVELS)
N_DECAY = NL + 2
DEPTH = 2
ALPHA = (2 * DEPTH) ** 0.25
LN_EPS = 1e-5
LAMBDA_INIT = 0.2
SM_SCALE = 64 ** -0.5
TWO_PI_1, TWO_PI_2, TWO_PI_3 = 6.28125, 0.0019350051879882812, 3.019916050561733e-07
ROUND = 1.5 * 2.0 ** 23
NEG = -1e30

C_ID = 0
C_CAUSAL = C_ID + P
C_INVF = C_CAUSAL + P
C_BAND = C_INVF + 32
C_DECAY = C_BAND + 4 * 3 * P
C_MASK = C_DECAY + N_DECAY * P
C_END = C_MASK + (NL + 1) * P

ORDER = ("F0", "AB", "F1", "F2", "C", "F3")


def build(nc, x, positions, ln_gain, ln_bias, ffn1_w_in, ffn1_w_out, ffn2_w_in, ffn2_w_out, ab_w_in, ab_w_o,
          diff_lambda, diff_subln, pool_w, pool_scale, c_w_in, c_w_o, c_norm, hgrn_gamma, consts, out):
    with ExitStack() as ctx:
        def sb(name, shape, dt=F32):
            return ctx.enter_context(nc.sbuf_tensor(name, shape, dt))

        def sem(name):
            return ctx.enter_context(nc.semaphore(name))

        raw = sb("raw", [P, RAW, UNIT])
        w_hi = sb("w_hi", [P, RING, UNIT], F32R)
        w_lo = sb("w_lo", [P, RING, UNIT], F32R)
        x_tok = sb("x_tok", [P, TT, D])
        xT_hi = sb("xT_hi", [P, KB, SEQ], F32R)
        xT_lo = sb("xT_lo", [P, KB, SEQ], F32R)
        hT_hi = sb("hT_hi", [P, 2, 512], F32R)
        hT_lo = sb("hT_lo", [P, 2, 512], F32R)
        ffn_tok = sb("ffn_tok", [P, 2, TT, FC])
        ln_gb = sb("ln_gb", [P, 2, D])
        arena = sb("arena", [P, 8704])
        decay = sb("decay", [P, N_DECAY, P], F32R)
        level_mask = sb("level_mask", [P, NL + 1, P], U8)
        ident = sb("ident", [P, P])
        causal = sb("causal", [P, P])
        stats = sb("stats", [P, TT, 2, 6])
        mv = sb("mv", [P, TT, 2])
        veps = sb("veps", [P, TT])
        rstd = sb("rstd", [P, TT])
        mhalf = sb("mhalf", [P, 8])
        cols = sb("cols", [P, 8])
        lam = sb("lam", [P, 8])
        sm_max = sb("sm_max", [P, TT, 2, 2])
        sm_sum = sb("sm_sum", [P, TT, 2, HEADS_A])
        sm_fac = sb("sm_fac", [P, TT, 4])
        eps_sum = sb("eps_sum", [P, TT, HEADS_A])
        pos_f = sb("pos_f", [P, TT])
        ssq = sb("ssq", [P, 2, 8])
        pos_i = sb("pos_i", [P, TT], I32)

        psum = ctx.enter_context(nc.psum_tensor("psum", [P, 8, 512], F32))
        bank = [psum[:, i] for i in (0, 1, 4, 5, 2, 3, 6, 7)]
        pair = [psum[:, 2 * i:2 * i + 2] for i in (0, 2, 1, 3)]
        Y = [bank[0:2], bank[2:4]]
        G = bank[4:6]
        T = bank[6:8]

        raw_landed = [sem(f"raw_landed{i}") for i in range(RAW)]
        hi_ready, lo_ready, unit_used = sem("hi_ready"), sem("lo_ready"), sem("unit_used")
        x_landed, const_landed, gb_landed = sem("x_landed"), sem("const_landed"), sem("gb_landed")
        chunk_done = [sem(f"chunk_done{t}") for t in range(TT)]
        silu_ready, hid_ready, hidT_done, hidT_hi, hidT_lo = (
            sem("silu_ready"), sem("hid_ready"), sem("hidT_done"), sem("hidT_hi_ready"), sem("hidT_lo_ready"))
        y_done, var_ready, rstd_ready, x_ready = sem("y_done"), sem("var_ready"), sem("rstd_ready"), sem("x_ready")
        gb_used = sem("gb_used")
        xT_done, xT_hi_ready, xT_lo_ready = sem("xT_done"), sem("xT_hi_ready"), sem("xT_lo_ready")
        dve_step, act_step, pool_step = sem("dve_step"), sem("act_step"), sem("pool_step")
        out_stored = sem("out_stored")
        S = {n: sem(n) for n in (
            "setup_pool", "ab_tables_landed", "rope_done", "mixA_evac", "u_ready", "v_ready", "dT_done", "dT_ready", "poolT_done",
            "poolT_hi", "poolT_lo", "qk_done", "qkT_done", "qkT_ready", "score_done", "prob_bias", "prob_ready",
            "w_ready", "wT_done", "wT_ready", "o_done", "eps_ready", "o_ssq", "o_rms", "o_ready", "oT_done", "oT_hi", "oT_lo",
            "ang_ready", "sincos_ready", "lam_prod", "lam_exp",
            "c_tables_landed", "gamma_landed", "gamma_used", "lb_arg", "lb_exp", "lb_ready", "sig_ready", "f_ready",
            "logf_ready", "logf_hi", "logf_lo", "q_ready", "val_ready", "gate_ready", "c_tab_ready",
            "c_kqT_done", "c_kqT_ready", "gate_sig", "expo_done", "expo_ready", "fac_ready", "lvl_done", "sc_ready",
            "klT_done", "klT_ready", "st_done", "st_ready", "co_done", "co_copied", "c_ssq", "c_rms", "c_on",
            "c_oT_done", "c_oT_hi", "c_oT_lo", "c_half_done")}

        FFN_UNITS = 3 * NC
        AB_CHUNKS = (0, 1, 2, 3)
        OUT_UNITS = {"AB": (2, 3, 0, 1), "C": (0, 1, 2, 3)}
        GROUPS = 4
        SLOTS = [((0, 0), (1, 0), (0, 1), (1, 1))] + [((0, 0), (0, 1), (1, 0), (1, 1))] * (GROUPS - 1)
        C_CHUNKS = tuple((g, j) for g in range(GROUPS) for j in range(2))
        phases, at = {}, 0
        for name, n in (("F0", FFN_UNITS), ("AB", 2 * len(AB_CHUNKS) + 4), ("F1", FFN_UNITS), ("F2", FFN_UNITS),
                        ("C", 2 * len(C_CHUNKS) + 4), ("F3", FFN_UNITS)):
            if name in ORDER:
                phases[name] = at
                at += n
        N_UNITS = at
        AHEAD = 3

        FFN = {"F0": (0, ffn1_w_in, ffn1_w_out), "F1": (0, ffn2_w_in, ffn2_w_out),
               "F2": (1, ffn1_w_in, ffn1_w_out), "F3": (1, ffn2_w_in, ffn2_w_out)}
        NORMS = {"F0": (0, 0.5 / ALPHA), "AB": (1, 1.0 / ALPHA), "F1": (2, 0.5 / ALPHA),
                 "F2": (3, 0.5 / ALPHA), "C": (4, 1.0 / ALPHA), "F3": (5, 0.5 / ALPHA)}
        SILUS = {"F0": 0, "F1": 1, "F2": 2, "F3": 3}

        BEFORE_C = "F2" if "C" in ORDER else None
        BEFORE_AB = "F0" if "AB" in ORDER else None
        CHUNKS_BEFORE, n = {}, 0
        for name in ORDER:
            CHUNKS_BEFORE[name] = n
            n += {"AB": len(AB_CHUNKS), "C": len(C_CHUNKS)}.get(name, NC)

        used_by = []
        n_used = n_chunk = 0
        for m, name in enumerate(ORDER):
            if name in FFN:
                kinds = "AB" + "ABO" * (NC - 1) + "Y"
            else:
                kinds = "AB" * len(AB_CHUNKS if name == "AB" else C_CHUNKS) + "OOOY"
            for kind in kinds:
                if kind in "AO":
                    n_used += 1
                    used_by.append((unit_used, n_used, 4))
                elif kind == "B":
                    n_chunk += 1
                    used_by.append((chunk_done[TT - 1], n_chunk, 2))
                else:
                    used_by.append((y_done, 2 * (m + 1), 0))

        block = ctx.enter_context(nc.Block())

        def region(a, *shape):
            n = 1
            for s in shape:
                n *= s
            v = arena[:, a:a + n]
            if len(shape) == 2:
                v = v.rearrange("p (a b) -> p a b", a=shape[0])
            if len(shape) == 3:
                v = v.rearrange("p (a b c) -> p a b c", a=shape[0], b=shape[1])
            return v

        def tile_half(a, t):
            return a.rearrange("p (j t f) -> p j t f", j=2, t=TT)[:, :, t]

        kT = region(0, HEADS_A, SEQ)
        v_tok = region(1024, TT, 512)
        qk_rot = region(2048, 2, TT, 512)
        u_tok = region(2048, TT, 512)
        qT = region(4096, HEADS_A, SEQ)
        dT = region(5120, 4, SEQ)
        band = region(6144, 4, 3 * P)
        o_tok = region(6144, TT, 512)
        poolw = region(7680, 4, P)
        rope_tmp = region(8192, 512)
        sincos = region(4096, 2, TT, 32)
        ang = region(4096 + 128, 6, TT * 32)
        invf = region(4096 + 512, 32)
        lamv = region(5120, 4, 64)
        probs = [region(8192, 512).rearrange("p (c h k) -> p c h k", c=2, h=2),
                 region(3072, 1024).rearrange("p (c h k) -> p c h k", c=2, h=2)]
        wts = [ln_gb[:, 0, 0:256].rearrange("p (h k) -> p h k", h=2),
               ln_gb[:, 0, 512:1024].rearrange("p (h k) -> p h k", h=2)]
        wT = [ln_gb[:, 1, 0:256].rearrange("p (h b f) -> p h b f", h=2, b=1),
              ln_gb[:, 1, 512:1024].rearrange("p (h b f) -> p h b f", h=2, b=2)]
        score = [pair[0][:, :, 0:2 * P].rearrange("p c (h k) -> p c h k", h=2),
                 pair[1].rearrange("p c (h k) -> p c h k", h=2)]

        qf = region(0, TT, 2, 256)
        q_tok, logf = qf[:, :, 0], qf[:, :, 1]
        k_tok = region(1024, TT, 256)
        val = region(1536, 2, TT, 256)
        gate = region(2560, 2, TT, 256)
        KQ = 3584
        kqT = region(KQ, 2, 4, P)
        fac = region(4608, NL + 1, TT, P)
        scT = region(6656, TT, P)
        state = region(6912, P)
        klT = region(7040, P)
        o_hi_heads = region(7168, TT, 512)
        stage = region(4096, N_DECAY + NL + 1, P)
        gam = region(1536, 2, D)
        lb_tmp = region(7168, D)
        o_half = [ffn_tok[:].rearrange("p a t f -> p (a t f)").rearrange("p (t f) -> p t f", t=TT), o_hi_heads]
        LV = [pair[1], pair[3]]
        Y_MIX = [bank[4:6], bank[0:2]]

        @block.sync
        def _(sp):
            def load_gate_up(n, n_static, w, kh, c):
                load_halves(n, n_static, w, kh, 2, 0, c)

            def load_halves(n, n_static, w, kh, parts, g0, c):
                if not (type(n) is int and n < RAW):
                    sp.wait_ge(lo_ready, n - RAW + 1)
                dst = raw[:, n_static % RAW].rearrange("p (k g f) -> p k g f", k=4, g=2)
                src = w.rearrange("(k p) (g f) -> p k g f", p=P, g=parts)
                for g in range(2):
                    sp.dma_start(dst[:, :, g], src[:, 4 * kh:4 * kh + 4, g0 + g, bass.ds(c * FC, FC)]
                                 ).then_inc(raw_landed[n_static % RAW], 16)

            def load_rows(n, n_static, w, c):
                sp.wait_ge(lo_ready, n - RAW + 1)
                for k in range(2):
                    sp.dma_start(raw[:, n_static % RAW, k * D:(k + 1) * D], w[bass.ds((2 * c + k) * P, P), :]
                                 ).then_inc(raw_landed[n_static % RAW], 16)

            for name in ORDER:
                s0 = phases[name]
                if name in FFN:
                    layer, w_in, w_out = FFN[name]
                    wi, wo = w_in[layer], w_out[layer]
                    for kh in range(2):
                        load_gate_up(s0 + kh, s0 + kh, wi, kh, 0)
                    for kh in range(2):
                        load_gate_up(s0 + 2 + kh, s0 + 2 + kh, wi, kh, 1)
                    load_rows(s0 + 4, s0 + 4, wo, 0)
                    with sp.Fori(0, NPAIR) as i:
                        for par in range(2):
                            a = s0 + 5 + 3 * par
                            for kh in range(2):
                                load_gate_up(i * 6 + (a + kh), a + kh, wi, kh, i * 2 + (2 + par))
                            load_rows(i * 6 + (a + 2), a + 2, wo, i * 2 + (1 + par))
                    a = s0 + FFN_UNITS - 4
                    for kh in range(2):
                        load_gate_up(a + kh, a + kh, wi, kh, NC - 1)
                    load_rows(a + 2, a + 2, wo, NC - 2)
                    load_rows(a + 3, a + 3, wo, NC - 1)
                else:
                    w_in, w_out, order = ((ab_w_in[0], ab_w_o[0], AB_CHUNKS) if name == "AB"
                                          else (c_w_in[0], c_w_o[0], C_CHUNKS))
                    for j, c in enumerate(order):
                        for kh in range(2):
                            n = s0 + 2 * j + kh
                            if name == "C":
                                load_halves(n, n, w_in, kh, 4, 2 * c[1], c[0])
                                continue
                            sp.wait_ge(lo_ready, n - RAW + 1)
                            for k in range(0, 4, 2):
                                sp.dma_start(
                                    raw[:, n % RAW, k * 512:(k + 2) * 512].rearrange("p (k f) -> p k f", k=2),
                                    w_in.rearrange("(k p) f -> p k f", p=P)[:, 4 * kh + k:4 * kh + k + 2,
                                                                            c * 512:(c + 1) * 512]
                                ).then_inc(raw_landed[n % RAW], 16)
                    for i, m in enumerate(OUT_UNITS[name]):
                        n = s0 + 2 * len(order) + i
                        load_rows(n, n, w_out, m)
            for t in range(TT):
                for h in range(2):
                    sp.wait_ge(x_ready, 4 * len(ORDER) - 3 + 2 * t + h)
                    sp.dma_start(out[0, t * P:(t + 1) * P, h * 512:(h + 1) * 512],
                                 x_tok[:, t, h * 512:(h + 1) * 512]).then_inc(out_stored, 16)
            sp.wait_ge(out_stored, 16 * 4)

        @block.scalar
        def _(act):
            steps = [0]

            def step(ins):
                steps[0] += 1
                ins.then_inc(act_step, 1)
                act.wait_ge(act_step, steps[0])

            def split_hi(n, i=None):
                slot, use = n % RAW, n // RAW
                if n >= N_UNITS:
                    return
                if i is None:
                    act.wait_ge(raw_landed[slot], 32 * (use + 1))
                    if n >= RING:
                        used, value, _ = used_by[n - RING]
                        act.wait_ge(used, value)
                else:
                    used, value, per_iteration = used_by[n - RING]
                    act.wait_ge(raw_landed[slot], i * (32 * RING // RAW) + 32 * (use + 1))
                    act.wait_ge(used, i * per_iteration + value)
                nc.scalar.copy(w_hi[:, n % RING], raw[:, slot]).then_inc(hi_ready, 1)

            def xT_split(m, t):
                for h in range(2):
                    act.wait_ge(xT_done, 4 * m + 2 * t + h + 1)
                    nc.scalar.copy(xT_hi[:, 4 * h:4 * h + 4, t * P:(t + 1) * P],
                                   T[h].rearrange("p (k f) -> p k f", k=4)).then_inc(xT_hi_ready, 1)

            def ffn_silu(name, t, c, g):
                act.wait_ge(chunk_done[t], c + (CHUNKS_BEFORE[name] + 1))
                nc.scalar.activation(ffn_tok[:, 0, t], g[:, 0:FC], ACT.Silu).then_inc(silu_ready, 1)

            def ffn_hidT(name, c, par):
                act.wait_ge(hidT_done, c + (SILUS[name] * NH + 1))
                nc.scalar.copy(hT_hi[:, par], T[0]).then_inc(hidT_hi, 1)

            def ffn(name, m):
                s0, hid = phases[name], 2 * SILUS[name] * NC
                if m:
                    xT_split(m, 0)
                split_hi(s0 + 3)
                ffn_silu(name, 0, 0, G[0])
                xT_split(m, 1)
                act.wait_ge(hid_ready, hid + 1)
                ffn_silu(name, 0, 1, G[1])
                split_hi(s0 + 4)
                ffn_silu(name, 1, 0, G[0])
                split_hi(s0 + 5)
                ffn_hidT(name, 0, 0)
                act.wait_ge(hid_ready, hid + 3)
                ffn_silu(name, 1, 1, G[1])
                split_hi(s0 + 6)
                split_hi(s0 + 7)
                ffn_hidT(name, 1, 1)
                if name == BEFORE_AB:
                    act.wait_ge(S["ang_ready"], 1)
                    nc.scalar.activation(sincos, ang[:, 4:6].rearrange("p a (t f) -> p a t f", t=TT), ACT.Sin
                                         ).then_inc(S["sincos_ready"], 1)
                    act.wait_ge(S["lam_prod"], 1)
                    nc.scalar.activation(lam[:, 2:4], lam[:, 0:2], ACT.Exp).then_inc(S["lam_exp"], 1)
                if name == BEFORE_C:
                    act.wait_ge(S["lb_arg"], 1)
                    nc.scalar.activation(gam, gam, ACT.Exp).then_inc(S["lb_exp"], 1)
                with act.Fori(0, NPAIR) as i:
                    for par in range(2):
                        n, c = s0 + 8 + 3 * par, i * 2 + (2 + par)
                        for t in range(TT):
                            split_hi(n + t, i)
                            ffn_silu(name, t, c, G[t])
                        split_hi(n + 2, i)
                        ffn_hidT(name, c, par)
                n, c = s0 + FFN_UNITS - 1, NC - 1
                split_hi(n)
                for t in range(TT):
                    ffn_silu(name, t, c, G[t])
                    if t == 0:
                        split_hi(n + 1)
                    act.wait_ge(hidT_done, c + t + (SILUS[name] * NH + 1))
                    nc.scalar.copy(tile_half(hT_hi[:, 0], t), tile_half(T[0], t)).then_inc(hidT_hi, 1)
                    if t == 0:
                        split_hi(n + 2)
                        split_hi(n + 3)

            def mix_ab(m):
                s0 = phases["AB"]
                k = CHUNKS_BEFORE["AB"]
                xT_split(m, 0)
                split_hi(s0 + AHEAD)
                xT_split(m, 1)
                for n in range(1, 4):
                    split_hi(s0 + AHEAD + n)
                split_hi(s0 + AHEAD + 4)
                act.wait_ge(chunk_done[0], k + 3)
                nc.scalar.copy(v_tok[:, 0], G[0]).then_inc(S["v_ready"], 1)
                for i in range(4):
                    act.wait_ge(S["qkT_done"], i + 1)
                    nc.scalar.activation((qT, kT)[i // 2][:, :, (i % 2) * P:(i % 2 + 1) * P],
                                         bank[i].rearrange("p (h f) -> p h f", h=4), ACT.Copy,
                                         scale=(SM_SCALE, 1.0)[i // 2]).then_inc(S["qkT_ready"], 1)
                split_hi(s0 + AHEAD + 5)
                act.wait_ge(chunk_done[1], k + 3)
                nc.scalar.copy(v_tok[:, 1], G[1]).then_inc(S["v_ready"], 1)
                exps(0)
                exps(1)
                split_hi(s0 + AHEAD + 6)
                u_copy(0)
                wT_copy(0)
                exps(2)
                split_hi(s0 + AHEAD + 7)
                u_copy(1)
                wT_copy(1)
                for b in range(2):
                    act.wait_ge(S["dT_done"], b + 1)
                    nc.scalar.copy(dT[:, 2 * b:2 * b + 2], bank[4 + b].rearrange("p (g f) -> p g f", g=2)
                                   ).then_inc(S["dT_ready"], 1)
                exps(3)
                wT_copy(2)
                act.wait_ge(S["setup_pool"], 16 * 4)
                for g in range(4):
                    act.wait_ge(S["poolT_done"], g // 2 + 1)
                    nc.scalar.activation(xT_hi[:, 4 + g], bank[4 + g // 2][:, (g % 2) * SEQ:(g % 2 + 1) * SEQ],
                                         ACT.Copy, scale=cols[:, 2 + g:3 + g]).then_inc(S["poolT_hi"], 1)
                squares(0)
                wT_copy(3)
                split_hi(s0 + AHEAD + 8)
                squares(1)
                for t in range(TT):
                    act.wait_ge(S["oT_done"], t + 1)
                    nc.scalar.activation(xT_hi[:, 0:4, t * P:(t + 1) * P],
                                         bank[2 + t].rearrange("p (h f) -> p h f", h=4),
                                         ACT.Copy, scale=cols[:, 0:1]).then_inc(S["oT_hi"], 1)
                for j in range(9, 12):
                    split_hi(s0 + AHEAD + j)

            def exps(it):
                hp, t = it // 2, it % 2
                act.wait_ge(S["prob_bias"], it + 1)
                if it >= 2:
                    act.wait_ge(S["w_ready"], it - 1)
                for c in range(2):
                    for h in range(2):
                        ins = nc.scalar.activation(probs[t][:, c, h], score[t][:, c, h], ACT.Exp,
                                                   bias=sm_max[:, t, c, h:h + 1],
                                                   accum_out=sm_sum[:, t, c, 2 * hp + h:2 * hp + h + 1])
                ins.then_inc(S["prob_ready"], 1)

            def u_copy(t):
                act.wait_ge(chunk_done[t], CHUNKS_BEFORE["AB"] + 4)
                nc.scalar.copy(u_tok[:, t], G[t]).then_inc(S["u_ready"], 1)

            def wT_copy(it):
                t = it % 2
                act.wait_ge(S["wT_done"], it + 1)
                nc.scalar.copy(wT[t].rearrange("p h b f -> p (h b f)"), bank[2 * t][:, 0:2 * P * (t + 1)]
                               ).then_inc(S["wT_ready"], 1)

            def squares(t):
                act.wait_ge(S["o_done"], t + 1)
                for h in range(HEADS_A):
                    col = 4 * t + h
                    ins = nc.scalar.activation(arena[:, 4096 + col * P:4096 + (col + 1) * P],
                                               T[t][:, h * P:(h + 1) * P], ACT.Square,
                                               accum_out=ssq[:, 0, col:col + 1])
                ins.then_inc(S["o_ssq"], 1)

            def mix_c(m):
                s0 = phases["C"]
                k = CHUNKS_BEFORE["C"]
                xT_split(m, 0)
                for g in range(GROUPS):
                    par = g % 2
                    for slot, (j, t) in enumerate(SLOTS[g]):
                        split_hi(s0 + AHEAD + 4 * g + slot)
                        if g == 0 and slot == 0:
                            xT_split(m, 1)
                        act.wait_ge(chunk_done[t], k + 2 * g + j + 1)
                        src = G[j] if g == 0 else G[t]
                        if j == 0:
                            if g:
                                act.wait_ge(S["c_kqT_done"], 2 * g)
                                act.wait_ge(S["logf_lo"], g)
                            nc.scalar.activation(qf[:, t], src.rearrange("p (a f) -> p a f", a=2), ACT.Sigmoid
                                                 ).then_inc(S["sig_ready"], 1)
                        else:
                            if g == 0:
                                act.wait_ge(S["lb_ready"], 1)
                            if g >= 2:
                                act.wait_ge(S["c_on"], 4 * (g - 1))
                            nc.scalar.copy(val[:, par, t], src[:, 0:256]).then_inc(S["val_ready"], 1)
                            nc.scalar.activation(gate[:, par, t], src[:, 256:512], ACT.Sigmoid
                                                 ).then_inc(S["gate_sig"], 1)
                        if slot == (2 if g else 3):
                            act.wait_ge(S["f_ready"], 2 * g + 2)
                            step(nc.scalar.activation(logf, logf, ACT.Ln))
                            if g >= 2:
                                act.wait_ge(S["expo_done"], 4 * (g - 1))
                            nc.scalar.copy(hT_hi[:, par].rearrange("p (t f) -> p t f", t=TT), logf
                                           ).then_inc(S["logf_hi"], 1)
                        if g:
                            hd = 2 * (g - 1) + slot // 2
                            if slot % 2 == 0:
                                if hd:
                                    head_squares(hd - 1)
                                if hd % 2 == 0:
                                    head_kqT(hd)
                                head_exp(hd)
                            else:
                                head_state(hd)
                        if slot == 3:
                            head_kqT(2 * g + 1)
                head_squares(5)
                head_kqT(6)
                head_exp(6)
                oT_split(0)
                split_hi(s0 + AHEAD + 16)
                head_state(6)
                oT_split(1)
                head_squares(6)
                head_exp(7)
                oT_split(2)
                split_hi(s0 + AHEAD + 17)
                head_state(7)
                split_hi(s0 + AHEAD + 18)
                head_squares(7)
                oT_split(3)
                split_hi(s0 + AHEAD + 19)

            def head_kqT(hd):
                act.wait_ge(S["c_kqT_done"], (hd ^ 1) + 1)
                if hd >= 2:
                    act.wait_ge(S["lvl_done"], 2 * hd - 2)
                nc.scalar.copy(kqT[:, hd % 2].rearrange("p a f -> p (a f)"), bank[0]).then_inc(S["c_kqT_ready"], 1)

            def head_exp(hd):
                for t in range(TT):
                    act.wait_ge(S["expo_done"], 2 * hd + t + 1)
                    if hd:
                        act.wait_ge(S["co_done"], hd)
                    nc.scalar.activation(fac[:, :, t], LV[t].rearrange("p a (b f) -> p (a b) f", b=4), ACT.Exp
                                         ).then_inc(S["expo_ready"], 1)

            def head_state(hd):
                act.wait_ge(S["klT_done"], hd + 1)
                nc.scalar.copy(klT, bank[0][:, 0:P]).then_inc(S["klT_ready"], 1)
                act.wait_ge(S["st_done"], hd + 1)
                nc.scalar.copy(state, bank[0][:, 0:P]).then_inc(S["st_ready"], 1)

            def head_squares(hd):
                act.wait_ge(S["co_done"], hd + 1)
                for t in range(TT):
                    col = 2 * (hd % 2) + t
                    nc.scalar.activation(bank[1][:, (2 + t) * P:(3 + t) * P], bank[1][:, t * P:(t + 1) * P],
                                         ACT.Square, accum_out=ssq[:, 0, col:col + 1]).then_inc(S["c_ssq"], 1)

            def oT_split(p):
                act.wait_ge(S["c_oT_done"], p + 1)
                nc.scalar.activation(xT_hi[:, 2 * p:2 * p + 2].rearrange("p h f -> p (h f)"), bank[0], ACT.Copy,
                                     scale=cols[:, 1:2]).then_inc(S["c_oT_hi"], 1)

            act.dma_start(ident[:], consts[:, C_ID:C_ID + P]).then_inc(const_landed, 16)
            for t in range(TT):
                act.dma_start(x_tok[:, t], x[0, t * P:(t + 1) * P]).then_inc(x_landed, 16)
            split_hi(0)
            split_hi(1)
            xT_split(0, 0)
            split_hi(2)
            for m, name in enumerate(ORDER):
                if name == "AB":
                    mix_ab(m)
                elif name == "C":
                    mix_c(m)
                else:
                    ffn(name, m)

        @block.vector
        def _(dve):
            steps = [0]

            def step(ins):
                steps[0] += 1
                ins.then_inc(dve_step, 1)
                dve.wait_ge(dve_step, steps[0])

            def split_lo(n, i=None):
                if n >= N_UNITS:
                    return
                dve.wait_ge(hi_ready, n + 1 if i is None else i * RING + (n + 1))
                nc.vector.tensor_tensor(w_lo[:, n % RING], raw[:, n % RAW], w_hi[:, n % RING].bitcast(F32),
                                        ALU.subtract).then_inc(lo_ready, 1)

            def xT_split(m, t):
                for h in range(2):
                    dve.wait_ge(xT_hi_ready, 4 * m + 2 * t + h + 1)
                    dst = (slice(None), slice(4 * h, 4 * h + 4), slice(t * P, (t + 1) * P))
                    nc.vector.tensor_tensor(xT_lo[dst], T[h].rearrange("p (k f) -> p k f", k=4),
                                            xT_hi[dst].bitcast(F32), ALU.subtract).then_inc(xT_lo_ready, 1)

            def norm_stats(name, t):
                n, factor = NORMS[name]
                y = Y if name in FFN else Y_MIX
                dve.wait_ge(y_done, 2 * n + t + 1)
                for h in range(2):
                    xs = x_tok[:, t, h * 512:(h + 1) * 512]
                    step(nc.vector.scalar_tensor_tensor(out=xs, in0=y[t][h], scalar=factor, in1=xs,
                                                        op0=ALU.mult, op1=ALU.add))
                    step(nc.vector.bn_stats(stats[:, t, h], xs))
                nc.vector.bn_aggr(mv[:, t], stats[:, t].rearrange("p a b -> p (a b)")).then_inc(var_ready, 1)

            def norm_gain(name, t):
                n = NORMS[name][0]
                dve.wait_ge(var_ready, 2 * n + t + 1)
                dve.wait_ge(gb_landed, 32 * (n + 1))
                for h in range(2):
                    xs = x_tok[:, t, h * 512:(h + 1) * 512]
                    ins = nc.vector.scalar_tensor_tensor(out=xs, in0=xs, scalar=mv[:, t, 0:1],
                                                         in1=ln_gb[:, 0, h * 512:(h + 1) * 512],
                                                         op0=ALU.subtract, op1=ALU.mult)
                step(ins)

            def norm_scale(name, t):
                n = NORMS[name][0]
                dve.wait_ge(rstd_ready, 2 * n + t + 1)
                for h in range(2):
                    xs = x_tok[:, t, h * 512:(h + 1) * 512]
                    nc.vector.scalar_tensor_tensor(out=xs, in0=xs, scalar=rstd[:, t:t + 1],
                                                   in1=ln_gb[:, 1, h * 512:(h + 1) * 512],
                                                   op0=ALU.mult, op1=ALU.add).then_inc(x_ready, 1)

            def norm(name, t):
                norm_stats(name, t)
                norm_gain(name, t)
                norm_scale(name, t)

            def ffn_hidden(name, t, g, nth, hid):
                dve.wait_ge(silu_ready, nth + (2 * SILUS[name] * NC + 1))
                nc.vector.tensor_tensor(hid, g[:, FC:2 * FC], ffn_tok[:, 0, t], ALU.mult).then_inc(hid_ready, 1)

            def ffn_hidT(name, c, par):
                dve.wait_ge(hidT_hi, c + (SILUS[name] * NH + 1))
                nc.vector.tensor_tensor(hT_lo[:, par], T[0], hT_hi[:, par].bitcast(F32),
                                        ALU.subtract).then_inc(hidT_lo, 1)

            def ffn(name, m):
                s0 = phases[name]
                if m:
                    xT_split(m, 0)
                    norm(ORDER[m - 1], 1)
                else:
                    split_lo(s0 + 3)
                ffn_hidden(name, 0, G[0], 0, ffn_tok[:, 1, 0])
                if m:
                    split_lo(s0 + 3)
                xT_split(m, 1)
                ffn_hidden(name, 0, G[1], 1, ffn_tok[:, 0, 0])
                split_lo(s0 + 4)
                ffn_hidden(name, 1, G[0], 2, ffn_tok[:, 1, 1])
                split_lo(s0 + 5)
                ffn_hidT(name, 0, 0)
                ffn_hidden(name, 1, G[1], 3, ffn_tok[:, 0, 1])
                if name == BEFORE_C:
                    layer_c_tables()
                    lower_bound_args()
                split_lo(s0 + 6)
                split_lo(s0 + 7)
                ffn_hidT(name, 1, 1)
                if name == BEFORE_AB:
                    rope_tables()
                if name == BEFORE_C:
                    lower_bound()
                with dve.Fori(0, NPAIR) as i:
                    for par in range(2):
                        n, c = s0 + 8 + 3 * par, i * 2 + (2 + par)
                        for t in range(TT):
                            split_lo(n + t, i)
                            ffn_hidden(name, t, G[t], c * 2 + t, ffn_tok[:, 1, t])
                        split_lo(n + 2, i)
                        ffn_hidT(name, c, par)
                n, c = s0 + FFN_UNITS - 1, NC - 1
                if name == BEFORE_AB:
                    head_constants()
                split_lo(n)
                for t in range(TT):
                    if t:
                        norm_stats(name, 0)
                    ffn_hidden(name, t, G[t], c * 2 + t, ffn_tok[:, 1, t])
                    if t:
                        norm_gain(name, 0)
                    else:
                        split_lo(n + 1)
                    dve.wait_ge(hidT_hi, c + t + (SILUS[name] * NH + 1))
                    nc.vector.tensor_tensor(tile_half(hT_lo[:, 0], t), tile_half(T[0], t),
                                            tile_half(hT_hi[:, 0], t).bitcast(F32), ALU.subtract).then_inc(hidT_lo, 1)
                    if t == 0:
                        split_lo(n + 2)
                        split_lo(n + 3)
                norm_scale(name, 0)

            def rope_tables():
                dve.wait_ge(S["ab_tables_landed"], 16 * 5)
                step(nc.vector.tensor_copy(pos_f[:], pos_i[:]))
                a3 = ang[:, 0].rearrange("p (t f) -> p t f", t=TT)
                for t in range(TT):
                    step(nc.vector.tensor_scalar(a3[:, t], invf, pos_f[:, t:t + 1], None, ALU.mult))
                step(nc.vector.tensor_scalar(ang[:, 1], ang[:, 0], 0.15915494309189535, ROUND, ALU.mult, ALU.add))
                step(nc.vector.tensor_scalar(ang[:, 2], ang[:, 1], ROUND, None, ALU.subtract))
                src = ang[:, 0]
                for part in (TWO_PI_1, TWO_PI_2, TWO_PI_3):
                    step(nc.vector.scalar_tensor_tensor(out=ang[:, 3], in0=ang[:, 2], scalar=-part, in1=src,
                                                        op0=ALU.mult, op1=ALU.add))
                    src = ang[:, 3]
                step(nc.vector.tensor_scalar(ang[:, 4], ang[:, 3], 3.1415925, -3.1415925, ALU.min, ALU.max))
                step(nc.vector.tensor_scalar(ang[:, 1], ang[:, 4], -1.0, None, ALU.mult))
                step(nc.vector.tensor_tensor(ang[:, 1], ang[:, 1], ang[:, 4], ALU.max))
                nc.vector.tensor_scalar(ang[:, 5], ang[:, 1], -1.0, 1.5707963267948966, ALU.mult, ALU.add
                                        ).then_inc(S["ang_ready"], 1)
                for a in range(2):
                    ins = nc.vector.tensor_tensor_reduce(out=ang[:, 2], in0=lamv[:, 2 * a], in1=lamv[:, 2 * a + 1],
                                                         scale=1.0, scalar=0.0, op0=ALU.mult, op1=ALU.add,
                                                         accum_out=lam[:, a:a + 1])
                    if a == 0:
                        step(ins)
                    else:
                        ins.then_inc(S["lam_prod"], 1)

            def head_constants():
                dve.wait_ge(S["lam_exp"], 1)
                step(nc.vector.tensor_tensor(lam[:, 4:5], lam[:, 3:4], lam[:, 2:3], ALU.subtract))
                step(nc.vector.tensor_scalar(lam[:, 5:6], lam[:, 4:5], LAMBDA_INIT, None, ALU.subtract))
                step(nc.vector.tensor_scalar(cols[:, 0:1], cols[:, 0:1], (1.0 - LAMBDA_INIT) * P ** 0.5, None, ALU.mult))

            def rope(i, t):
                dve.wait_ge(chunk_done[t], CHUNKS_BEFORE["AB"] + i + 1)
                g = G[i].rearrange("p (h a f) -> p h a f", h=8, a=2)
                o = qk_rot[:, i, t].rearrange("p (h a f) -> p h a f", h=8, a=2)
                tmp = rope_tmp.rearrange("p (h a f) -> p h a f", h=8, a=2)
                sn = sincos[:, 0, t].unsqueeze(1).to_broadcast([P, 8, 32])
                cs = sincos[:, 1, t].unsqueeze(1).to_broadcast([P, 8, 32])
                for a in range(2):
                    nc.vector.tensor_tensor(o[:, :, a], g[:, :, a], cs, ALU.mult)
                if 2 * t + i:
                    dve.wait_ge(S["rope_done"], 2 * t + i)
                for a in range(2):
                    ins = nc.vector.tensor_tensor(tmp[:, :, a], g[:, :, 1 - a], sn, ALU.mult)
                step(ins)
                nc.vector.tensor_tensor(o[:, :, 0], o[:, :, 0], tmp[:, :, 0], ALU.subtract)
                nc.vector.tensor_tensor(o[:, :, 1], o[:, :, 1], tmp[:, :, 1], ALU.add).then_inc(S["rope_done"], 1)

            def mix_ab(m):
                s0 = phases["AB"]
                xT_split(m, 0)
                norm(ORDER[m - 1], 1)
                split_lo(s0 + AHEAD)
                dve.wait_ge(S["sincos_ready"], 1)
                rope(0, 0)
                xT_split(m, 1)
                split_lo(s0 + AHEAD + 1)
                rope(1, 0)
                split_lo(s0 + AHEAD + 2)
                rope(0, 1)
                split_lo(s0 + AHEAD + 3)
                rope(1, 1)
                split_lo(s0 + AHEAD + 4)
                split_lo(s0 + AHEAD + 5)
                maxima(0)
                maxima(1)
                weights(0)
                split_lo(s0 + AHEAD + 6)
                weights(1)
                maxima(2)
                split_lo(s0 + AHEAD + 7)
                weights(2)
                maxima(3)
                weights(3)
                for g in range(4):
                    dve.wait_ge(S["poolT_hi"], 2 * (g // 2) + 2)
                    nc.vector.scalar_tensor_tensor(
                        out=xT_lo[:, 4 + g], in0=bank[4 + g // 2][:, (g % 2) * SEQ:(g % 2 + 1) * SEQ],
                        scalar=cols[:, 2 + g:3 + g], in1=xT_hi[:, 4 + g].bitcast(F32),
                        op0=ALU.mult, op1=ALU.subtract).then_inc(S["poolT_lo"], 1)
                split_lo(s0 + AHEAD + 8)
                for t in range(TT):
                    dve.wait_ge(S["o_rms"], t + 1)
                    nc.vector.tensor_tensor(o_tok[:, t].rearrange("p (h f) -> p h f", h=4),
                                            T[t].rearrange("p (h f) -> p h f", h=4),
                                            ssq[:, 1, 4 * t:4 * t + 4].unsqueeze(2).to_broadcast([P, 4, P]),
                                            ALU.mult).then_inc(S["o_ready"], 1)
                for t in range(TT):
                    dve.wait_ge(S["oT_hi"], t + 1)
                    nc.vector.scalar_tensor_tensor(
                        out=xT_lo[:, 0:4, t * P:(t + 1) * P], in0=bank[2 + t].rearrange("p (h f) -> p h f", h=4),
                        scalar=cols[:, 0:1], in1=xT_hi[:, 0:4, t * P:(t + 1) * P].bitcast(F32),
                        op0=ALU.mult, op1=ALU.subtract).then_inc(S["oT_lo"], 1)
                split_lo(s0 + AHEAD + 9)
                split_lo(s0 + AHEAD + 10)
                norm("AB", 0)
                split_lo(s0 + AHEAD + 11)

            def maxima(it):
                t = it % 2
                dve.wait_ge(S["score_done"], it + 1)
                diag = score[t][:, :, :, t * P:(t + 1) * P]
                for c in range(2):
                    ins = nc.vector.tensor_tensor(diag[:, c], diag[:, c],
                                                  causal[:].unsqueeze(1).to_broadcast([P, 2, P]), ALU.add)
                step(ins)
                nc.vector.tensor_reduce(sm_max[:, t], score[t], AX.X, ALU.max, negate=True
                                        ).then_inc(S["prob_bias"], 1)

            def weights(it):
                hp, t = it // 2, it % 2
                hs = slice(2 * hp, 2 * hp + 2)
                dve.wait_ge(S["prob_ready"], it + 1)
                step(nc.vector.reciprocal(sm_fac[:, t, 0:2], sm_sum[:, t, 1, hs]))
                step(nc.vector.scalar_tensor_tensor(out=sm_fac[:, t, 2:4], in0=sm_fac[:, t, 0:2], scalar=lam[:, 5:6],
                                                    in1=sm_sum[:, t, 0, hs], op0=ALU.mult, op1=ALU.mult))
                if it >= 2:
                    dve.wait_ge(S["wT_done"], it - 1)
                for h in range(2):
                    ins = nc.vector.scalar_tensor_tensor(out=wts[t][:, h], in0=probs[t][:, 1, h],
                                                         scalar=sm_fac[:, t, 2 + h:3 + h], in1=probs[t][:, 0, h],
                                                         op0=ALU.mult, op1=ALU.add)
                ins.then_inc(S["w_ready"], 1)
                if hp == 1:
                    nc.vector.scalar_tensor_tensor(out=eps_sum[:, t], in0=sm_sum[:, t, 0], scalar=LN_EPS * P,
                                                   in1=sm_sum[:, t, 0], op0=ALU.mult, op1=ALU.mult
                                                   ).then_inc(S["eps_ready"], 1)

            def layer_c_tables():
                dve.wait_ge(S["c_tables_landed"], 16)
                nc.vector.tensor_copy(decay[:], stage[:, 0:N_DECAY])
                nc.vector.tensor_copy(level_mask[:], stage[:, N_DECAY:]).then_inc(S["c_tab_ready"], 1)
                dve.wait_ge(S["c_tab_ready"], 1)
                step(nc.vector.memset(scT, 0.0))

            def lower_bound_args():
                g0, g1 = gam[:, 0], gam[:, 1]
                dve.wait_ge(S["gamma_landed"], 32)
                step(nc.vector.tensor_tensor(lb_tmp, g0, g1, ALU.max))
                nc.vector.tensor_tensor(g0, g0, lb_tmp, ALU.subtract)
                nc.vector.tensor_tensor(g1, g1, lb_tmp, ALU.subtract).then_inc(S["lb_arg"], 1)

            def lower_bound():
                g0, g1 = gam[:, 0], gam[:, 1]
                dve.wait_ge(S["lb_exp"], 1)
                step(nc.vector.tensor_tensor(lb_tmp, g0, g1, ALU.add))
                step(nc.vector.reciprocal(lb_tmp, lb_tmp))
                step(nc.vector.tensor_tensor(g0, lb_tmp, g0, ALU.mult))
                step(nc.vector.tensor_tensor(g1, lb_tmp, g1, ALU.mult))

            def mix_c(m):
                s0 = phases["C"]
                xT_split(m, 0)
                norm(ORDER[m - 1], 1)
                for g in range(GROUPS):
                    par = g % 2
                    for slot, (j, t) in enumerate(SLOTS[g]):
                        split_lo(s0 + AHEAD + 4 * g + slot)
                        src = G[j] if g == 0 else G[t]
                        if g == 0 and slot == 0:
                            xT_split(m, 1)
                            nc.vector.tensor_copy(ln_gb[:], gam).then_inc(S["lb_ready"], 1)
                            dve.wait_ge(S["lb_ready"], 1)
                        if j == 0:
                            gs = slice(g * 256, (g + 1) * 256)
                            rest, lb, f = ln_gb[:, 0, gs], ln_gb[:, 1, gs], logf[:, t]
                            dve.wait_ge(S["sig_ready"], 2 * g + t + 1)
                            nc.vector.tensor_tensor(q_tok[:, t], q_tok[:, t], src[:, 0:256], ALU.mult
                                                    ).then_inc(S["q_ready"], 1)
                            step(nc.vector.tensor_tensor(f, f, rest, ALU.mult))
                            step(nc.vector.tensor_tensor(k_tok[:, t], rest, f, ALU.subtract))
                            nc.vector.scalar_tensor_tensor(out=f, in0=f, scalar=1e-18, in1=lb,
                                                           op0=ALU.max, op1=ALU.add).then_inc(S["f_ready"], 1)
                        else:
                            dve.wait_ge(S["gate_sig"], 2 * g + t + 1)
                            nc.vector.tensor_tensor(gate[:, par, t], gate[:, par, t], src[:, 256:512], ALU.mult
                                                    ).then_inc(S["gate_ready"], 1)
                        if slot == 3:
                            dve.wait_ge(S["logf_hi"], g + 1)
                            nc.vector.tensor_tensor(hT_lo[:, par].rearrange("p (t f) -> p t f", t=TT), logf,
                                                    hT_hi[:, par].rearrange("p (t f) -> p t f", t=TT).bitcast(F32),
                                                    ALU.subtract).then_inc(S["logf_lo"], 1)
                        if g:
                            hd = 2 * (g - 1) + slot // 2
                            if slot % 2 == 0:
                                if hd:
                                    head_out(hd - 1)
                                head_factors(hd)
                            else:
                                head_scores(hd)
                head_out(5)
                head_factors(6)
                oT_split(0)
                split_lo(s0 + AHEAD + 16)
                head_scores(6)
                oT_split(1)
                head_out(6)
                head_factors(7)
                oT_split(2)
                split_lo(s0 + AHEAD + 17)
                head_scores(7)
                split_lo(s0 + AHEAD + 18)
                head_out(7)
                oT_split(3)
                norm("C", 0)
                split_lo(s0 + AHEAD + 19)

            def head_factors(hd):
                dve.wait_ge(S["c_kqT_ready"], (hd ^ 1) + 1)
                dve.wait_ge(S["expo_ready"], 2 * hd + 2)
                a = kqT[:, hd % 2]
                ins = nc.vector.tensor_tensor(fac[:, 0], fac[:, 0],
                                              bass.AP(a.tensor, a.offset, [a.ap[0], (3 * P, 2), (1, P)]), ALU.mult)
                for l, half in enumerate(LEVELS):
                    v = fac[:, 1 + l].rearrange("p t f -> p (t f)").rearrange("p (n s j) -> p n s j", s=2, j=half)
                    o = bass.AP(a.tensor, a.offset, [a.ap[0], (2 * half, SEQ // (2 * half)), (2 * P + half, 2),
                                                     (1, half)])
                    ins = nc.vector.tensor_tensor(v, v, o, ALU.mult)
                ins.then_inc(S["fac_ready"], 1)

            def head_scores(hd):
                dve.wait_ge(S["lvl_done"], 2 * hd + 2)
                if hd:
                    dve.wait_ge(S["co_done"], hd)
                both = psum[:, 4:8].rearrange("p (t b) f -> p t b f", b=2)
                for l in range(NL + 1):
                    ins = nc.vector.copy_predicated(scT, level_mask[:, l].unsqueeze(1).to_broadcast([P, TT, P]),
                                                    both[:, :, l // 4, (l % 4) * P:(l % 4 + 1) * P])
                    if l < NL:
                        step(ins)
                ins.then_inc(S["sc_ready"], 1)

            def head_out(hd):
                g = hd // 2
                dve.wait_ge(S["c_rms"], hd + 1)
                dve.wait_ge(S["gate_ready"], 2 * g + 2)
                for t in range(TT):
                    col = 2 * (hd % 2) + t
                    nc.vector.scalar_tensor_tensor(
                        out=o_half[hd // 4][:, t, (hd % 4) * P:(hd % 4 + 1) * P], in0=bank[1][:, t * P:(t + 1) * P],
                        scalar=ssq[:, 1, col:col + 1], in1=gate[:, g % 2, t, (hd % 2) * P:(hd % 2 + 1) * P],
                        op0=ALU.mult, op1=ALU.mult).then_inc(S["c_on"], 1)

            def oT_split(p):
                dve.wait_ge(S["c_oT_hi"], p + 1)
                dst = xT_lo[:, 2 * p:2 * p + 2].rearrange("p h f -> p (h f)")
                src = xT_hi[:, 2 * p:2 * p + 2].rearrange("p h f -> p (h f)")
                nc.vector.scalar_tensor_tensor(out=dst, in0=bank[0], scalar=cols[:, 1:2], in1=src.bitcast(F32),
                                               op0=ALU.mult, op1=ALU.subtract).then_inc(S["c_oT_lo"], 1)

            split_lo(0)
            split_lo(1)
            xT_split(0, 0)
            split_lo(2)
            for m, name in enumerate(ORDER):
                if name == "AB":
                    mix_ab(m)
                elif name == "C":
                    mix_c(m)
                else:
                    ffn(name, m)
            norm(ORDER[-1], 1)

        @block.gpsimd
        def _(pool):
            steps = [0]

            def step(ins):
                steps[0] += 1
                ins.then_inc(pool_step, 1)
                pool.wait_ge(pool_step, steps[0])

            step(nc.gpsimd.memset(mhalf[:], -0.5))

            def load_gb(n):
                l, j = divmod(n, 3)
                for a, src in enumerate((ln_gain, ln_bias)):
                    pool.dma_start(ln_gb[:, a], src[l, j:j + 1].to_broadcast([P, D])).then_inc(gb_landed, 16)

            def norm(n):
                for t in range(TT):
                    pool.wait_ge(var_ready, 2 * n + t + 1)
                    step(nc.gpsimd.tensor_scalar(veps[:, t:t + 1], mv[:, t, 1:2], 1.0, LN_EPS / ALPHA ** 2,
                                                 ALU.mult, ALU.add))
                    nc.gpsimd.tensor_tensor(rstd[:, t:t + 1], veps[:, t:t + 1], mhalf[:, 0:1], ALU.pow
                                            ).then_inc(rstd_ready, 1)

            with nc.allow_non_contiguous_dma(reason="a few columns of parameters"):
                pool.dma_start(causal[:], consts[:, C_CAUSAL:C_CAUSAL + P]).then_inc(S["ab_tables_landed"], 16)
                pool.dma_start(pos_i[:], positions[0].rearrange("(t p) -> p t", p=P)
                               ).then_inc(S["ab_tables_landed"], 16)
                pool.dma_start(invf, consts[:, C_INVF:C_INVF + 32]).then_inc(S["ab_tables_landed"], 16)
                pool.dma_start(lamv.rearrange("p a b -> p (a b)"),
                               diff_lambda.rearrange("n a b -> n (a b)").to_broadcast([P, 256])
                               ).then_inc(S["ab_tables_landed"], 16)
                pool.dma_start(cols[:, 0:1], diff_subln.rearrange("n p -> p n")).then_inc(S["ab_tables_landed"], 16)
                pool.dma_start(cols[:, 1:2], c_norm.rearrange("n p -> p n")).then_inc(S["setup_pool"], 16)
                pool.dma_start(cols[:, 2:6], pool_scale[0].rearrange("(g p) -> p g", p=P)
                               ).then_inc(S["setup_pool"], 16)
                pool.dma_start(poolw, pool_w[0].rearrange("g p f -> p g f")).then_inc(S["setup_pool"], 16)
                pool.dma_start(band, consts[:, C_BAND:C_DECAY].rearrange("p (g f) -> p g f", g=4)
                               ).then_inc(S["setup_pool"], 16)
            load_gb(0)
            for n, name in enumerate(ORDER):
                if name == "AB":
                    for t in range(TT):
                        pool.wait_ge(S["eps_ready"], t + 1)
                        pool.wait_ge(S["o_ssq"], t + 1)
                        step(nc.gpsimd.tensor_tensor(ssq[:, 0, 4 * t:4 * t + 4], ssq[:, 0, 4 * t:4 * t + 4],
                                                     eps_sum[:, t], ALU.add))
                        nc.gpsimd.tensor_tensor(ssq[:, 1, 4 * t:4 * t + 4], ssq[:, 0, 4 * t:4 * t + 4],
                                                mhalf[:, 0:4], ALU.pow).then_inc(S["o_rms"], 1)
                    load_gb(n)
                if name == "C":
                    for hd in range(8):
                        pool.wait_ge(S["c_ssq"], 2 * hd + 2)
                        cs = slice(2 * (hd % 2), 2 * (hd % 2) + 2)
                        step(nc.gpsimd.tensor_scalar(ssq[:, 0, cs], ssq[:, 0, cs], 1.0 / P, LN_EPS,
                                                     ALU.mult, ALU.add))
                        nc.gpsimd.tensor_tensor(ssq[:, 1, cs], ssq[:, 0, cs], mhalf[:, 0:2], ALU.pow
                                                ).then_inc(S["c_rms"], 1)
                    load_gb(n)
                norm(n)
                pool.wait_ge(x_ready, 4 * (n + 1))
                if n + 1 < len(ORDER) and ORDER[n + 1] in FFN:
                    load_gb(n + 1)
                if name == "AB":
                    pool.dma_start(stage.rearrange("p a b -> p (a b)"), consts[:, C_DECAY:C_END]
                                   ).then_inc(S["c_tables_landed"], 16)
                    for l in range(2):
                        pool.dma_start(gam[:, l], hgrn_gamma[l:l + 1].to_broadcast([P, D])
                                       ).then_inc(S["gamma_landed"], 16)

        @block.tensor
        def _(pe):
            def xT(m, t):
                for h in range(2):
                    if m:
                        pe.wait_ge(x_ready, 4 * (m - 1) + 2 * t + h + 1)
                    elif h == 0:
                        pe.wait_ge(x_landed, 32)
                    if t:
                        pe.wait_ge(xT_lo_ready, 4 * m + h + 1)
                    for k in range(4):
                        ins = nc.tensor.transpose(T[h][:, k * P:(k + 1) * P],
                                                  x_tok[:, t, (4 * h + k) * P:(4 * h + k + 1) * P], ident[:])
                    ins.then_inc(xT_done, 1)

            def three_passes(dst, a_hi, a_lo, b_hi, b_lo, first, last):
                nc.tensor.matmul(dst, a_hi, b_hi, start=first, stop=False)
                nc.tensor.matmul(dst, a_hi, b_lo, start=False, stop=False)
                return nc.tensor.matmul(dst, a_lo, b_hi, start=False, stop=last)

            def project(n, i, t, g, halves=(0, 1)):
                for kh in halves:
                    pe.wait_ge(lo_ready, n + kh + 1 if i is None else i * RING + (n + kh + 1))
                    slot = (n + kh) % RING
                    for k in range(4):
                        kk, ts = 4 * kh + k, slice(t * P, (t + 1) * P)
                        ins = three_passes(g, xT_hi[:, kk, ts], xT_lo[:, kk, ts],
                                           w_hi[:, slot, k * 512:(k + 1) * 512], w_lo[:, slot, k * 512:(k + 1) * 512],
                                           kk == 0, kk == KB - 1)
                    if kh:
                        ins.then_inc(chunk_done[t], 1)
                    elif t == TT - 1:
                        ins.then_inc(unit_used, 1)

            def first_chunks(m, n):
                if m == 0:
                    xT(0, 0)
                pe.wait_ge(xT_lo_ready, 4 * m + 2)
                project(n, None, 0, G[0])
                project(n + 2, None, 0, G[1], (0,))
                xT(m, 1)
                project(n + 2, None, 0, G[1], (1,))
                pe.wait_ge(xT_lo_ready, 4 * m + 4)

            def rows(n, i, t, a_hi, a_lo, first, last, free, y=Y, ks=(0, 1)):
                pe.wait_ge(lo_ready, n + 1 if i is None else i * RING + (n + 1))
                slot = n % RING
                for k in ks:
                    for h in range(2):
                        cs = slice(k * D + h * 512, k * D + (h + 1) * 512)
                        ins = three_passes(y[t][h], a_hi(k), a_lo(k), w_hi[:, slot, cs], w_lo[:, slot, cs],
                                           first and k == 0, last and k == 1)
                if free and not last and 1 in ks:
                    ins.then_inc(unit_used, 1)
                return ins

            def down(name, n, i, c, par, t, first, last, ks=(0, 1)):
                if t == 0 or c is NC - 1:
                    pe.wait_ge(hidT_lo, c + (SILUS[name] * NH + 1) + (t if c is NC - 1 else 0))
                o = t * P
                ins = rows(n, i, t, lambda k: hT_hi[:, par, k * SEQ + o:k * SEQ + o + P],
                           lambda k: hT_lo[:, par, k * SEQ + o:k * SEQ + o + P], first, last, t == TT - 1, ks=ks)
                if last and 1 in ks:
                    ins.then_inc(y_done, 1)

            def hidden_T(name, readings, tiles=(0, 1)):
                for t, (nth, src) in zip(tiles, readings):
                    pe.wait_ge(hid_ready, nth + (2 * SILUS[name] * NC + 1))
                    for j in range(2):
                        ins = nc.tensor.transpose(T[0][:, j * SEQ + t * P:j * SEQ + (t + 1) * P],
                                                  src[:, j * P:(j + 1) * P], ident[:])
                ins.then_inc(hidT_done, 1)

            def ffn(name, m):
                s0, hid = phases[name], 2 * SILUS[name] * NC
                first_chunks(m, s0)
                pe.wait_ge(hid_ready, hid + 1)
                project(s0, None, 1, G[0])
                pe.wait_ge(hid_ready, hid + 2)
                project(s0 + 2, None, 1, G[1], (0,))
                hidden_T(name, ((0, ffn_tok[:, 1, 0]), (2, ffn_tok[:, 1, 1])))
                project(s0 + 2, None, 1, G[1], (1,))
                for t in range(TT):
                    down(name, s0 + 4, None, 0, 0, t, True, False)
                hidden_T(name, ((1, ffn_tok[:, 0, 0]), (3, ffn_tok[:, 0, 1])))
                with pe.Fori(0, NPAIR) as i:
                    for par in range(2):
                        n, c = s0 + 5 + 3 * par, i * 2 + (2 + par)
                        for t in range(TT):
                            pe.wait_ge(hid_ready, c * 2 + (hid - 1 + t))
                            project(n, i, t, G[t])
                        for t in range(TT):
                            down(name, n + 2, i, c - 1, (1 + par) % 2, t, False, False)
                        hidden_T(name, ((c * 2, ffn_tok[:, 1, 0]), (c * 2 + 1, ffn_tok[:, 1, 1])))
                a, c = s0 + FFN_UNITS - 4, NC - 1
                pe.wait_ge(hid_ready, c * 2 + (hid - 1))
                project(a, None, 0, G[0])
                down(name, a + 2, None, c - 1, 1, 0, False, False)
                hidden_T(name, ((c * 2, ffn_tok[:, 1, 0]),), (0,))
                pe.wait_ge(hid_ready, c * 2 + hid)
                project(a, None, 1, G[1], (0,))
                down(name, a + 3, None, c, 0, 0, False, True)
                project(a, None, 1, G[1], (1,))
                down(name, a + 2, None, c - 1, 1, 1, False, False, (0,))
                hidden_T(name, ((c * 2 + 1, ffn_tok[:, 1, 1]),), (1,))
                down(name, a + 2, None, c - 1, 1, 1, False, False, (1,))
                down(name, a + 3, None, c, 0, 1, False, True, (0,))
                if m + 1 < len(ORDER):
                    xT(m + 1, 0)
                down(name, a + 3, None, c, 0, 1, False, True, (1,))

            def mix_ab(m):
                s0 = phases["AB"]
                u0 = s0 + 2 * len(AB_CHUNKS)

                def scores(it):
                    hp, t = it // 2, it % 2
                    if it >= 2:
                        pe.wait_ge(S["wT_ready"], it - 1)
                    for h in range(2):
                        for c in range(2):
                            rs = slice(64 * c, 64 * c + 64)
                            ins = nc.tensor.matmul(score[t][:, c, h], qT[rs, 2 * hp + h, t * P:(t + 1) * P],
                                                   kT[rs, 2 * hp + h, 0:P * (t + 1)], start=True, stop=True)
                    ins.then_inc(S["score_done"], 1)

                def weights_T(it):
                    t = it % 2
                    pe.wait_ge(S["w_ready"], it + 1)
                    for h in range(2):
                        for kb in range(t + 1):
                            b = h * (t + 1) + kb
                            ins = nc.tensor.transpose(bank[2 * t][:, b * P:(b + 1) * P],
                                                      wts[t][:, h, kb * P:(kb + 1) * P], ident[:])
                    ins.then_inc(S["wT_done"], 1)

                def outputs(it):
                    hp, t = it // 2, it % 2
                    pe.wait_ge(S["wT_ready"], it + 1)
                    for h in range(2):
                        hs = slice((2 * hp + h) * P, (2 * hp + h + 1) * P)
                        for kb in range(t + 1):
                            ins = nc.tensor.matmul(T[t][:, hs], wT[t][:, h, kb], v_tok[:, kb, hs],
                                                   start=kb == 0, stop=kb == t)
                    if hp == 1:
                        ins.then_inc(S["o_done"], 1)

                def out_rows(t, i):
                    j = OUT_UNITS["AB"][i]
                    ts = slice(t * P, (t + 1) * P)
                    return rows(u0 + i, None, t, lambda k: xT_hi[:, 2 * j + k, ts], lambda k: xT_lo[:, 2 * j + k, ts],
                                i == 0, i == 3, t == TT - 1, Y_MIX)

                first_chunks(m, s0)
                for j in range(2):
                    pe.wait_ge(S["rope_done"], j + 1)
                    project(s0 + 2 * j, None, 1, G[j])
                pe.wait_ge(S["rope_done"], 3)
                project(s0 + 4, None, 0, G[0])
                pe.wait_ge(S["rope_done"], 4)
                for i in range(4):
                    for h in range(HEADS_A):
                        ins = nc.tensor.transpose(bank[i][:, h * P:(h + 1) * P],
                                                  qk_rot[:, i // 2, i % 2, h * P:(h + 1) * P], ident[:])
                    ins.then_inc(S["qkT_done"], 1)
                project(s0 + 4, None, 1, G[1])
                pe.wait_ge(S["qkT_ready"], 4)
                scores(0)
                scores(1)
                pe.wait_ge(S["v_ready"], 1)
                project(s0 + 6, None, 0, G[0])
                weights_T(0)
                outputs(0)
                scores(2)
                pe.wait_ge(S["v_ready"], 2)
                project(s0 + 6, None, 1, G[1])
                weights_T(1)
                pe.wait_ge(S["u_ready"], 2)
                pe.wait_ge(S["setup_pool"], 16 * 4)
                for g in range(4):
                    dst, us = bank[4 + g // 2][:, (g % 2) * SEQ:(g % 2 + 1) * SEQ], slice(g * P, (g + 1) * P)
                    nc.tensor.matmul(dst, u_tok[:, 0, us], band[:, g, 0:SEQ], start=True, stop=False)
                    ins = nc.tensor.matmul(dst[:, P:SEQ], u_tok[:, 1, us], band[:, g, SEQ:], start=False, stop=True)
                    if g % 2:
                        ins.then_inc(S["dT_done"], 1)
                outputs(1)
                scores(3)
                weights_T(2)
                for b in range(2):
                    pe.wait_ge(S["dT_ready"], b + 1)
                    for g in (2 * b, 2 * b + 1):
                        ins = nc.tensor.matmul(bank[4 + b][:, (g % 2) * SEQ:(g % 2 + 1) * SEQ], poolw[:, g], dT[:, g],
                                               start=True, stop=True)
                    ins.then_inc(S["poolT_done"], 1)
                outputs(2)
                weights_T(3)
                outputs(3)
                pe.wait_ge(S["poolT_lo"], 4)
                out_rows(0, 0)
                for t in range(TT):
                    if t:
                        out_rows(0, 1)
                    pe.wait_ge(S["o_ready"], t + 1)
                    for h in range(HEADS_A):
                        ins = nc.tensor.transpose(bank[2 + t][:, h * P:(h + 1) * P],
                                                  o_tok[:, t, h * P:(h + 1) * P], ident[:])
                    ins.then_inc(S["oT_done"], 1)
                pe.wait_ge(S["oT_lo"], 1)
                out_rows(0, 2)
                out_rows(0, 3).then_inc(y_done, 1)
                pe.wait_ge(S["oT_lo"], 2)
                for i in range(3):
                    out_rows(1, i)
                if m + 1 < len(ORDER):
                    xT(m + 1, 0)
                out_rows(1, 3).then_inc(y_done, 1)

            def mix_c(m):
                s0 = phases["C"]
                first_chunks(m, s0)
                for g in range(GROUPS):
                    for slot, (j, t) in enumerate(SLOTS[g]):
                        if g == 0:
                            if t == 0:
                                continue
                            if j == 0:
                                pe.wait_ge(S["q_ready"], 1)
                                pe.wait_ge(S["sig_ready"], 1)
                            else:
                                pe.wait_ge(S["gate_ready"], 1)
                            project(s0 + 2 * j, None, 1, G[j])
                        else:
                            if g == 1 and j == 0 and t == 0:
                                pe.wait_ge(S["q_ready"], 2)
                                pe.wait_ge(S["sig_ready"], 2)
                            elif j == 0:
                                pe.wait_ge(S["gate_ready"], 2 * (g - 1) + t + 1)
                            else:
                                pe.wait_ge(S["q_ready"], 2 * g + t + 1)
                                pe.wait_ge(S["sig_ready"], 2 * g + t + 1)
                            project(s0 + 2 * (2 * g + j), None, t, G[t])
                        if g:
                            hd = 2 * (g - 1) + slot // 2
                            if slot % 2 == 0:
                                if hd:
                                    head_outputs(hd - 1)
                                if hd % 2 == 0:
                                    head_kqT(hd)
                                head_exponents(hd)
                            else:
                                head_levels(hd)
                        if slot == 3:
                            head_kqT(2 * g + 1)
                u0 = s0 + 2 * len(C_CHUNKS)
                head_outputs(5)
                head_kqT(6)
                head_exponents(6)
                head_oT(0)
                out_rows(u0, 0, 0)
                head_levels(6)
                head_oT(1)
                head_outputs(6)
                head_exponents(7)
                out_rows(u0, 0, 1)
                head_oT(2)
                out_rows(u0, 0, 2)
                head_levels(7)
                head_outputs(7)
                head_oT(3)
                out_rows(u0, 0, 3).then_inc(y_done, 1)
                for j in range(3):
                    out_rows(u0, 1, j)
                if m + 1 < len(ORDER):
                    xT(m + 1, 0)
                out_rows(u0, 1, 3).then_inc(y_done, 1)

            def out_rows(u0, t, j):
                pe.wait_ge(S["c_oT_lo"], j + 1)
                if t == 0 and j == 0:
                    pe.wait_ge(S["gate_ready"], 2 * GROUPS)
                ts = slice(t * P, (t + 1) * P)
                return rows(u0 + j, None, t, lambda k: xT_hi[:, 2 * j + k, ts], lambda k: xT_lo[:, 2 * j + k, ts],
                            j == 0, j == 3, t == TT - 1, Y_MIX)

            def head_kqT(hd):
                g, hs = hd // 2, slice((hd % 2) * P, (hd % 2 + 1) * P)
                pe.wait_ge(S["q_ready"], 2 * g + 2)
                pe.wait_ge(S["f_ready"], 2 * g + 2)
                if hd % 2 == 0:
                    pe.wait_ge(S["c_kqT_ready"], hd + 1)
                elif g:
                    pe.wait_ge(S["st_ready"], 2 * g)
                for a, src in enumerate((k_tok, q_tok)):
                    for t in range(TT):
                        ins = nc.tensor.transpose(bank[0][:, (2 * a + t) * P:(2 * a + t + 1) * P], src[:, t, hs],
                                                  ident[:])
                ins.then_inc(S["c_kqT_done"], 1)

            def head_exponents(hd):
                g, hs = hd // 2, slice((hd % 2) * P, (hd % 2 + 1) * P)
                pe.wait_ge(S["logf_lo"], g + 1)
                if hd:
                    pe.wait_ge(S["sc_ready"], hd)
                hi, lo = (h[:, g % 2].rearrange("p (t f) -> p t f", t=TT) for h in (hT_hi, hT_lo))
                for t in range(TT):
                    for b, d0, d1 in (((0, 0, 4), (1, 4, 8)) if t == 0 else ((0, 8, 9), (0, 1, 4), (1, 4, 8))):
                        c0 = P if (d0, d1) == (1, 4) else 0
                        dst = LV[t][:, b, c0:c0 + (d1 - d0) * P]
                        rhs = decay[:, d0:d1].rearrange("p l f -> p (l f)")
                        nc.tensor.matmul(dst, hi[:, t, hs], rhs, start=True, stop=False)
                        ins = nc.tensor.matmul(dst, lo[:, t, hs], rhs, start=False, stop=True)
                    ins.then_inc(S["expo_done"], 1)

            def head_levels(hd):
                g, hs = hd // 2, slice((hd % 2) * P, (hd % 2 + 1) * P)
                pe.wait_ge(S["fac_ready"], hd + 1)
                if hd >= 6:
                    pe.wait_ge(S["c_oT_lo"], (1, 3)[hd - 6])
                elif hd % 2 == 0:
                    pe.wait_ge(S["c_kqT_ready"], hd + 2)
                else:
                    pe.wait_ge(S["st_ready"], hd)
                nc.tensor.transpose(bank[0][:, 0:P], fac[:, 0, 0], ident[:]).then_inc(S["klT_done"], 1)
                for t in range(TT):
                    for l in range(NL + 1):
                        k_side = fac[:, 1 + l, t] if l < NL else kqT[:, hd % 2, t]
                        q_side = fac[:, 1 + l, t] if l < NL else kqT[:, hd % 2, 2 + t]
                        ins = nc.tensor.matmul(LV[t][:, l // 4, (l % 4) * P:(l % 4 + 1) * P], k_side, q_side,
                                               start=True, stop=True)
                    ins.then_inc(S["lvl_done"], 1)
                    if t == 0:
                        pe.wait_ge(S["klT_ready"], hd + 1)
                        pe.wait_ge(S["val_ready"], 2 * g + 2)
                        nc.tensor.matmul(bank[0][:, 0:P], klT, val[:, g % 2, 0, hs], start=True, stop=True
                                         ).then_inc(S["st_done"], 1)

            def head_outputs(hd):
                g, hs = hd // 2, slice((hd % 2) * P, (hd % 2 + 1) * P)
                pe.wait_ge(S["st_ready"], hd + 1)
                pe.wait_ge(S["sc_ready"], hd + 1)
                if hd:
                    pe.wait_ge(S["c_on"], 2 * hd)
                nc.tensor.matmul(bank[1][:, 0:P], scT[:, 0], val[:, g % 2, 0, hs], start=True, stop=True)
                nc.tensor.matmul(bank[1][:, P:2 * P], scT[:, 1], val[:, g % 2, 1, hs], start=True, stop=False)
                nc.tensor.matmul(bank[1][:, P:2 * P], fac[:, 0, 1], state, start=False, stop=True
                                 ).then_inc(S["co_done"], 1)

            def head_oT(p):
                pe.wait_ge(S["c_on"], 4 * p + 4)
                last_read, count = ((S["c_kqT_ready"], 8), (S["st_ready"], 7), (S["c_oT_lo"], 2),
                                    (S["st_ready"], 8))[p]
                pe.wait_ge(last_read, count)
                for h in range(2):
                    hh = 2 * p + h
                    for t in range(TT):
                        ins = nc.tensor.transpose(bank[0][:, (2 * h + t) * P:(2 * h + t + 1) * P],
                                                  o_half[hh // 4][:, t, (hh % 4) * P:(hh % 4 + 1) * P], ident[:])
                ins.then_inc(S["c_oT_done"], 1)

            pe.wait_ge(const_landed, 16)
            for m, name in enumerate(ORDER):
                if name == "AB":
                    mix_ab(m)
                elif name == "C":
                    mix_c(m)
                else:
                    ffn(name, m)


def shape_constants():
    import numpy as np
    c = np.zeros((P, C_END), np.float32)
    p, f = np.arange(P)[:, None], np.arange(P)[None, :]
    c[:, C_ID:C_ID + P] = p == f
    c[:, C_CAUSAL:C_CAUSAL + P] = np.where(f <= p, 0.0, NEG)
    c[:, C_INVF:C_INVF + 32] = (10000.0 ** (-np.arange(0, 64, 2) / 64)).astype(np.float32)
    tok = np.arange(SEQ)[None, :]
    for g, w in enumerate(POOLS):
        b = np.zeros((SEQ, SEQ))
        s = np.arange(SEQ)[:, None]
        b += np.where((s <= tok) & (s > tok - w), 1.0 / np.minimum(tok + 1, w), 0.0)
        b -= s == tok
        c[:, C_BAND + g * 3 * P:C_BAND + g * 3 * P + SEQ] = b[0:P]
        c[:, C_BAND + g * 3 * P + SEQ:C_BAND + (g + 1) * 3 * P] = b[P:, P:]
    decay = [p > f]
    mask = []
    for half in LEVELS:
        mid = f // (2 * half) * (2 * half) + half
        decay.append(np.where(f >= mid, (p >= mid) & (p <= f), (p > f) & (p < mid)))
        same = p // (2 * half) == f // (2 * half)
        mask.append(same & (p % (2 * half) < half) & (f % (2 * half) >= half))
    decay.append(p <= f)
    mask.append(p == f)
    for i, a in enumerate(decay + mask):
        c[:, C_DECAY + i * P:C_DECAY + (i + 1) * P] = a
    return c


_INS = ["x", "positions", "ln_gain", "ln_bias", "ffn1_w_in", "ffn1_w_out", "ffn2_w_in", "ffn2_w_out", "ab_w_in",
        "ab_w_o", "diff_lambda", "diff_subln", "pool_w", "pool_scale", "c_w_in", "c_w_o", "c_norm", "hgrn_gamma"]


def kernel(**inputs):
    import numpy as np
    import concourse.bacc as bacc
    from concourse.bass_utils import run_bass_kernel_spmd

    nc = bacc.Bacc("TRN2", target_bir_lowering=False, num_devices=1)
    arrays, args = {}, []
    for name in _INS:
        a = np.ascontiguousarray(inputs[name])
        arrays[f"in_{name}"] = a
        args.append(nc.dram_tensor(f"in_{name}", a.shape, mybir.dt.from_np(a.dtype), kind="ExternalInput").ap())
    arrays["shape_constants"] = shape_constants()
    args.append(nc.dram_tensor("shape_constants", (P, C_END), F32, kind="ExternalInput").ap())
    args.append(nc.dram_tensor("out_x", (1, SEQ, D), F32, kind="ExternalOutput").ap())
    build(nc, *args)
    r = run_bass_kernel_spmd(nc, [arrays], core_ids=[0])
    return r.results[0]["out_x"]
```

```python
from contextlib import ExitStack

import concourse.bass as bass
from concourse import mybir

ALU = mybir.AluOpType
ACT = mybir.ActivationFunctionType
AX = mybir.AxisListType
F32 = mybir.dt.float32
F32R = mybir.dt.float32r
I32 = mybir.dt.int32
U8 = mybir.dt.uint8

P = 128
D = 1024
SEQ = 256
TT = SEQ // P
KB = D // P
D_FF = 2816
FC = 256
NC = D_FF // FC
NPAIR = (NC - 3) // 2
NH = NC + 1
HEADS_A = 4
POOLS = (2, 4, 8, 16)
UNIT = 2048
RAW = 3
RING = 6
LEVELS = (64, 32, 16, 8, 4, 2, 1)
NL = len(LEVELS)
N_DECAY = NL + 2
DEPTH = 2
ALPHA = (2 * DEPTH) ** 0.25
LN_EPS = 1e-5
LAMBDA_INIT = 0.2
SM_SCALE = 64 ** -0.5
TWO_PI_1, TWO_PI_2, TWO_PI_3 = 6.28125, 0.0019350051879882812, 3.019916050561733e-07
ROUND = 1.5 * 2.0 ** 23
NEG = -1e30

C_ID = 0
C_CAUSAL = C_ID + P
C_INVF = C_CAUSAL + P
C_BAND = C_INVF + 32
C_DECAY = C_BAND + 4 * 3 * P
C_MASK = C_DECAY + N_DECAY * P
C_END = C_MASK + NL * P

ORDER = ("F0", "AB", "F1", "F2", "C", "F3")


def build(nc, x, positions, ln_gain, ln_bias, ffn1_w_in, ffn1_w_out, ffn2_w_in, ffn2_w_out, ab_w_in, ab_w_o,
          diff_lambda, diff_subln, pool_w, pool_scale, c_w_in, c_w_o, c_norm, hgrn_gamma, consts, out):
    with ExitStack() as ctx:
        def sb(name, shape, dt=F32):
            return ctx.enter_context(nc.sbuf_tensor(name, shape, dt))

        def sem(name):
            return ctx.enter_context(nc.semaphore(name))

        raw = sb("raw", [P, RAW, UNIT])
        w_hi = sb("w_hi", [P, RING, UNIT], F32R)
        w_lo = sb("w_lo", [P, RING, UNIT], F32R)
        x_tok = sb("x_tok", [P, TT, D])
        xT_hi = sb("xT_hi", [P, KB, SEQ], F32R)
        xT_lo = sb("xT_lo", [P, KB, SEQ], F32R)
        hT_hi = sb("hT_hi", [P, 2, 512], F32R)
        hT_lo = sb("hT_lo", [P, 2, 512], F32R)
        ffn_tok = sb("ffn_tok", [P, 2, TT, FC])
        ln_gb = sb("ln_gb", [P, 2, D])
        arena = sb("arena", [P, 8704])
        decay = sb("decay", [P, N_DECAY, P], F32R)
        level_mask = sb("level_mask", [P, NL, P], U8)
        ident = sb("ident", [P, P])
        causal = sb("causal", [P, P])
        stats = sb("stats", [P, TT, 2, 6])
        mv = sb("mv", [P, TT, 2])
        veps = sb("veps", [P, TT])
        rstd = sb("rstd", [P, TT])
        mhalf = sb("mhalf", [P, 8])
        cols = sb("cols", [P, 8])
        lam = sb("lam", [P, 8])
        sm_max = sb("sm_max", [P, TT, 2, 2])
        sm_sum = sb("sm_sum", [P, TT, 2, HEADS_A])
        sm_fac = sb("sm_fac", [P, TT, 4])
        eps_sum = sb("eps_sum", [P, TT, HEADS_A])
        pos_f = sb("pos_f", [P, TT])
        ssq = sb("ssq", [P, 2, 8])
        kq_own = sb("kq_own", [P, 2, TT, 2])
        pos_i = sb("pos_i", [P, TT], I32)

        psum = ctx.enter_context(nc.psum_tensor("psum", [P, 8, 512], F32))
        bank = [psum[:, i] for i in (0, 1, 4, 5, 2, 3, 6, 7)]
        pair = [psum[:, 2 * i:2 * i + 2] for i in (0, 2, 1, 3)]
        Y = [bank[0:2], bank[2:4]]
        G = bank[4:6]
        T = bank[6:8]

        raw_landed = [sem(f"raw_landed{i}") for i in range(RAW)]
        hi_ready, lo_ready, unit_used = sem("hi_ready"), sem("lo_ready"), sem("unit_used")
        x_landed = [sem(f"x_landed{t}") for t in range(TT)]
        const_landed, gb_landed = sem("const_landed"), sem("gb_landed")
        chunk_done = [sem(f"chunk_done{t}") for t in range(TT)]
        silu_ready, hid_ready, hidT_done, hidT_hi, hidT_lo = (
            sem("silu_ready"), sem("hid_ready"), sem("hidT_done"), sem("hidT_hi_ready"), sem("hidT_lo_ready"))
        y_done, var_ready, rstd_ready, x_ready = sem("y_done"), sem("var_ready"), sem("rstd_ready"), sem("x_ready")
        xT_done, xT_hi_ready, xT_lo_ready = sem("xT_done"), sem("xT_hi_ready"), sem("xT_lo_ready")
        dve_step, act_step, pool_step = sem("dve_step"), sem("act_step"), sem("pool_step")
        out_stored = sem("out_stored")
        S = {n: sem(n) for n in (
            "ab_tables_landed", "pool_tables_landed", "angles_ready", "sincos_ready", "lambda_products", "lambda_exps",
            "rope_done", "u_ready", "v_ready", "qkT_done", "qkT_ready",
            "scores_done", "maxima_ready", "probs_ready", "weights_ready", "weightsT_done", "weightsT_ready", "o_done",
            "eps_ready", "o_squares", "o_rms", "o_ready", "oT_done", "oT_hi", "oT_lo",
            "dT_done", "dT_ready", "poolT_done", "poolT_hi", "poolT_lo",
            "c_tables_landed", "gamma_landed", "bound_args", "bound_exps", "bound_ready",
            "qf_sigmoids", "q_ready", "f_ready", "logf_hi", "logf_lo", "val_ready", "gate_sigmoid", "gate_ready",
            "kqT_done", "kqT_ready", "exponents_done", "decays_ready", "factors_ready",
            "levels_done", "head_scores_ready", "klT_done", "klT_ready", "state_done", "state_ready",
            "head_done", "head_squares", "head_rms", "head_ready", "headT_done", "headT_hi", "headT_lo")}

        FFN_UNITS = 3 * NC
        AB_CHUNKS = (0, 1, 2, 3)
        OUT_UNITS = {"AB": (2, 3, 0, 1), "C": (0, 1, 2, 3)}
        GROUPS = 4
        SLOTS = [((0, 0), (1, 0), (0, 1), (1, 1))] + [((0, 0), (0, 1), (1, 0), (1, 1))] * (GROUPS - 1)
        C_CHUNKS = tuple((g, j) for g in range(GROUPS) for j in range(2))
        phases, at = {}, 0
        for name, n in (("F0", FFN_UNITS), ("AB", 2 * len(AB_CHUNKS) + 4), ("F1", FFN_UNITS), ("F2", FFN_UNITS),
                        ("C", 2 * len(C_CHUNKS) + 4), ("F3", FFN_UNITS)):
            if name in ORDER:
                phases[name] = at
                at += n
        N_UNITS = at
        AHEAD = 3

        FFN = {"F0": (0, ffn1_w_in, ffn1_w_out), "F1": (0, ffn2_w_in, ffn2_w_out),
               "F2": (1, ffn1_w_in, ffn1_w_out), "F3": (1, ffn2_w_in, ffn2_w_out)}
        NORMS = {"F0": (0, 0.5 / ALPHA), "AB": (1, 1.0 / ALPHA), "F1": (2, 0.5 / ALPHA),
                 "F2": (3, 0.5 / ALPHA), "C": (4, 1.0 / ALPHA), "F3": (5, 0.5 / ALPHA)}
        SILUS = {"F0": 0, "F1": 1, "F2": 2, "F3": 3}

        BEFORE_C = "F2" if "C" in ORDER else None
        BEFORE_AB = "F0" if "AB" in ORDER else None
        CHUNKS_BEFORE, n = {}, 0
        for name in ORDER:
            CHUNKS_BEFORE[name] = n
            n += {"AB": len(AB_CHUNKS), "C": len(C_CHUNKS)}.get(name, NC)

        used_by = []
        n_used = n_chunk = 0
        for m, name in enumerate(ORDER):
            if name in FFN:
                kinds = "AB" + "ABO" * (NC - 1) + "Y"
            else:
                kinds = "AB" * len(AB_CHUNKS if name == "AB" else C_CHUNKS) + "OOOY"
            for kind in kinds:
                if kind in "AO":
                    n_used += 1
                    used_by.append((unit_used, n_used, 4))
                elif kind == "B":
                    n_chunk += 1
                    used_by.append((chunk_done[TT - 1], n_chunk, 2))
                else:
                    used_by.append((y_done, 2 * (m + 1), 0))

        block = ctx.enter_context(nc.Block())

        def region(a, *shape):
            n = 1
            for s in shape:
                n *= s
            v = arena[:, a:a + n]
            if len(shape) == 2:
                v = v.rearrange("p (a b) -> p a b", a=shape[0])
            if len(shape) == 3:
                v = v.rearrange("p (a b c) -> p a b c", a=shape[0], b=shape[1])
            return v

        def tile_half(a, t):
            return a.rearrange("p (j t f) -> p j t f", j=2, t=TT)[:, :, t]

        kT = region(0, HEADS_A, SEQ)
        v_tok = region(1024, TT, 512)
        qk_rot = region(2048, 2, TT, 512)
        u_tok = region(2048, TT, 512)
        qT = region(4096, HEADS_A, SEQ)
        dT = region(5120, 4, SEQ)
        band = region(6144, 4, 3 * P)
        o_tok = region(6144, TT, 512)
        poolw = region(7680, 4, P)
        rope_tmp = region(8192, 512)
        sincos = region(4096, 2, TT, 32)
        ang = region(4096 + 128, 6, TT * 32)
        invf = region(4096 + 512, 32)
        lamv = region(5120, 4, 64)
        probs = [region(8192, 512).rearrange("p (c h k) -> p c h k", c=2, h=2),
                 region(3072, 1024).rearrange("p (c h k) -> p c h k", c=2, h=2)]
        wts = [ln_gb[:, 0, 0:256].rearrange("p (h k) -> p h k", h=2),
               ln_gb[:, 0, 512:1024].rearrange("p (h k) -> p h k", h=2)]
        wT = [ln_gb[:, 1, 0:256].rearrange("p (h b f) -> p h b f", h=2, b=1),
              ln_gb[:, 1, 512:1024].rearrange("p (h b f) -> p h b f", h=2, b=2)]
        score = [pair[0][:, :, 0:2 * P].rearrange("p c (h k) -> p c h k", h=2),
                 pair[1].rearrange("p c (h k) -> p c h k", h=2)]

        qf = region(0, TT, 2, 256)
        q_tok, logf = qf[:, :, 0], qf[:, :, 1]
        k_tok = region(1024, TT, 256)
        val = region(1536, 2, TT, 256)
        gate = region(2560, 2, TT, 256)
        kqT = region(3584, 2, 4, P)
        fac = region(4608, NL + 1, TT, P)
        scT = region(6656, TT, P)
        levels_both = psum[:, 4:8].rearrange("p (t b) f -> p t b f", b=2)
        state = region(6912, P)
        kq_tmp = region(8192, 2, P)
        klT = region(7040, P)
        o_hi_heads = region(7168, TT, 512)
        stage = region(4096, N_DECAY + NL, P)
        gam = region(1536, 2, D)
        lb_tmp = region(7168, D)
        o_half = [ffn_tok[:].rearrange("p a t f -> p (a t f)").rearrange("p (t f) -> p t f", t=TT), o_hi_heads]
        LV = [pair[1], pair[3]]
        Y_MIX = {"AB": [bank[4:6], bank[0:2]], "C": [bank[4:6], bank[2:4]]}

        @block.sync
        def _(sp):
            def load_gate_up(n, n_static, w, kh, c):
                load_halves(n, n_static, w, kh, 2, 0, c)

            def load_halves(n, n_static, w, kh, parts, g0, c):
                if not (type(n) is int and n < RAW):
                    sp.wait_ge(lo_ready, n - RAW + 1)
                dst = raw[:, n_static % RAW].rearrange("p (k g f) -> p k g f", k=4, g=2)
                src = w.rearrange("(k p) (g f) -> p k g f", p=P, g=parts)
                for g in range(2):
                    sp.dma_start(dst[:, :, g], src[:, 4 * kh:4 * kh + 4, g0 + g, bass.ds(c * FC, FC)]
                                 ).then_inc(raw_landed[n_static % RAW], 16)

            def load_rows(n, n_static, w, c):
                sp.wait_ge(lo_ready, n - RAW + 1)
                for k in range(2):
                    sp.dma_start(raw[:, n_static % RAW, k * D:(k + 1) * D], w[bass.ds((2 * c + k) * P, P), :]
                                 ).then_inc(raw_landed[n_static % RAW], 16)

            for name in ORDER:
                s0 = phases[name]
                if name in FFN:
                    layer, w_in, w_out = FFN[name]
                    wi, wo = w_in[layer], w_out[layer]
                    for kh in range(2):
                        load_gate_up(s0 + kh, s0 + kh, wi, kh, 0)
                    if s0 == 0:
                        sp.dma_start(x_tok[:, 1], x[0, P:2 * P]).then_inc(x_landed[1], 16)
                    for kh in range(2):
                        load_gate_up(s0 + 2 + kh, s0 + 2 + kh, wi, kh, 1)
                    load_rows(s0 + 4, s0 + 4, wo, 0)
                    with sp.Fori(0, NPAIR) as i:
                        for par in range(2):
                            a = s0 + 5 + 3 * par
                            for kh in range(2):
                                load_gate_up(i * 6 + (a + kh), a + kh, wi, kh, i * 2 + (2 + par))
                            load_rows(i * 6 + (a + 2), a + 2, wo, i * 2 + (1 + par))
                    a = s0 + FFN_UNITS - 4
                    for kh in range(2):
                        load_gate_up(a + kh, a + kh, wi, kh, NC - 1)
                    load_rows(a + 2, a + 2, wo, NC - 2)
                    load_rows(a + 3, a + 3, wo, NC - 1)
                else:
                    w_in, w_out, order = ((ab_w_in[0], ab_w_o[0], AB_CHUNKS) if name == "AB"
                                          else (c_w_in[0], c_w_o[0], C_CHUNKS))
                    for j, c in enumerate(order):
                        for kh in range(2):
                            n = s0 + 2 * j + kh
                            if name == "C":
                                load_halves(n, n, w_in, kh, 4, 2 * c[1], c[0])
                                continue
                            sp.wait_ge(lo_ready, n - RAW + 1)
                            for k in range(0, 4, 2):
                                sp.dma_start(
                                    raw[:, n % RAW, k * 512:(k + 2) * 512].rearrange("p (k f) -> p k f", k=2),
                                    w_in.rearrange("(k p) f -> p k f", p=P)[:, 4 * kh + k:4 * kh + k + 2,
                                                                            c * 512:(c + 1) * 512]
                                ).then_inc(raw_landed[n % RAW], 16)
                    for i, m in enumerate(OUT_UNITS[name]):
                        n = s0 + 2 * len(order) + i
                        load_rows(n, n, w_out, m)
            for t in range(TT):
                for h in range(2):
                    sp.wait_ge(x_ready, 4 * len(ORDER) - 3 + 2 * t + h)
                    sp.dma_start(out[0, t * P:(t + 1) * P, h * 512:(h + 1) * 512],
                                 x_tok[:, t, h * 512:(h + 1) * 512]).then_inc(out_stored, 16)
            sp.wait_ge(out_stored, 16 * 4)

        @block.scalar
        def _(act):
            steps = [0]

            def step(ins):
                steps[0] += 1
                ins.then_inc(act_step, 1)
                act.wait_ge(act_step, steps[0])

            def split_hi(n, i=None):
                slot, use = n % RAW, n // RAW
                if n >= N_UNITS:
                    return
                if i is None:
                    act.wait_ge(raw_landed[slot], 32 * (use + 1))
                    if n >= RING:
                        used, value, _ = used_by[n - RING]
                        act.wait_ge(used, value)
                else:
                    used, value, per_iteration = used_by[n - RING]
                    act.wait_ge(raw_landed[slot], i * (32 * RING // RAW) + 32 * (use + 1))
                    act.wait_ge(used, i * per_iteration + value)
                nc.scalar.copy(w_hi[:, n % RING], raw[:, slot]).then_inc(hi_ready, 1)

            def xT_split(m, t):
                for h in range(2):
                    act.wait_ge(xT_done, 4 * m + 2 * t + h + 1)
                    nc.scalar.copy(xT_hi[:, 4 * h:4 * h + 4, t * P:(t + 1) * P],
                                   T[h].rearrange("p (k f) -> p k f", k=4)).then_inc(xT_hi_ready, 1)

            def ffn_silu(name, t, c, g):
                act.wait_ge(chunk_done[t], c + (CHUNKS_BEFORE[name] + 1))
                nc.scalar.activation(ffn_tok[:, 0, t], g[:, 0:FC], ACT.Silu).then_inc(silu_ready, 1)

            def ffn_hidT(name, c, par):
                act.wait_ge(hidT_done, c + (SILUS[name] * NH + 1))
                nc.scalar.copy(hT_hi[:, par], T[0]).then_inc(hidT_hi, 1)

            def ffn(name, m):
                s0, hid = phases[name], 2 * SILUS[name] * NC
                if m:
                    xT_split(m, 0)
                split_hi(s0 + 3)
                ffn_silu(name, 0, 0, G[0])
                xT_split(m, 1)
                act.wait_ge(hid_ready, hid + 1)
                ffn_silu(name, 0, 1, G[1])
                split_hi(s0 + 4)
                ffn_silu(name, 1, 0, G[0])
                split_hi(s0 + 5)
                ffn_hidT(name, 0, 0)
                act.wait_ge(hid_ready, hid + 3)
                ffn_silu(name, 1, 1, G[1])
                split_hi(s0 + 6)
                split_hi(s0 + 7)
                ffn_hidT(name, 1, 1)
                if name == BEFORE_AB:
                    act.wait_ge(S["angles_ready"], 1)
                    nc.scalar.activation(sincos, ang[:, 4:6].rearrange("p a (t f) -> p a t f", t=TT), ACT.Sin
                                         ).then_inc(S["sincos_ready"], 1)
                    act.wait_ge(S["lambda_products"], 1)
                    nc.scalar.activation(lam[:, 2:4], lam[:, 0:2], ACT.Exp).then_inc(S["lambda_exps"], 1)
                if name == "F1" and BEFORE_C:
                    act.wait_ge(S["bound_args"], 1)
                    nc.scalar.activation(gam, gam, ACT.Exp).then_inc(S["bound_exps"], 1)
                with act.Fori(0, NPAIR) as i:
                    for par in range(2):
                        n, c = s0 + 8 + 3 * par, i * 2 + (2 + par)
                        for t in range(TT):
                            split_hi(n + t, i)
                            ffn_silu(name, t, c, G[t])
                        split_hi(n + 2, i)
                        ffn_hidT(name, c, par)
                n, c = s0 + FFN_UNITS - 1, NC - 1
                split_hi(n)
                split_hi(n + 1)
                for t in range(TT):
                    ffn_silu(name, t, c, G[t])
                    if t == 0:
                        split_hi(n + 2)
                    act.wait_ge(hidT_done, c + t + (SILUS[name] * NH + 1))
                    nc.scalar.copy(tile_half(hT_hi[:, 0], t), tile_half(T[0], t)).then_inc(hidT_hi, 1)
                    if t == 0:
                        split_hi(n + 3)

            def mix_ab(m):
                s0 = phases["AB"]
                k = CHUNKS_BEFORE["AB"]
                xT_split(m, 0)
                split_hi(s0 + AHEAD)
                xT_split(m, 1)
                for n in range(1, 4):
                    split_hi(s0 + AHEAD + n)
                split_hi(s0 + AHEAD + 4)
                act.wait_ge(chunk_done[0], k + 3)
                nc.scalar.copy(v_tok[:, 0], G[0]).then_inc(S["v_ready"], 1)
                for i in range(4):
                    act.wait_ge(S["qkT_done"], i + 1)
                    nc.scalar.activation((qT, kT)[i // 2][:, :, (i % 2) * P:(i % 2 + 1) * P],
                                         bank[i].rearrange("p (h f) -> p h f", h=4), ACT.Copy,
                                         scale=(SM_SCALE, 1.0)[i // 2]).then_inc(S["qkT_ready"], 1)
                split_hi(s0 + AHEAD + 5)
                act.wait_ge(chunk_done[1], k + 3)
                nc.scalar.copy(v_tok[:, 1], G[1]).then_inc(S["v_ready"], 1)
                exps(0)
                exps(1)
                wT_copy(0)
                split_hi(s0 + AHEAD + 6)
                u_copy(0)
                exps(2)
                wT_copy(1)
                split_hi(s0 + AHEAD + 7)
                u_copy(1)
                for b in range(2):
                    act.wait_ge(S["dT_done"], b + 1)
                    nc.scalar.copy(dT[:, 2 * b:2 * b + 2], bank[4 + b].rearrange("p (g f) -> p g f", g=2)
                                   ).then_inc(S["dT_ready"], 1)
                exps(3)
                wT_copy(2)
                act.wait_ge(S["pool_tables_landed"], 16 * 4)
                for g in range(4):
                    act.wait_ge(S["poolT_done"], g // 2 + 1)
                    nc.scalar.activation(xT_hi[:, 4 + g], bank[4 + g // 2][:, (g % 2) * SEQ:(g % 2 + 1) * SEQ],
                                         ACT.Copy, scale=cols[:, 2 + g:3 + g]).then_inc(S["poolT_hi"], 1)
                squares(0)
                wT_copy(3)
                split_hi(s0 + AHEAD + 8)
                split_hi(s0 + AHEAD + 9)
                squares(1)
                split_hi(s0 + AHEAD + 10)
                for t in range(TT):
                    act.wait_ge(S["oT_done"], t + 1)
                    nc.scalar.activation(xT_hi[:, 0:4, t * P:(t + 1) * P],
                                         bank[2 + t].rearrange("p (h f) -> p h f", h=4),
                                         ACT.Copy, scale=cols[:, 0:1]).then_inc(S["oT_hi"], 1)
                split_hi(s0 + AHEAD + 11)

            def exps(it):
                hp, t = it // 2, it % 2
                act.wait_ge(S["maxima_ready"], it + 1)
                if it >= 2:
                    act.wait_ge(S["weights_ready"], it - 1)
                for c in range(2):
                    for h in range(2):
                        ins = nc.scalar.activation(probs[t][:, c, h], score[t][:, c, h], ACT.Exp,
                                                   bias=sm_max[:, t, c, h:h + 1],
                                                   accum_out=sm_sum[:, t, c, 2 * hp + h:2 * hp + h + 1])
                ins.then_inc(S["probs_ready"], 1)

            def u_copy(t):
                act.wait_ge(chunk_done[t], CHUNKS_BEFORE["AB"] + 4)
                nc.scalar.copy(u_tok[:, t], G[t]).then_inc(S["u_ready"], 1)

            def wT_copy(it):
                t = it % 2
                act.wait_ge(S["weightsT_done"], it + 1)
                nc.scalar.copy(wT[t].rearrange("p h b f -> p (h b f)"), bank[2 * t][:, 0:2 * P * (t + 1)]
                               ).then_inc(S["weightsT_ready"], 1)

            def squares(t):
                act.wait_ge(S["o_done"], t + 1)
                for h in range(HEADS_A):
                    col = 4 * t + h
                    ins = nc.scalar.activation(arena[:, 4096 + col * P:4096 + (col + 1) * P],
                                               T[t][:, h * P:(h + 1) * P], ACT.Square,
                                               accum_out=ssq[:, 0, col:col + 1])
                ins.then_inc(S["o_squares"], 1)

            def mix_c(m):
                s0 = phases["C"]
                k = CHUNKS_BEFORE["C"]
                xT_split(m, 0)
                for g in range(GROUPS):
                    par = g % 2
                    for slot, (j, t) in enumerate(SLOTS[g]):
                        split_hi(s0 + AHEAD + 4 * g + slot)
                        if g == 0 and slot == 0:
                            xT_split(m, 1)
                        if g == 0 and slot == 3:
                            log_decay(g)
                            head_kqT(0)
                        act.wait_ge(chunk_done[t], k + 2 * g + j + 1)
                        src = G[j] if g == 0 else G[t]
                        if j == 0:
                            if g:
                                act.wait_ge(S["kqT_done"], 2 * g)
                                act.wait_ge(S["logf_lo"], g)
                            nc.scalar.activation(qf[:, t], src.rearrange("p (a f) -> p a f", a=2), ACT.Sigmoid
                                                 ).then_inc(S["qf_sigmoids"], 1)
                        else:
                            if g == 0:
                                act.wait_ge(S["bound_ready"], 1)
                            if g >= 2:
                                act.wait_ge(S["head_ready"], 4 * (g - 1))
                            nc.scalar.copy(val[:, par, t], src[:, 0:256]).then_inc(S["val_ready"], 1)
                            nc.scalar.activation(gate[:, par, t], src[:, 256:512], ACT.Sigmoid
                                                 ).then_inc(S["gate_sigmoid"], 1)
                        hd = (4 * g + slot - 3) // 2
                        if hd < 0:
                            continue
                        if hd == 6:
                            oT_split(0)
                            head_squares(5)
                            oT_split(1)
                            head_exp(6)
                            head_kqT(7)
                        elif slot % 2:
                            head_exp(hd)
                            if hd:
                                head_squares(hd - 1)
                            if hd % 2 == 0:
                                head_kqT(hd + 1)
                        else:
                            if hd % 2:
                                head_kqT(hd + 1)
                            head_state(hd)
                            if slot == 2:
                                log_decay(g)
                oT_split(2)
                head_state(6)
                split_hi(s0 + AHEAD + 16)
                split_hi(s0 + AHEAD + 17)
                head_exp(7)
                head_squares(6)
                split_hi(s0 + AHEAD + 18)
                head_state(7)
                head_squares(7)
                oT_split(3)
                split_hi(s0 + AHEAD + 19)

            def log_decay(g):
                par = g % 2
                act.wait_ge(S["f_ready"], 2 * g + 2)
                step(nc.scalar.activation(logf, logf, ACT.Ln))
                if g >= 2:
                    act.wait_ge(S["exponents_done"], 4 * (g - 1))
                nc.scalar.copy(hT_hi[:, par].rearrange("p (t f) -> p t f", t=TT), logf).then_inc(S["logf_hi"], 1)

            def head_kqT(hd):
                act.wait_ge(S["kqT_done"], hd + 1)
                if hd >= 2:
                    act.wait_ge(S["levels_done"], 2 * hd - 2)
                nc.scalar.copy(kqT[:, hd % 2].rearrange("p a f -> p (a f)"), bank[0]).then_inc(S["kqT_ready"], 1)

            def head_exp(hd):
                act.wait_ge(S["exponents_done"], 2 * hd + 2)
                if hd:
                    act.wait_ge(S["head_done"], hd)
                for b in range(2):
                    nc.scalar.activation(fac[:, 4 * b:4 * b + 4].rearrange("p l t f -> p t l f"),
                                         levels_both[:, :, b].rearrange("p t (l f) -> p t l f", l=4), ACT.Exp
                                         ).then_inc(S["decays_ready"], 1)

            def head_state(hd):
                act.wait_ge(S["klT_done"], hd + 1)
                nc.scalar.copy(klT, bank[0][:, 0:P]).then_inc(S["klT_ready"], 1)
                act.wait_ge(S["state_done"], hd + 1)
                nc.scalar.copy(state, bank[0][:, 0:P]).then_inc(S["state_ready"], 1)

            def head_squares(hd):
                act.wait_ge(S["head_done"], hd + 1)
                for t in range(TT):
                    col = 2 * (hd % 2) + t
                    nc.scalar.activation(bank[1][:, (2 + t) * P:(3 + t) * P], bank[1][:, t * P:(t + 1) * P],
                                         ACT.Square, accum_out=ssq[:, 0, col:col + 1]).then_inc(S["head_squares"], 1)

            def oT_split(p):
                act.wait_ge(S["headT_done"], p + 1)
                nc.scalar.activation(xT_hi[:, 2 * p:2 * p + 2].rearrange("p h f -> p (h f)"), bank[0], ACT.Copy,
                                     scale=cols[:, 1:2]).then_inc(S["headT_hi"], 1)

            act.dma_start(ident[:], consts[:, C_ID:C_ID + P]).then_inc(const_landed, 16)
            act.dma_start(x_tok[:, 0], x[0, 0:P]).then_inc(x_landed[0], 16)
            split_hi(0)
            xT_split(0, 0)
            split_hi(1)
            split_hi(2)
            for m, name in enumerate(ORDER):
                if name == "AB":
                    mix_ab(m)
                elif name == "C":
                    mix_c(m)
                else:
                    ffn(name, m)

        @block.vector
        def _(dve):
            steps = [0]

            def step(ins):
                steps[0] += 1
                ins.then_inc(dve_step, 1)
                dve.wait_ge(dve_step, steps[0])

            def split_lo(n, i=None):
                if n >= N_UNITS:
                    return
                dve.wait_ge(hi_ready, n + 1 if i is None else i * RING + (n + 1))
                nc.vector.tensor_tensor(w_lo[:, n % RING], raw[:, n % RAW], w_hi[:, n % RING].bitcast(F32),
                                        ALU.subtract).then_inc(lo_ready, 1)

            def xT_split(m, t):
                for h in range(2):
                    dve.wait_ge(xT_hi_ready, 4 * m + 2 * t + h + 1)
                    dst = (slice(None), slice(4 * h, 4 * h + 4), slice(t * P, (t + 1) * P))
                    nc.vector.tensor_tensor(xT_lo[dst], T[h].rearrange("p (k f) -> p k f", k=4),
                                            xT_hi[dst].bitcast(F32), ALU.subtract).then_inc(xT_lo_ready, 1)

            def norm_stats(name, t):
                n, factor = NORMS[name]
                y = Y if name in FFN else Y_MIX[name]
                dve.wait_ge(y_done, 2 * n + t + 1)
                for h in range(2):
                    xs = x_tok[:, t, h * 512:(h + 1) * 512]
                    step(nc.vector.scalar_tensor_tensor(out=xs, in0=y[t][h], scalar=factor, in1=xs,
                                                        op0=ALU.mult, op1=ALU.add))
                    step(nc.vector.bn_stats(stats[:, t, h], xs))
                nc.vector.bn_aggr(mv[:, t], stats[:, t].rearrange("p a b -> p (a b)")).then_inc(var_ready, 1)

            def norm_gain(name, t):
                n = NORMS[name][0]
                dve.wait_ge(var_ready, 2 * n + t + 1)
                dve.wait_ge(gb_landed, 32 * (n + 1))
                for h in range(2):
                    xs = x_tok[:, t, h * 512:(h + 1) * 512]
                    ins = nc.vector.scalar_tensor_tensor(out=xs, in0=xs, scalar=mv[:, t, 0:1],
                                                         in1=ln_gb[:, 0, h * 512:(h + 1) * 512],
                                                         op0=ALU.subtract, op1=ALU.mult)
                step(ins)

            def norm_scale(name, t):
                n = NORMS[name][0]
                dve.wait_ge(rstd_ready, 2 * n + t + 1)
                for h in range(2):
                    xs = x_tok[:, t, h * 512:(h + 1) * 512]
                    nc.vector.scalar_tensor_tensor(out=xs, in0=xs, scalar=rstd[:, t:t + 1],
                                                   in1=ln_gb[:, 1, h * 512:(h + 1) * 512],
                                                   op0=ALU.mult, op1=ALU.add).then_inc(x_ready, 1)

            def norm(name, t):
                norm_stats(name, t)
                norm_gain(name, t)
                norm_scale(name, t)

            def ffn_hidden(name, t, g, nth, hid):
                dve.wait_ge(silu_ready, nth + (2 * SILUS[name] * NC + 1))
                nc.vector.tensor_tensor(hid, g[:, FC:2 * FC], ffn_tok[:, 0, t], ALU.mult).then_inc(hid_ready, 1)

            def ffn_hidT(name, c, par):
                dve.wait_ge(hidT_hi, c + (SILUS[name] * NH + 1))
                nc.vector.tensor_tensor(hT_lo[:, par], T[0], hT_hi[:, par].bitcast(F32),
                                        ALU.subtract).then_inc(hidT_lo, 1)

            def ffn(name, m):
                s0 = phases[name]
                if m:
                    xT_split(m, 0)
                else:
                    split_lo(s0 + 2)
                if m:
                    norm(ORDER[m - 1], 1)
                else:
                    split_lo(s0 + 3)
                ffn_hidden(name, 0, G[0], 0, ffn_tok[:, 1, 0])
                if m:
                    split_lo(s0 + 3)
                xT_split(m, 1)
                ffn_hidden(name, 0, G[1], 1, ffn_tok[:, 0, 0])
                split_lo(s0 + 4)
                if name == BEFORE_C:
                    lower_bound(0)
                ffn_hidden(name, 1, G[0], 2, ffn_tok[:, 1, 1])
                split_lo(s0 + 5)
                ffn_hidT(name, 0, 0)
                ffn_hidden(name, 1, G[1], 3, ffn_tok[:, 0, 1])
                if name == "F1" and BEFORE_C:
                    layer_c_tables()
                if name == BEFORE_C:
                    lower_bound(1)
                split_lo(s0 + 6)
                split_lo(s0 + 7)
                ffn_hidT(name, 1, 1)
                if name == BEFORE_AB:
                    rope_tables()
                if name == "F1" and BEFORE_C:
                    lower_bound_args()
                if name == BEFORE_C:
                    lower_bound(2)
                    lower_bound(3)
                with dve.Fori(0, NPAIR) as i:
                    for par in range(2):
                        n, c = s0 + 8 + 3 * par, i * 2 + (2 + par)
                        for t in range(TT):
                            split_lo(n + t, i)
                            ffn_hidden(name, t, G[t], c * 2 + t, ffn_tok[:, 1, t])
                        split_lo(n + 2, i)
                        ffn_hidT(name, c, par)
                n, c = s0 + FFN_UNITS - 1, NC - 1
                if name == BEFORE_AB:
                    head_constants()
                split_lo(n)
                split_lo(n + 1)
                ffn_hidden(name, 0, G[0], c * 2, ffn_tok[:, 1, 0])
                split_lo(n + 2)
                last_hidT(name, 0)
                split_lo(n + 3)
                norm_stats(name, 0)
                ffn_hidden(name, 1, G[1], c * 2 + 1, ffn_tok[:, 1, 1])
                norm_gain(name, 0)
                last_hidT(name, 1)
                norm_scale(name, 0)

            def last_hidT(name, t):
                dve.wait_ge(hidT_hi, NC + t + SILUS[name] * NH)
                nc.vector.tensor_tensor(tile_half(hT_lo[:, 0], t), tile_half(T[0], t),
                                        tile_half(hT_hi[:, 0], t).bitcast(F32), ALU.subtract).then_inc(hidT_lo, 1)

            def rope_tables():
                dve.wait_ge(S["ab_tables_landed"], 16 * 5)
                step(nc.vector.tensor_copy(pos_f[:], pos_i[:]))
                a3 = ang[:, 0].rearrange("p (t f) -> p t f", t=TT)
                for t in range(TT):
                    step(nc.vector.tensor_scalar(a3[:, t], invf, pos_f[:, t:t + 1], None, ALU.mult))
                step(nc.vector.tensor_scalar(ang[:, 1], ang[:, 0], 0.15915494309189535, ROUND, ALU.mult, ALU.add))
                step(nc.vector.tensor_scalar(ang[:, 2], ang[:, 1], ROUND, None, ALU.subtract))
                src = ang[:, 0]
                for part in (TWO_PI_1, TWO_PI_2, TWO_PI_3):
                    step(nc.vector.scalar_tensor_tensor(out=ang[:, 3], in0=ang[:, 2], scalar=-part, in1=src,
                                                        op0=ALU.mult, op1=ALU.add))
                    src = ang[:, 3]
                step(nc.vector.tensor_scalar(ang[:, 4], ang[:, 3], 3.1415925, -3.1415925, ALU.min, ALU.max))
                step(nc.vector.tensor_scalar(ang[:, 1], ang[:, 4], -1.0, None, ALU.mult))
                step(nc.vector.tensor_tensor(ang[:, 1], ang[:, 1], ang[:, 4], ALU.max))
                nc.vector.tensor_scalar(ang[:, 5], ang[:, 1], -1.0, 1.5707963267948966, ALU.mult, ALU.add
                                        ).then_inc(S["angles_ready"], 1)
                for a in range(2):
                    ins = nc.vector.tensor_tensor_reduce(out=ang[:, 2], in0=lamv[:, 2 * a], in1=lamv[:, 2 * a + 1],
                                                         scale=1.0, scalar=0.0, op0=ALU.mult, op1=ALU.add,
                                                         accum_out=lam[:, a:a + 1])
                    if a == 0:
                        step(ins)
                    else:
                        ins.then_inc(S["lambda_products"], 1)

            def head_constants():
                dve.wait_ge(S["lambda_exps"], 1)
                step(nc.vector.tensor_tensor(lam[:, 4:5], lam[:, 3:4], lam[:, 2:3], ALU.subtract))
                step(nc.vector.tensor_scalar(lam[:, 5:6], lam[:, 4:5], LAMBDA_INIT, None, ALU.subtract))
                factor = (1.0 - LAMBDA_INIT) * P ** 0.5
                step(nc.vector.tensor_scalar(cols[:, 0:1], cols[:, 0:1], factor, None, ALU.mult))

            def rope(i, t):
                dve.wait_ge(chunk_done[t], CHUNKS_BEFORE["AB"] + i + 1)
                g = G[i].rearrange("p (h a f) -> p h a f", h=8, a=2)
                o = qk_rot[:, i, t].rearrange("p (h a f) -> p h a f", h=8, a=2)
                tmp = rope_tmp.rearrange("p (h a f) -> p h a f", h=8, a=2)
                sn = sincos[:, 0, t].unsqueeze(1).to_broadcast([P, 8, 32])
                cs = sincos[:, 1, t].unsqueeze(1).to_broadcast([P, 8, 32])
                for a in range(2):
                    nc.vector.tensor_tensor(o[:, :, a], g[:, :, a], cs, ALU.mult)
                if 2 * t + i:
                    dve.wait_ge(S["rope_done"], 2 * t + i)
                for a in range(2):
                    ins = nc.vector.tensor_tensor(tmp[:, :, a], g[:, :, 1 - a], sn, ALU.mult)
                step(ins)
                nc.vector.tensor_tensor(o[:, :, 0], o[:, :, 0], tmp[:, :, 0], ALU.subtract)
                nc.vector.tensor_tensor(o[:, :, 1], o[:, :, 1], tmp[:, :, 1], ALU.add).then_inc(S["rope_done"], 1)

            def mix_ab(m):
                s0 = phases["AB"]
                xT_split(m, 0)
                norm(ORDER[m - 1], 1)
                split_lo(s0 + AHEAD)
                dve.wait_ge(S["sincos_ready"], 1)
                rope(0, 0)
                xT_split(m, 1)
                split_lo(s0 + AHEAD + 1)
                rope(1, 0)
                split_lo(s0 + AHEAD + 2)
                rope(0, 1)
                split_lo(s0 + AHEAD + 3)
                rope(1, 1)
                split_lo(s0 + AHEAD + 4)
                split_lo(s0 + AHEAD + 5)
                maxima(0)
                maxima(1)
                weights(0)
                weights(1)
                split_lo(s0 + AHEAD + 6)
                maxima(2)
                weights(2)
                split_lo(s0 + AHEAD + 7)
                maxima(3)
                weights(3)
                for g in range(4):
                    dve.wait_ge(S["poolT_hi"], 2 * (g // 2) + 2)
                    nc.vector.scalar_tensor_tensor(
                        out=xT_lo[:, 4 + g], in0=bank[4 + g // 2][:, (g % 2) * SEQ:(g % 2 + 1) * SEQ],
                        scalar=cols[:, 2 + g:3 + g], in1=xT_hi[:, 4 + g].bitcast(F32),
                        op0=ALU.mult, op1=ALU.subtract).then_inc(S["poolT_lo"], 1)
                split_lo(s0 + AHEAD + 8)
                split_lo(s0 + AHEAD + 9)
                for t in range(TT):
                    dve.wait_ge(S["o_rms"], t + 1)
                    nc.vector.tensor_tensor(o_tok[:, t].rearrange("p (h f) -> p h f", h=4),
                                            T[t].rearrange("p (h f) -> p h f", h=4),
                                            ssq[:, 1, 4 * t:4 * t + 4].unsqueeze(2).to_broadcast([P, 4, P]),
                                            ALU.mult).then_inc(S["o_ready"], 1)
                split_lo(s0 + AHEAD + 10)
                for t in range(TT):
                    dve.wait_ge(S["oT_hi"], t + 1)
                    nc.vector.scalar_tensor_tensor(
                        out=xT_lo[:, 0:4, t * P:(t + 1) * P], in0=bank[2 + t].rearrange("p (h f) -> p h f", h=4),
                        scalar=cols[:, 0:1], in1=xT_hi[:, 0:4, t * P:(t + 1) * P].bitcast(F32),
                        op0=ALU.mult, op1=ALU.subtract).then_inc(S["oT_lo"], 1)
                split_lo(s0 + AHEAD + 11)
                norm("AB", 0)

            def maxima(it):
                t = it % 2
                dve.wait_ge(S["scores_done"], it + 1)
                diag = score[t][:, :, :, t * P:(t + 1) * P]
                for c in range(2):
                    ins = nc.vector.tensor_tensor(diag[:, c], diag[:, c],
                                                  causal[:].unsqueeze(1).to_broadcast([P, 2, P]), ALU.add)
                step(ins)
                nc.vector.tensor_reduce(sm_max[:, t], score[t], AX.X, ALU.max, negate=True
                                        ).then_inc(S["maxima_ready"], 1)

            def weights(it):
                hp, t = it // 2, it % 2
                hs = slice(2 * hp, 2 * hp + 2)
                dve.wait_ge(S["probs_ready"], it + 1)
                step(nc.vector.reciprocal(sm_fac[:, t, 0:2], sm_sum[:, t, 1, hs]))
                step(nc.vector.scalar_tensor_tensor(out=sm_fac[:, t, 2:4], in0=sm_fac[:, t, 0:2], scalar=lam[:, 5:6],
                                                    in1=sm_sum[:, t, 0, hs], op0=ALU.mult, op1=ALU.mult))
                if it >= 2:
                    dve.wait_ge(S["weightsT_done"], it - 1)
                for h in range(2):
                    ins = nc.vector.scalar_tensor_tensor(out=wts[t][:, h], in0=probs[t][:, 1, h],
                                                         scalar=sm_fac[:, t, 2 + h:3 + h], in1=probs[t][:, 0, h],
                                                         op0=ALU.mult, op1=ALU.add)
                ins.then_inc(S["weights_ready"], 1)
                if hp == 1:
                    nc.vector.scalar_tensor_tensor(out=eps_sum[:, t], in0=sm_sum[:, t, 0], scalar=LN_EPS * P,
                                                   in1=sm_sum[:, t, 0], op0=ALU.mult, op1=ALU.mult
                                                   ).then_inc(S["eps_ready"], 1)

            def layer_c_tables():
                dve.wait_ge(S["c_tables_landed"], 16)
                nc.vector.tensor_copy(decay[:], stage[:, 0:N_DECAY])
                step(nc.vector.tensor_copy(level_mask[:], stage[:, N_DECAY:]))

            def lower_bound_args():
                g0, g1 = gam[:, 0], gam[:, 1]
                dve.wait_ge(S["gamma_landed"], 32)
                step(nc.vector.tensor_tensor(lb_tmp, g0, g1, ALU.max))
                nc.vector.tensor_tensor(g0, g0, lb_tmp, ALU.subtract)
                nc.vector.tensor_tensor(g1, g1, lb_tmp, ALU.subtract).then_inc(S["bound_args"], 1)

            def lower_bound(part):
                cs = slice(part * 256, (part + 1) * 256)
                g0, g1, total = gam[:, 0, cs], gam[:, 1, cs], lb_tmp[:, cs]
                dve.wait_ge(S["bound_exps"], 1)
                step(nc.vector.tensor_tensor(total, g0, g1, ALU.add))
                step(nc.vector.reciprocal(total, total))
                nc.vector.tensor_tensor(g0, total, g0, ALU.mult)
                step(nc.vector.tensor_tensor(g1, total, g1, ALU.mult))

            def mix_c(m):
                s0 = phases["C"]
                xT_split(m, 0)
                norm(ORDER[m - 1], 1)
                for g in range(GROUPS):
                    par = g % 2
                    for slot, (j, t) in enumerate(SLOTS[g]):
                        if slot == 3 and g:
                            logf_split(g)
                        split_lo(s0 + AHEAD + 4 * g + slot)
                        src = G[j] if g == 0 else G[t]
                        if g == 0 and slot == 0:
                            dve.wait_ge(x_ready, 4 * m)
                            nc.vector.tensor_copy(ln_gb[:], gam).then_inc(S["bound_ready"], 1)
                            xT_split(m, 1)
                            dve.wait_ge(S["bound_ready"], 1)
                        if slot == 3 and g == 0:
                            logf_split(g)
                        if j == 0:
                            gs = slice(g * 256, (g + 1) * 256)
                            rest, lb, f = ln_gb[:, 0, gs], ln_gb[:, 1, gs], logf[:, t]
                            dve.wait_ge(S["qf_sigmoids"], 2 * g + t + 1)
                            nc.vector.tensor_tensor(q_tok[:, t], q_tok[:, t], src[:, 0:256], ALU.mult
                                                    ).then_inc(S["q_ready"], 1)
                            step(nc.vector.tensor_tensor(f, f, rest, ALU.mult))
                            step(nc.vector.tensor_tensor(k_tok[:, t], rest, f, ALU.subtract))
                            nc.vector.scalar_tensor_tensor(out=f, in0=f, scalar=1e-18, in1=lb,
                                                           op0=ALU.max, op1=ALU.add).then_inc(S["f_ready"], 1)
                            for h in range(2):
                                hs = slice(h * P, (h + 1) * P)
                                ins = nc.vector.tensor_tensor_reduce(
                                    out=kq_tmp[:, h], in0=k_tok[:, t, hs], in1=q_tok[:, t, hs], scale=1.0, scalar=0.0,
                                    op0=ALU.mult, op1=ALU.add, accum_out=kq_own[:, par, t, h:h + 1])
                            step(ins)
                        else:
                            dve.wait_ge(S["gate_sigmoid"], 2 * g + t + 1)
                            nc.vector.tensor_tensor(gate[:, par, t], gate[:, par, t], src[:, 256:512], ALU.mult
                                                    ).then_inc(S["gate_ready"], 1)
                        hd = (4 * g + slot - 3) // 2
                        if hd < 0:
                            continue
                        if hd == 6:
                            oT_split(0)
                            head_out(5)
                            oT_split(1)
                            head_factors(6)
                        elif slot % 2:
                            head_factors(hd)
                            if hd:
                                head_out(hd - 1)
                        else:
                            head_scores(hd)
                oT_split(2)
                head_scores(6)
                split_lo(s0 + AHEAD + 16)
                split_lo(s0 + AHEAD + 17)
                head_factors(7)
                head_out(6)
                head_scores(7)
                split_lo(s0 + AHEAD + 18)
                head_out(7)
                oT_split(3)
                split_lo(s0 + AHEAD + 19)
                norm("C", 0)

            def logf_split(g):
                hi, lo = (a[:, g % 2].rearrange("p (t f) -> p t f", t=TT) for a in (hT_hi, hT_lo))
                dve.wait_ge(S["logf_hi"], g + 1)
                nc.vector.tensor_tensor(lo, logf, hi.bitcast(F32), ALU.subtract).then_inc(S["logf_lo"], 1)

            def head_factors(hd):
                dve.wait_ge(S["kqT_ready"], hd + 1)
                dve.wait_ge(S["decays_ready"], 2 * hd + 1)
                a = kqT[:, hd % 2]
                nc.vector.tensor_tensor(fac[:, 0], fac[:, 0],
                                        bass.AP(a.tensor, a.offset, [a.ap[0], (3 * P, 2), (1, P)]), ALU.mult)
                for l, half in enumerate(LEVELS):
                    if l == 3:
                        dve.wait_ge(S["decays_ready"], 2 * hd + 2)
                    v = fac[:, 1 + l].rearrange("p t f -> p (t f)").rearrange("p (n s j) -> p n s j", s=2, j=half)
                    o = bass.AP(a.tensor, a.offset, [a.ap[0], (2 * half, SEQ // (2 * half)), (2 * P + half, 2),
                                                     (1, half)])
                    ins = nc.vector.tensor_tensor(v, v, o, ALU.mult)
                    if l in (2, NL - 1):
                        ins.then_inc(S["factors_ready"], 1)

            def head_scores(hd):
                if hd:
                    dve.wait_ge(S["head_done"], hd)
                for t in range(TT):
                    own = kq_own[:, (hd // 2) % 2, t, hd % 2:hd % 2 + 1]
                    ins = nc.vector.tensor_scalar(scT[:, t], ident[:], own, None, ALU.mult)
                step(ins)
                lead = 4
                order = [(l, 0) for l in range(lead)]
                for l in range(NL):
                    order += [(l + lead, 0)] * (l + lead < NL) + [(l, 1)]
                written = {}
                for l, t in order:
                    if l:
                        dve.wait_ge(dve_step, written[t])
                    else:
                        dve.wait_ge(S["levels_done"], 2 * hd + t + 1)
                    ins = nc.vector.copy_predicated(scT[:, t], level_mask[:, l],
                                                    levels_both[:, t, l // 4, (l % 4) * P:(l % 4 + 1) * P])
                    if l < NL - 1:
                        steps[0] += 1
                        written[t] = steps[0]
                        ins.then_inc(dve_step, 1)
                    else:
                        ins.then_inc(S["head_scores_ready"], 1)

            def head_out(hd):
                g = hd // 2
                dve.wait_ge(S["head_rms"], hd + 1)
                dve.wait_ge(S["gate_ready"], 2 * g + 2)
                for t in range(TT):
                    col = 2 * (hd % 2) + t
                    nc.vector.scalar_tensor_tensor(
                        out=o_half[hd // 4][:, t, (hd % 4) * P:(hd % 4 + 1) * P], in0=bank[1][:, t * P:(t + 1) * P],
                        scalar=ssq[:, 1, col:col + 1], in1=gate[:, g % 2, t, (hd % 2) * P:(hd % 2 + 1) * P],
                        op0=ALU.mult, op1=ALU.mult).then_inc(S["head_ready"], 1)

            def oT_split(p):
                dve.wait_ge(S["headT_hi"], p + 1)
                dst = xT_lo[:, 2 * p:2 * p + 2].rearrange("p h f -> p (h f)")
                src = xT_hi[:, 2 * p:2 * p + 2].rearrange("p h f -> p (h f)")
                nc.vector.scalar_tensor_tensor(out=dst, in0=bank[0], scalar=cols[:, 1:2], in1=src.bitcast(F32),
                                               op0=ALU.mult, op1=ALU.subtract).then_inc(S["headT_lo"], 1)

            split_lo(0)
            xT_split(0, 0)
            split_lo(1)
            for m, name in enumerate(ORDER):
                if name == "AB":
                    mix_ab(m)
                elif name == "C":
                    mix_c(m)
                else:
                    ffn(name, m)
            norm(ORDER[-1], 1)

        @block.gpsimd
        def _(pool):
            steps = [0]

            def step(ins):
                steps[0] += 1
                ins.then_inc(pool_step, 1)
                pool.wait_ge(pool_step, steps[0])

            step(nc.gpsimd.memset(mhalf[:], -0.5))

            def load_gb(n):
                l, j = divmod(n, 3)
                for a, src in enumerate((ln_gain, ln_bias)):
                    pool.dma_start(ln_gb[:, a], src[l, j:j + 1].to_broadcast([P, D])).then_inc(gb_landed, 16)

            def norm(n):
                for t in range(TT):
                    pool.wait_ge(var_ready, 2 * n + t + 1)
                    step(nc.gpsimd.tensor_scalar(veps[:, t:t + 1], mv[:, t, 1:2], 1.0, LN_EPS / ALPHA ** 2,
                                                 ALU.mult, ALU.add))
                    nc.gpsimd.tensor_tensor(rstd[:, t:t + 1], veps[:, t:t + 1], mhalf[:, 0:1], ALU.pow
                                            ).then_inc(rstd_ready, 1)

            pool.wait_ge(x_landed[TT - 1], 16)
            with nc.allow_non_contiguous_dma(reason="a few columns of parameters"):
                pool.dma_start(causal[:], consts[:, C_CAUSAL:C_CAUSAL + P]).then_inc(S["ab_tables_landed"], 16)
                pool.dma_start(pos_i[:], positions[0].rearrange("(t p) -> p t", p=P)
                               ).then_inc(S["ab_tables_landed"], 16)
                pool.dma_start(invf, consts[:, C_INVF:C_INVF + 32]).then_inc(S["ab_tables_landed"], 16)
                pool.dma_start(lamv.rearrange("p a b -> p (a b)"),
                               diff_lambda.rearrange("n a b -> n (a b)").to_broadcast([P, 256])
                               ).then_inc(S["ab_tables_landed"], 16)
                pool.dma_start(cols[:, 0:1], diff_subln.rearrange("n p -> p n")).then_inc(S["ab_tables_landed"], 16)
                pool.dma_start(cols[:, 1:2], c_norm.rearrange("n p -> p n")).then_inc(S["pool_tables_landed"], 16)
                pool.dma_start(cols[:, 2:6], pool_scale[0].rearrange("(g p) -> p g", p=P)
                               ).then_inc(S["pool_tables_landed"], 16)
                pool.dma_start(poolw, pool_w[0].rearrange("g p f -> p g f")).then_inc(S["pool_tables_landed"], 16)
                pool.dma_start(band, consts[:, C_BAND:C_DECAY].rearrange("p (g f) -> p g f", g=4)
                               ).then_inc(S["pool_tables_landed"], 16)
            load_gb(0)
            for n, name in enumerate(ORDER):
                if name == "AB":
                    for t in range(TT):
                        pool.wait_ge(S["eps_ready"], t + 1)
                        pool.wait_ge(S["o_squares"], t + 1)
                        step(nc.gpsimd.tensor_tensor(ssq[:, 0, 4 * t:4 * t + 4], ssq[:, 0, 4 * t:4 * t + 4],
                                                     eps_sum[:, t], ALU.add))
                        nc.gpsimd.tensor_tensor(ssq[:, 1, 4 * t:4 * t + 4], ssq[:, 0, 4 * t:4 * t + 4],
                                                mhalf[:, 0:4], ALU.pow).then_inc(S["o_rms"], 1)
                    load_gb(n)
                if name == "C":
                    for hd in range(8):
                        pool.wait_ge(S["head_squares"], 2 * hd + 2)
                        cs = slice(2 * (hd % 2), 2 * (hd % 2) + 2)
                        step(nc.gpsimd.tensor_scalar(ssq[:, 0, cs], ssq[:, 0, cs], 1.0 / P, LN_EPS,
                                                     ALU.mult, ALU.add))
                        nc.gpsimd.tensor_tensor(ssq[:, 1, cs], ssq[:, 0, cs], mhalf[:, 0:2], ALU.pow
                                                ).then_inc(S["head_rms"], 1)
                    load_gb(n)
                norm(n)
                pool.wait_ge(x_ready, 4 * (n + 1))
                if n + 1 < len(ORDER) and ORDER[n + 1] in FFN:
                    load_gb(n + 1)
                if name == "AB":
                    pool.dma_start(stage.rearrange("p a b -> p (a b)"), consts[:, C_DECAY:C_END]
                                   ).then_inc(S["c_tables_landed"], 16)
                    for l in range(2):
                        pool.dma_start(gam[:, l], hgrn_gamma[l:l + 1].to_broadcast([P, D])
                                       ).then_inc(S["gamma_landed"], 16)

        @block.tensor
        def _(pe):
            def xT(m, t):
                for h in range(2):
                    if m:
                        pe.wait_ge(x_ready, 4 * (m - 1) + 2 * t + h + 1)
                    elif h == 0:
                        pe.wait_ge(x_landed[t], 16)
                    if t:
                        pe.wait_ge(xT_lo_ready, 4 * m + h + 1)
                    for k in range(4):
                        ins = nc.tensor.transpose(T[h][:, k * P:(k + 1) * P],
                                                  x_tok[:, t, (4 * h + k) * P:(4 * h + k + 1) * P], ident[:])
                    ins.then_inc(xT_done, 1)

            def three_passes(dst, a_hi, a_lo, b_hi, b_lo, first, last):
                nc.tensor.matmul(dst, a_hi, b_hi, start=first, stop=False)
                nc.tensor.matmul(dst, a_hi, b_lo, start=False, stop=False)
                return nc.tensor.matmul(dst, a_lo, b_hi, start=False, stop=last)

            FIRST, SECOND = range(4), range(4, KB)

            def project(n, i, t, g, blocks=range(KB)):
                for kh in range(2):
                    kks = [kk for kk in blocks if kk // 4 == kh]
                    if not kks:
                        continue
                    pe.wait_ge(lo_ready, n + kh + 1 if i is None else i * RING + (n + kh + 1))
                    slot = (n + kh) % RING
                    for kk in kks:
                        k, ts = kk % 4, slice(t * P, (t + 1) * P)
                        ins = three_passes(g, xT_hi[:, kk, ts], xT_lo[:, kk, ts],
                                           w_hi[:, slot, k * 512:(k + 1) * 512], w_lo[:, slot, k * 512:(k + 1) * 512],
                                           kk == 0, kk == KB - 1)
                    if kk == KB - 1:
                        ins.then_inc(chunk_done[t], 1)
                    elif t == TT - 1 and kk == 3:
                        ins.then_inc(unit_used, 1)

            def first_chunks(m, n):
                if m == 0:
                    xT(0, 0)
                pe.wait_ge(xT_lo_ready, 4 * m + 2)
                project(n, None, 0, G[0])
                project(n + 2, None, 0, G[1], FIRST)
                xT(m, 1)
                project(n + 2, None, 0, G[1], SECOND)
                pe.wait_ge(xT_lo_ready, 4 * m + 4)

            def rows(n, i, t, a_hi, a_lo, first, last, free, y=Y, ks=(0, 1)):
                pe.wait_ge(lo_ready, n + 1 if i is None else i * RING + (n + 1))
                slot = n % RING
                for k in ks:
                    for h in range(2):
                        cs = slice(k * D + h * 512, k * D + (h + 1) * 512)
                        ins = three_passes(y[t][h], a_hi(k), a_lo(k), w_hi[:, slot, cs], w_lo[:, slot, cs],
                                           first and k == 0, last and k == 1)
                if free and not last and 1 in ks:
                    ins.then_inc(unit_used, 1)
                return ins

            def down(name, n, i, c, par, t, first, last, ks=(0, 1)):
                if t == 0 or last_chunk(c):
                    pe.wait_ge(hidT_lo, c + (SILUS[name] * NH + 1) + (t if last_chunk(c) else 0))
                o = t * P
                ins = rows(n, i, t, lambda k: hT_hi[:, par, k * SEQ + o:k * SEQ + o + P],
                           lambda k: hT_lo[:, par, k * SEQ + o:k * SEQ + o + P], first, last, t == TT - 1, ks=ks)
                if last and 1 in ks:
                    ins.then_inc(y_done, 1)

            def last_chunk(c):
                return type(c) is int and c == NC - 1

            def hidden_T(name, readings, tiles=(0, 1)):
                for t, (nth, src) in zip(tiles, readings):
                    pe.wait_ge(hid_ready, nth + (2 * SILUS[name] * NC + 1))
                    for j in range(2):
                        ins = nc.tensor.transpose(T[0][:, j * SEQ + t * P:j * SEQ + (t + 1) * P],
                                                  src[:, j * P:(j + 1) * P], ident[:])
                ins.then_inc(hidT_done, 1)

            def ffn(name, m):
                s0, hid = phases[name], 2 * SILUS[name] * NC
                first_chunks(m, s0)
                pe.wait_ge(hid_ready, hid + 1)
                project(s0, None, 1, G[0])
                pe.wait_ge(hid_ready, hid + 2)
                project(s0 + 2, None, 1, G[1], FIRST)
                hidden_T(name, ((0, ffn_tok[:, 1, 0]), (2, ffn_tok[:, 1, 1])))
                project(s0 + 2, None, 1, G[1], SECOND)
                for t in range(TT):
                    down(name, s0 + 4, None, 0, 0, t, True, False)
                hidden_T(name, ((1, ffn_tok[:, 0, 0]), (3, ffn_tok[:, 0, 1])))
                with pe.Fori(0, NPAIR) as i:
                    for par in range(2):
                        n, c = s0 + 5 + 3 * par, i * 2 + (2 + par)
                        for t in range(TT):
                            pe.wait_ge(hid_ready, c * 2 + (hid - 1 + t))
                            project(n, i, t, G[t])
                        for t in range(TT):
                            down(name, n + 2, i, c - 1, (1 + par) % 2, t, False, False)
                        hidden_T(name, ((c * 2, ffn_tok[:, 1, 0]), (c * 2 + 1, ffn_tok[:, 1, 1])))
                a, c = s0 + FFN_UNITS - 4, NC - 1
                pe.wait_ge(hid_ready, c * 2 + (hid - 1))
                project(a, None, 0, G[0])
                pe.wait_ge(hid_ready, c * 2 + hid)
                project(a, None, 1, G[1], FIRST)
                down(name, a + 2, None, c - 1, 1, 0, False, False, (0,))
                hidden_T(name, ((c * 2, ffn_tok[:, 1, 0]),), (0,))
                down(name, a + 2, None, c - 1, 1, 0, False, False, (1,))
                down(name, a + 3, None, c, 0, 0, False, True)
                project(a, None, 1, G[1], SECOND)
                down(name, a + 2, None, c - 1, 1, 1, False, False, (0,))
                hidden_T(name, ((c * 2 + 1, ffn_tok[:, 1, 1]),), (1,))
                down(name, a + 2, None, c - 1, 1, 1, False, False, (1,))
                down(name, a + 3, None, c, 0, 1, False, True, (0,))
                if m + 1 < len(ORDER):
                    xT(m + 1, 0)
                down(name, a + 3, None, c, 0, 1, False, True, (1,))

            def mix_ab(m):
                s0 = phases["AB"]
                u0 = s0 + 2 * len(AB_CHUNKS)

                def scores(it):
                    hp, t = it // 2, it % 2
                    if it >= 2:
                        pe.wait_ge(S["weightsT_ready"], it - 1)
                    for h in range(2):
                        for c in range(2):
                            rs = slice(64 * c, 64 * c + 64)
                            ins = nc.tensor.matmul(score[t][:, c, h], qT[rs, 2 * hp + h, t * P:(t + 1) * P],
                                                   kT[rs, 2 * hp + h, 0:P * (t + 1)], start=True, stop=True)
                    ins.then_inc(S["scores_done"], 1)

                def weights_T(it):
                    t = it % 2
                    pe.wait_ge(S["weights_ready"], it + 1)
                    for h in range(2):
                        for kb in range(t + 1):
                            b = h * (t + 1) + kb
                            ins = nc.tensor.transpose(bank[2 * t][:, b * P:(b + 1) * P],
                                                      wts[t][:, h, kb * P:(kb + 1) * P], ident[:])
                    ins.then_inc(S["weightsT_done"], 1)

                def outputs(it):
                    hp, t = it // 2, it % 2
                    pe.wait_ge(S["weightsT_ready"], it + 1)
                    for h in range(2):
                        hs = slice((2 * hp + h) * P, (2 * hp + h + 1) * P)
                        for kb in range(t + 1):
                            ins = nc.tensor.matmul(T[t][:, hs], wT[t][:, h, kb], v_tok[:, kb, hs],
                                                   start=kb == 0, stop=kb == t)
                    if hp == 1:
                        ins.then_inc(S["o_done"], 1)

                def out_rows(t, i, ks=(0, 1)):
                    j = OUT_UNITS["AB"][i]
                    ts = slice(t * P, (t + 1) * P)
                    return rows(u0 + i, None, t, lambda k: xT_hi[:, 2 * j + k, ts], lambda k: xT_lo[:, 2 * j + k, ts],
                                i == 0, i == 3, t == TT - 1, Y_MIX["AB"], ks)

                first_chunks(m, s0)
                for j in range(2):
                    pe.wait_ge(S["rope_done"], j + 1)
                    project(s0 + 2 * j, None, 1, G[j])
                pe.wait_ge(S["rope_done"], 3)
                project(s0 + 4, None, 0, G[0])
                pe.wait_ge(S["rope_done"], 4)
                for i in range(4):
                    for h in range(HEADS_A):
                        ins = nc.tensor.transpose(bank[i][:, h * P:(h + 1) * P],
                                                  qk_rot[:, i // 2, i % 2, h * P:(h + 1) * P], ident[:])
                    ins.then_inc(S["qkT_done"], 1)
                project(s0 + 4, None, 1, G[1])
                pe.wait_ge(S["qkT_ready"], 4)
                scores(0)
                scores(1)
                pe.wait_ge(S["v_ready"], 1)
                project(s0 + 6, None, 0, G[0], FIRST)
                weights_T(0)
                project(s0 + 6, None, 0, G[0], SECOND)
                outputs(0)
                scores(2)
                pe.wait_ge(S["v_ready"], 2)
                project(s0 + 6, None, 1, G[1], FIRST)
                weights_T(1)
                project(s0 + 6, None, 1, G[1], SECOND)
                scores(3)
                pe.wait_ge(S["u_ready"], 2)
                pe.wait_ge(S["pool_tables_landed"], 16 * 4)
                for g in range(4):
                    dst, us = bank[4 + g // 2][:, (g % 2) * SEQ:(g % 2 + 1) * SEQ], slice(g * P, (g + 1) * P)
                    nc.tensor.matmul(dst, u_tok[:, 0, us], band[:, g, 0:SEQ], start=True, stop=False)
                    ins = nc.tensor.matmul(dst[:, P:SEQ], u_tok[:, 1, us], band[:, g, SEQ:], start=False, stop=True)
                    if g % 2:
                        ins.then_inc(S["dT_done"], 1)
                outputs(1)
                weights_T(2)
                for b in range(2):
                    pe.wait_ge(S["dT_ready"], b + 1)
                    for g in (2 * b, 2 * b + 1):
                        ins = nc.tensor.matmul(bank[4 + b][:, (g % 2) * SEQ:(g % 2 + 1) * SEQ], poolw[:, g], dT[:, g],
                                               start=True, stop=True)
                    ins.then_inc(S["poolT_done"], 1)
                outputs(2)
                weights_T(3)
                pe.wait_ge(S["poolT_lo"], 4)
                out_rows(0, 0)
                outputs(3)
                out_rows(0, 1)
                out_rows(1, 0)
                for t in range(TT):
                    pe.wait_ge(S["o_ready"], t + 1)
                    for h in range(HEADS_A):
                        ins = nc.tensor.transpose(bank[2 + t][:, h * P:(h + 1) * P],
                                                  o_tok[:, t, h * P:(h + 1) * P], ident[:])
                    ins.then_inc(S["oT_done"], 1)
                    if t == 0:
                        out_rows(1, 1, (0,))
                pe.wait_ge(S["oT_lo"], 1)
                out_rows(0, 2)
                out_rows(0, 3).then_inc(y_done, 1)
                out_rows(1, 1, (1,))
                pe.wait_ge(S["oT_lo"], 2)
                out_rows(1, 2)
                out_rows(1, 3, (0,))
                if m + 1 < len(ORDER):
                    xT(m + 1, 0)
                out_rows(1, 3, (1,)).then_inc(y_done, 1)

            def mix_c(m):
                s0 = phases["C"]
                first_chunks(m, s0)
                for g in range(GROUPS):
                    for slot, (j, t) in enumerate(SLOTS[g]):
                        if g == 0:
                            if t == 0:
                                continue
                            if j == 0:
                                pe.wait_ge(S["q_ready"], 1)
                                pe.wait_ge(S["qf_sigmoids"], 1)
                                project(s0, None, 1, G[0])
                            else:
                                pe.wait_ge(S["gate_ready"], 1)
                                project(s0 + 2, None, 1, G[1], FIRST)
                                head_kqT(0)
                                project(s0 + 2, None, 1, G[1], SECOND)
                        else:
                            if g == 1 and j == 0 and t == 0:
                                pe.wait_ge(S["q_ready"], 2)
                                pe.wait_ge(S["qf_sigmoids"], 2)
                            elif j == 0:
                                pe.wait_ge(S["gate_ready"], 2 * (g - 1) + t + 1)
                            else:
                                pe.wait_ge(S["q_ready"], 2 * g + t + 1)
                                pe.wait_ge(S["qf_sigmoids"], 2 * g + t + 1)
                            project(s0 + 2 * (2 * g + j), None, t, G[t])
                        hd = (4 * g + slot - 3) // 2
                        if hd < 0:
                            continue
                        if hd == 6:
                            head_oT(0)
                            head_outputs(5)
                            head_exponents(6)
                        elif slot % 2:
                            if hd:
                                head_outputs(hd - 1)
                            head_exponents(hd)
                            if hd % 2 == 0:
                                head_kqT(hd + 1)
                        else:
                            if hd % 2:
                                head_kqT(hd + 1)
                            head_levels(hd)
                u0 = s0 + 2 * len(C_CHUNKS)
                head_oT(1)
                out_rows(u0, 0, 0)
                head_kqT(7)
                out_rows(u0, 0, 1)
                head_oT(2)
                head_levels(6)
                out_rows(u0, 0, 2)
                head_outputs(6)
                head_exponents(7)
                head_levels(7)
                head_outputs(7)
                out_rows(u0, 1, 0)
                out_rows(u0, 1, 1, (0,))
                head_oT(3)
                out_rows(u0, 1, 1, (1,))
                out_rows(u0, 0, 3).then_inc(y_done, 1)
                out_rows(u0, 1, 2)
                out_rows(u0, 1, 3, (0,))
                if m + 1 < len(ORDER):
                    xT(m + 1, 0)
                out_rows(u0, 1, 3, (1,)).then_inc(y_done, 1)

            def out_rows(u0, t, j, ks=(0, 1)):
                pe.wait_ge(S["headT_lo"], j + 1)
                if t == 0 and j == 0:
                    pe.wait_ge(S["gate_ready"], 2 * GROUPS)
                ts = slice(t * P, (t + 1) * P)
                return rows(u0 + j, None, t, lambda k: xT_hi[:, 2 * j + k, ts], lambda k: xT_lo[:, 2 * j + k, ts],
                            j == 0, j == 3, t == TT - 1, Y_MIX["C"], ks)

            def head_kqT(hd):
                g, hs = hd // 2, slice((hd % 2) * P, (hd % 2 + 1) * P)
                pe.wait_ge(S["q_ready"], 2 * g + 2)
                pe.wait_ge(S["f_ready"], 2 * g + 2)
                if hd == 7:
                    pe.wait_ge(S["headT_lo"], 2)
                elif hd >= 2:
                    pe.wait_ge(S["state_ready"], hd - 1)
                elif hd == 1:
                    pe.wait_ge(S["kqT_ready"], 1)
                for a, src in enumerate((k_tok, q_tok)):
                    for t in range(TT):
                        ins = nc.tensor.transpose(bank[0][:, (2 * a + t) * P:(2 * a + t + 1) * P], src[:, t, hs],
                                                  ident[:])
                ins.then_inc(S["kqT_done"], 1)

            def head_exponents(hd):
                g, hs = hd // 2, slice((hd % 2) * P, (hd % 2 + 1) * P)
                pe.wait_ge(S["logf_lo"], g + 1)
                if hd:
                    pe.wait_ge(S["head_scores_ready"], 2 * hd)
                hi, lo = (h[:, g % 2].rearrange("p (t f) -> p t f", t=TT) for h in (hT_hi, hT_lo))
                for t in range(TT):
                    for b, d0, d1 in (((0, 0, 4), (1, 4, 8)) if t == 0 else ((0, 8, 9), (0, 1, 4), (1, 4, 8))):
                        c0 = P if (d0, d1) == (1, 4) else 0
                        dst = LV[t][:, b, c0:c0 + (d1 - d0) * P]
                        rhs = decay[:, d0:d1].rearrange("p l f -> p (l f)")
                        nc.tensor.matmul(dst, hi[:, t, hs], rhs, start=True, stop=False)
                        ins = nc.tensor.matmul(dst, lo[:, t, hs], rhs, start=False, stop=True)
                    ins.then_inc(S["exponents_done"], 1)

            def head_levels(hd):
                g, hs = hd // 2, slice((hd % 2) * P, (hd % 2 + 1) * P)
                pe.wait_ge(S["factors_ready"], 2 * hd + 1)
                for t in range(TT):
                    for l in range(NL):
                        if (t, l) == (0, 3):
                            pe.wait_ge(S["factors_ready"], 2 * hd + 2)
                        ins = nc.tensor.matmul(LV[t][:, l // 4, (l % 4) * P:(l % 4 + 1) * P],
                                               fac[:, 1 + l, t], fac[:, 1 + l, t], start=True, stop=True)
                    ins.then_inc(S["levels_done"], 1)
                    if t == 0:
                        last_read, count = {6: (S["headT_lo"], 3), 7: (S["state_ready"], 7)}.get(
                            hd, (S["kqT_ready"], hd + 2))
                        pe.wait_ge(last_read, count)
                        nc.tensor.transpose(bank[0][:, 0:P], fac[:, 0, 0], ident[:]).then_inc(S["klT_done"], 1)
                pe.wait_ge(S["klT_ready"], hd + 1)
                pe.wait_ge(S["val_ready"], 2 * g + 2)
                nc.tensor.matmul(bank[0][:, 0:P], klT, val[:, g % 2, 0, hs], start=True, stop=True
                                 ).then_inc(S["state_done"], 1)

            def head_outputs(hd):
                g, hs = hd // 2, slice((hd % 2) * P, (hd % 2 + 1) * P)
                pe.wait_ge(S["state_ready"], hd + 1)
                pe.wait_ge(S["head_scores_ready"], 2 * hd + 2)
                if hd:
                    pe.wait_ge(S["head_ready"], 2 * hd)
                nc.tensor.matmul(bank[1][:, 0:P], scT[:, 0], val[:, g % 2, 0, hs], start=True, stop=True)
                nc.tensor.matmul(bank[1][:, P:2 * P], scT[:, 1], val[:, g % 2, 1, hs], start=True, stop=False)
                nc.tensor.matmul(bank[1][:, P:2 * P], fac[:, 0, 1], state, start=False, stop=True
                                 ).then_inc(S["head_done"], 1)

            def head_oT(p):
                pe.wait_ge(S["head_ready"], 4 * p + 4)
                last_read, count = ((S["state_ready"], 6), (S["headT_lo"], 1), (S["kqT_ready"], 8),
                                    (S["state_ready"], 8))[p]
                pe.wait_ge(last_read, count)
                for h in range(2):
                    hh = 2 * p + h
                    for t in range(TT):
                        ins = nc.tensor.transpose(bank[0][:, (2 * h + t) * P:(2 * h + t + 1) * P],
                                                  o_half[hh // 4][:, t, (hh % 4) * P:(hh % 4 + 1) * P], ident[:])
                ins.then_inc(S["headT_done"], 1)

            pe.wait_ge(const_landed, 16)
            for m, name in enumerate(ORDER):
                if name == "AB":
                    mix_ab(m)
                elif name == "C":
                    mix_c(m)
                else:
                    ffn(name, m)


def shape_constants():
    import numpy as np
    c = np.zeros((P, C_END), np.float32)
    p, f = np.arange(P)[:, None], np.arange(P)[None, :]
    c[:, C_ID:C_ID + P] = p == f
    c[:, C_CAUSAL:C_CAUSAL + P] = np.where(f <= p, 0.0, NEG)
    c[:, C_INVF:C_INVF + 32] = (10000.0 ** (-np.arange(0, 64, 2) / 64)).astype(np.float32)
    tok = np.arange(SEQ)[None, :]
    for g, w in enumerate(POOLS):
        b = np.zeros((SEQ, SEQ))
        s = np.arange(SEQ)[:, None]
        b += np.where((s <= tok) & (s > tok - w), 1.0 / np.minimum(tok + 1, w), 0.0)
        b -= s == tok
        c[:, C_BAND + g * 3 * P:C_BAND + g * 3 * P + SEQ] = b[0:P]
        c[:, C_BAND + g * 3 * P + SEQ:C_BAND + (g + 1) * 3 * P] = b[P:, P:]
    decay = [p > f]
    mask = []
    for half in LEVELS:
        mid = f // (2 * half) * (2 * half) + half
        decay.append(np.where(f >= mid, (p >= mid) & (p <= f), (p > f) & (p < mid)))
        same = p // (2 * half) == f // (2 * half)
        mask.append(same & (p % (2 * half) < half) & (f % (2 * half) >= half))
    decay.append(p <= f)
    for i, a in enumerate(decay + mask):
        c[:, C_DECAY + i * P:C_DECAY + (i + 1) * P] = a
    return c


_INS = ["x", "positions", "ln_gain", "ln_bias", "ffn1_w_in", "ffn1_w_out", "ffn2_w_in", "ffn2_w_out", "ab_w_in",
        "ab_w_o", "diff_lambda", "diff_subln", "pool_w", "pool_scale", "c_w_in", "c_w_o", "c_norm", "hgrn_gamma"]


def kernel(**inputs):
    import numpy as np
    import concourse.bacc as bacc
    from concourse.bass_utils import run_bass_kernel_spmd

    nc = bacc.Bacc("TRN2", target_bir_lowering=False, num_devices=1)
    arrays, args = {}, []
    for name in _INS:
        a = np.ascontiguousarray(inputs[name])
        arrays[f"in_{name}"] = a
        args.append(nc.dram_tensor(f"in_{name}", a.shape, mybir.dt.from_np(a.dtype), kind="ExternalInput").ap())
    arrays["shape_constants"] = shape_constants()
    args.append(nc.dram_tensor("shape_constants", (P, C_END), F32, kind="ExternalInput").ap())
    args.append(nc.dram_tensor("out_x", (1, SEQ, D), F32, kind="ExternalOutput").ap())
    build(nc, *args)
    r = run_bass_kernel_spmd(nc, [arrays], core_ids=[0])
    return r.results[0]["out_x"]
```
